# Optimizing a Trainium2 kernel written in Bass

```python
import math, functools
import jax, jax.numpy as jnp
from jax import lax
import numpy as np

D_MODEL = 1024
BATCH = 1
SEQ = 512
DEPTH = 1
DEC_BATCH = 8
DEC_SEQ = 1
PAST_LEN = 4096
PAGE_SIZE = 128

D_A = D_MODEL
H_A = 8
DK_A = D_A // H_A
DV_A = D_A // H_A
D_B = D_MODEL
P_B = 64
H_B = D_B // P_B
N_STATE = 128
G_B = 2
CONV_W = 4
D_CONV_A = 2 * D_A
D_CONV_B = D_B + 2 * G_B * N_STATE
D_MIX = D_A + D_B
SPLIT_SIZES = (D_A, D_A, D_A, D_A, H_A, H_A, D_B, D_CONV_B, H_B)
D_PROJ = sum(SPLIT_SIZES)
CHUNK = 128
PEER_HEADS = 8
N_KEYS = 128
N_EXPERTS = N_KEYS * N_KEYS
D_KEY = 256
PEER_TOPK = 16
PEER_BLOCK = 256
EPS = 1e-6

kernel_name = 'hymba_mlstm_ssd_peer_step'

def rmsnorm(x, g):
    xf = x.astype(jnp.float32)
    y = xf * lax.rsqrt(jnp.mean(xf * xf, axis=-1, keepdims=True) + EPS)
    return (y * g.astype(jnp.float32)).astype(x.dtype)

def head_layernorm(h, g):
    hc = h - jnp.mean(h, axis=-1, keepdims=True)
    y = hc * lax.rsqrt(jnp.mean(hc * hc, axis=-1, keepdims=True) + EPS)
    return y.reshape(h.shape[0], h.shape[1], -1) * g.astype(jnp.float32)

def causal_conv_silu(x, buf, w, b):
    T = x.shape[1]
    xp = jnp.concatenate([buf.astype(x.dtype), x], axis=1)
    y = b + w[0] * xp[:, 0:T]
    for j in range(1, CONV_W):
        y = y + w[j] * xp[:, j:j + T]
    return jax.nn.silu(y), xp[:, xp.shape[1] - (CONV_W - 1):]

def to_chunks(a, L):
    b, T = a.shape[0], a.shape[1]
    return jnp.moveaxis(a.reshape((b, T // L, L) + a.shape[2:]), 1, 0)

def from_chunks(a):
    a = jnp.moveaxis(a, 0, 1)
    return a.reshape((a.shape[0], a.shape[1] * a.shape[2]) + a.shape[3:])

def mlstm_chunk(carry, inp):
    C, n, m = carry
    q, k, v, ig, lf = inp
    L = q.shape[1]
    bt = jnp.moveaxis(jnp.cumsum(lf, axis=1), 1, 2)
    igt = jnp.moveaxis(ig, 1, 2)
    causal = jnp.tril(jnp.ones((L, L), dtype=bool))
    log_d = jnp.where(causal, bt[..., :, None] - bt[..., None, :] + igt[..., None, :], -jnp.inf)
    log_inter = bt + m[..., None]
    m_t = jnp.maximum(log_inter, jnp.max(log_d, axis=-1))
    dmat = jnp.exp(log_d - m_t[..., None])
    inter = jnp.exp(log_inter - m_t)
    s = jnp.einsum('blhd,bshd->bhls', q, k) * dmat
    inter_l = jnp.moveaxis(inter, 1, 2)[..., None]
    num = jnp.einsum('bhls,bshv->blhv', s, v) + jnp.einsum('blhd,bhdv->blhv', q, C) * inter_l
    den = jnp.sum(s, axis=-1) + jnp.einsum('blhd,bhd->bhl', q, n) * inter
    denom = jnp.maximum(jnp.abs(den), jnp.exp(-m_t))
    h = num / jnp.moveaxis(denom, 1, 2)[..., None]
    b_last = bt[..., -1]
    log_w = b_last[..., None] - bt + igt
    m_new = jnp.maximum(b_last + m, jnp.max(log_w, axis=-1))
    w = jnp.exp(log_w - m_new[..., None])
    decay = jnp.exp(b_last + m - m_new)
    C_new = decay[..., None, None] * C + jnp.einsum('bhs,bshd,bshv->bhdv', w, k, v)
    n_new = decay[..., None] * n + jnp.einsum('bhs,bshd->bhd', w, k)
    return (C_new, n_new, m_new), h

def ssd_chunk(A, S, inp):
    x, dt, Bm, Cm = inp
    L = x.shape[1]
    rep = H_B // G_B
    Bh = jnp.repeat(Bm, rep, axis=2)
    Ch = jnp.repeat(Cm, rep, axis=2)
    cum = jnp.cumsum(jnp.moveaxis(dt * A, 1, 2), axis=-1)
    causal = jnp.tril(jnp.ones((L, L), dtype=bool))
    decay = jnp.exp(jnp.where(causal, cum[..., :, None] - cum[..., None, :], -jnp.inf))
    xdt = x * dt[..., None]
    scores = jnp.einsum('blhn,bshn->bhls', Ch, Bh) * decay
    y = jnp.einsum('bhls,bshp->blhp', scores, xdt) \
        + jnp.einsum('blhn,bhpn->blhp', Ch, S) * jnp.moveaxis(jnp.exp(cum), 1, 2)[..., None]
    w = jnp.exp(cum[..., -1:] - cum)
    S_new = jnp.exp(cum[..., -1])[..., None, None] * S + jnp.einsum('bhs,bshp,bshn->bhpn', w, xdt, Bh)
    return S_new, y

def peer_ffn(h, w_query, sub_keys, peer_u, peer_v):
    bsz, T, D = h.shape
    flat = h.reshape(bsz * T, D)
    ntok = flat.shape[0]
    pad = (-ntok) % PEER_BLOCK
    blocks = jnp.pad(flat, ((0, pad), (0, 0))).reshape(-1, PEER_BLOCK, D)
    keys = sub_keys.astype(jnp.float32)

    def one_block(xb):
        qry = jnp.einsum('td,de->te', xb, w_query).astype(jnp.float32)
        qry = qry.reshape(PEER_BLOCK, PEER_HEADS, 2, D_KEY // 2)
        s = jnp.einsum('thjd,jkd->thjk', qry, keys)
        s_top, i_top = lax.top_k(s, PEER_TOPK)
        cand = s_top[:, :, 0, :, None] + s_top[:, :, 1, None, :]
        cand_idx = i_top[:, :, 0, :, None] * N_KEYS + i_top[:, :, 1, None, :]
        cand = cand.reshape(PEER_BLOCK, PEER_HEADS, PEER_TOPK * PEER_TOPK)
        cand_idx = cand_idx.reshape(PEER_BLOCK, PEER_HEADS, PEER_TOPK * PEER_TOPK)
        best, pos = lax.top_k(cand, PEER_TOPK)
        idx = jnp.take_along_axis(cand_idx, pos, axis=-1)
        gates = jax.nn.softmax(best, axis=-1)
        u = peer_u[idx]
        act = jax.nn.gelu(jnp.einsum('thkd,td->thk', u, xb).astype(jnp.float32), approximate=False)
        wts = (gates * act).astype(xb.dtype)
        return jnp.einsum('thk,thkd->td', wts, peer_v[idx])

    out = lax.map(one_block, blocks).reshape(-1, D)[:ntok]
    return out.reshape(bsz, T, D)

def hybrid_layer(x, c, st, wl):
    (w_ada, b_ada, norm1_g, norm2_g, w_in, gate_b, conv_a_w, conv_a_b, mlstm_norm_g,
     conv_b_w, conv_b_b, dt_bias, a_log, d_skip, ssm_norm_g, w_out,
     w_query, sub_keys, peer_u, peer_v) = wl
    C0, n0, m0, conv_a0, S0, conv_b0 = st
    f32 = jnp.float32
    bsz, T, _ = x.shape
    chunk = CHUNK if T % CHUNK == 0 else T
    mod = jnp.einsum('bd,de->be', jax.nn.silu(c), w_ada) + b_ada
    sh1, sc1, g1, sh2, sc2, g2 = jnp.split(mod[:, None, :], 6, axis=-1)
    h = rmsnorm(x, norm1_g) * (1 + sc1) + sh1
    proj = jnp.einsum('btd,de->bte', h, w_in)
    bounds = np.cumsum(SPLIT_SIZES)[:-1].tolist()
    q, k, v, o, ig, fg, z, xbc, dt = jnp.split(proj, bounds, axis=-1)

    qk, conv_a1 = causal_conv_silu(jnp.concatenate([q, k], axis=-1), conv_a0, conv_a_w, conv_a_b)
    q, k = jnp.split(qk, 2, axis=-1)
    qh = q.reshape(bsz, T, H_A, DK_A).astype(f32)
    kh = k.reshape(bsz, T, H_A, DK_A).astype(f32) * (DK_A ** -0.5)
    vh = v.reshape(bsz, T, H_A, DV_A).astype(f32)
    log_i = ig.astype(f32) + gate_b[0].astype(f32)
    log_f = jax.nn.log_sigmoid(fg.astype(f32) + gate_b[1].astype(f32))
    xs_a = tuple(to_chunks(a, chunk) for a in (qh, kh, vh, log_i, log_f))
    (C1, n1, m1), h_a = lax.scan(mlstm_chunk, (C0.astype(f32), n0.astype(f32), m0.astype(f32)), xs_a)
    h_a = head_layernorm(from_chunks(h_a), mlstm_norm_g)
    h_a = (h_a * jax.nn.sigmoid(o.astype(f32))).astype(x.dtype)

    xbc, conv_b1 = causal_conv_silu(xbc, conv_b0, conv_b_w, conv_b_b)
    xs_b, Bm, Cm = jnp.split(xbc, [D_B, D_B + G_B * N_STATE], axis=-1)
    xh = xs_b.reshape(bsz, T, H_B, P_B).astype(f32)
    Bm = Bm.reshape(bsz, T, G_B, N_STATE).astype(f32)
    Cm = Cm.reshape(bsz, T, G_B, N_STATE).astype(f32)
    dt = jax.nn.softplus(dt.astype(f32) + dt_bias.astype(f32))
    A = -jnp.exp(a_log.astype(f32))
    xs_s = tuple(to_chunks(a, chunk) for a in (xh, dt, Bm, Cm))
    S1, y_b = lax.scan(functools.partial(ssd_chunk, A), S0.astype(f32), xs_s)
    y_b = from_chunks(y_b) + d_skip.astype(f32)[:, None] * xh
    y_b = y_b.reshape(bsz, T, D_B) * jax.nn.silu(z.astype(f32))
    y_b = rmsnorm(y_b, ssm_norm_g).astype(x.dtype)

    mixed = jnp.einsum('bte,ed->btd', jnp.concatenate([h_a, y_b], axis=-1), w_out)
    x = x + g1 * mixed
    h2 = rmsnorm(x, norm2_g) * (1 + sc2) + sh2
    x = x + g2 * peer_ffn(h2, w_query, sub_keys, peer_u, peer_v)
    return x, (C1, n1, m1, conv_a1, S1, conv_b1)

def setup_inputs(seed: int = 0) -> dict:
    key = jax.random.key(seed)
    ks = iter(jax.random.split(key, 40))

    def nrm(shape, scale):
        return jax.random.normal(next(ks), shape, jnp.float32) * scale

    dt0 = jnp.exp(jax.random.uniform(next(ks), (DEPTH, H_B), jnp.float32,
                                     minval=math.log(1e-3), maxval=math.log(1e-1)))
    gate_b = jnp.stack([nrm((DEPTH, H_A), 0.1) - 2.0,
                        jnp.linspace(3.0, 6.0, H_A)[None, :] + nrm((DEPTH, H_A), 0.1)], axis=1)
    return {
        'x_prompt': nrm((BATCH, SEQ, D_MODEL), 1.0),
        'x_sample': nrm((DEC_BATCH, DEC_SEQ, D_MODEL), 1.0),
        'c_prompt': nrm((BATCH, D_MODEL), 1.0),
        'c_sample': nrm((DEC_BATCH, D_MODEL), 1.0),
        'state_mlstm_c': nrm((DEPTH, DEC_BATCH, H_A, DK_A, DV_A), 0.1),
        'state_mlstm_n': nrm((DEPTH, DEC_BATCH, H_A, DK_A), 0.5),
        'state_mlstm_m': nrm((DEPTH, DEC_BATCH, H_A), 1.0),
        'state_mlstm_conv': nrm((DEPTH, DEC_BATCH, CONV_W - 1, D_CONV_A), 1.0),
        'state_ssm': nrm((DEPTH, DEC_BATCH, H_B, P_B, N_STATE), 0.5),
        'state_ssm_conv': nrm((DEPTH, DEC_BATCH, CONV_W - 1, D_CONV_B), 1.0),
        'w_ada': nrm((DEPTH, D_MODEL, 6 * D_MODEL), 0.5 * D_MODEL ** -0.5),
        'b_ada': nrm((DEPTH, 6 * D_MODEL), 0.02),
        'norm1_g': 1.0 + nrm((DEPTH, D_MODEL), 0.02),
        'norm2_g': 1.0 + nrm((DEPTH, D_MODEL), 0.02),
        'w_in': nrm((DEPTH, D_MODEL, D_PROJ), D_MODEL ** -0.5),
        'mlstm_gate_b': gate_b,
        'conv_a_w': nrm((DEPTH, CONV_W, D_CONV_A), CONV_W ** -0.5),
        'conv_a_b': nrm((DEPTH, D_CONV_A), 0.02),
        'mlstm_norm_g': 1.0 + nrm((DEPTH, D_A), 0.02),
        'conv_b_w': nrm((DEPTH, CONV_W, D_CONV_B), CONV_W ** -0.5),
        'conv_b_b': nrm((DEPTH, D_CONV_B), 0.02),
        'dt_bias': dt0 + jnp.log(-jnp.expm1(-dt0)),
        'a_log': jnp.log(jax.random.uniform(next(ks), (DEPTH, H_B), jnp.float32, minval=1.0, maxval=16.0)),
        'd_skip': 1.0 + nrm((DEPTH, H_B), 0.1),
        'ssm_norm_g': 1.0 + nrm((DEPTH, D_B), 0.02),
        'w_out': nrm((DEPTH, D_MIX, D_MODEL), D_MIX ** -0.5),
        'peer_w_query': nrm((DEPTH, D_MODEL, PEER_HEADS * D_KEY), D_MODEL ** -0.5),
        'peer_sub_keys': nrm((DEPTH, 2, N_KEYS, D_KEY // 2), (D_KEY // 2) ** -0.5),
        'peer_u': nrm((DEPTH, N_EXPERTS, D_MODEL), D_MODEL ** -0.5),
        'peer_v': nrm((DEPTH, N_EXPERTS, D_MODEL), PEER_HEADS ** -0.5),
        'final_norm_g': 1.0 + nrm((D_MODEL,), 0.02),
    }

def reference(x_prompt, x_sample, c_prompt, c_sample, state_mlstm_c, state_mlstm_n, state_mlstm_m,
              state_mlstm_conv, state_ssm, state_ssm_conv, w_ada, b_ada, norm1_g, norm2_g, w_in,
              mlstm_gate_b, conv_a_w, conv_a_b, mlstm_norm_g, conv_b_w, conv_b_b, dt_bias, a_log,
              d_skip, ssm_norm_g, w_out, peer_w_query, peer_sub_keys, peer_u, peer_v, final_norm_g):
    f32 = jnp.float32
    bp = x_prompt.shape[0]
    zero_state = (jnp.zeros((bp, H_A, DK_A, DV_A), f32),
                  jnp.zeros((bp, H_A, DK_A), f32),
                  jnp.zeros((bp, H_A), f32),
                  jnp.zeros((bp, CONV_W - 1, D_CONV_A), x_prompt.dtype),
                  jnp.zeros((bp, H_B, P_B, N_STATE), f32),
                  jnp.zeros((bp, CONV_W - 1, D_CONV_B), x_prompt.dtype))
    hp, hs = x_prompt, x_sample
    new_p, new_s = [], []
    for l in range(DEPTH):
        wl = (w_ada[l], b_ada[l], norm1_g[l], norm2_g[l], w_in[l], mlstm_gate_b[l], conv_a_w[l],
              conv_a_b[l], mlstm_norm_g[l], conv_b_w[l], conv_b_b[l], dt_bias[l], a_log[l],
              d_skip[l], ssm_norm_g[l], w_out[l], peer_w_query[l], peer_sub_keys[l],
              peer_u[l], peer_v[l])
        hp, st_p = hybrid_layer(hp, c_prompt, zero_state, wl)
        st_in = (state_mlstm_c[l], state_mlstm_n[l], state_mlstm_m[l], state_mlstm_conv[l],
                 state_ssm[l], state_ssm_conv[l])
        hs, st_s = hybrid_layer(hs, c_sample, st_in, wl)
        new_p.append(st_p)
        new_s.append(st_s)
    y_prompt = rmsnorm(hp, final_norm_g)
    y_sample = rmsnorm(hs, final_norm_g)
    dtypes = (state_mlstm_c.dtype, state_mlstm_n.dtype, state_mlstm_m.dtype,
              state_mlstm_conv.dtype, state_ssm.dtype, state_ssm_conv.dtype)

    def stacked(states, i):
        return jnp.stack([s[i] for s in states], axis=0).astype(dtypes[i])

    return (y_prompt, y_sample,
            stacked(new_p, 0), stacked(new_p, 1), stacked(new_p, 2),
            stacked(new_p, 3), stacked(new_p, 4), stacked(new_p, 5),
            stacked(new_s, 0), stacked(new_s, 1), stacked(new_s, 2),
            stacked(new_s, 3), stacked(new_s, 4), stacked(new_s, 5))


_drawn_inputs = setup_inputs


def setup_inputs(seed=0):
    import zlib

    import numpy as np

    out = dict(_drawn_inputs(seed))
    spreads = {}
    factors = {'norm2_g': 21.854,
     'mlstm_norm_g': 29.533,
     'd_skip': 3.14,
     'ssm_norm_g': 37.199,
     'final_norm_g': 23.526}
    for name, (base, spread) in spreads.items():
        noise = np.random.default_rng([zlib.crc32(name.encode()), seed]).standard_normal(out[name].shape)
        drawn = base * np.exp(spread * noise) if base else spread * noise
        out[name] = __import__('jax').numpy.asarray(drawn.astype(out[name].dtype))
    for name, factor in factors.items():
        out[name] = (out[name] * factor).astype(out[name].dtype)
    return out
```

```python
from contextlib import ExitStack

import concourse.bass as bass
from concourse import mybir

F32 = mybir.dt.float32
U32 = mybir.dt.uint32
ALU = mybir.AluOpType
ACT = mybir.ActivationFunctionType
AX_X = mybir.AxisListType.X

P = 128
D = 1024
KD = D // P
T = 512
B = 8
N = T + B
HN = N // 2
L = 128
NC = T // L
H_A = 8
H_B = 16
P_B = 64
G_B = 2
CONV = 4
NQ, NK, NV, NO, NZ, NX = 0, 8, 16, 24, 32, 40
SLOTS = 52
IG0, Z0, DT0 = 4096, 4112, 6672
PH = 8
NKEY = 128
TOPK = 16
EPS = 1e-6
FAR = 1e4
KSCALE = float(P) ** -0.5

V_BADA, V_N1, V_N2, V_CAW = 0, 48, 56, 64
V_CAB, V_CBW, V_CBB, V_GA, V_GB, V_GF = 128, 144, 192, 204, 212, 220
NVEC = 228


class Chain:

    def __init__(self, engine, sem):
        self.engine, self.sem, self.n = engine, sem, 0

    def __call__(self, instruction):
        self.n += 1
        instruction.then_inc(self.sem, 1)
        self.engine.wait_ge(self.sem, self.n)


class Phase(ExitStack):

    def __init__(self, nc):
        super().__init__()
        self.nc, self.semaphores = nc, []
        self.callback(self.clear)

    def sem(self, name):
        self.semaphores.append(self.nc.alloc_semaphore(name=name))
        return self.semaphores[-1]

    def clear(self):
        self.nc.all_engine_barrier()
        self.nc.clear_and_free_semaphores(self.semaphores)
        self.nc.all_engine_barrier()


def halves(t):
    return t.rearrange("p (a n) -> p a n", a=2)


def setup_phase(nc, A, S):
    with Phase(nc) as ctx:
        sem = ctx.sem
        rows = ctx.enter_context(nc.sbuf_tensor("rows", [P, 11, P], F32))
        xrow = ctx.enter_context(nc.sbuf_tensor("xrow", [P, NC, D], F32))
        ps = [ctx.enter_context(nc.psum_tensor(f"ps_set{i}", [P, 512], F32)) for i in range(8)]
        rows_in, x_in, small_in = sem("rows_in"), sem("x_in"), sem("small_in")
        zeroed, consts, turned, moved, moved_c = sem("zeroed"), sem("consts"), sem("turned"), sem("moved"), sem("moved_c")
        pool_own = sem("pool_own_set")
        loads = [
            (0, 0, A["b_ada"][0].rearrange("(r p) -> r p", p=P)),
            (0, 48, A["norm1_g"][0].rearrange("(r p) -> r p", p=P)),
            (0, 56, A["norm2_g"][0].rearrange("(r p) -> r p", p=P)),
            (0, 64, A["conv_a_w"][0].rearrange("j (r p) -> (j r) p", p=P)),
            (1, 0, A["conv_a_b"][0].rearrange("(r p) -> r p", p=P)),
            (1, 16, A["conv_b_w"][0].rearrange("j (r p) -> (j r) p", p=P)),
            (1, 64, A["conv_b_b"][0].rearrange("(r p) -> r p", p=P)),
            (1, 76, A["mlstm_norm_g"][0].rearrange("(r p) -> r p", p=P)),
            (1, 84, A["ssm_norm_g"][0].rearrange("(r p) -> r p", p=P)),
            (1, 92, A["final_norm_g"].rearrange("(r p) -> r p", p=P)),
            (2, 0, A["c_prompt"].rearrange("b (r p) -> (b r) p", p=P)),
            (2, 8, A["c_sample"].rearrange("b (r p) -> (b r) p", p=P)),
            (3, 0, A["x_sample"].rearrange("b t (r p) -> (b t r) p", p=P)),
            (3, 64, A["state_mlstm_n"][0].rearrange("b h d -> (b h) d")),
        ]
        ca = A["state_mlstm_conv"][0].rearrange("b j (r p) -> (b j r) p", p=P)
        cb = A["state_ssm_conv"][0].rearrange("b j (r p) -> (b j r) p", p=P)
        loads += [(4 + i, 0, ca[i * P:(i + 1) * P]) for i in range(3)]
        loads += [(7 + i, 0, cb[i * P:min((i + 1) * P, 288)]) for i in range(3)]
        height = [P, 100, 72, P, P, P, P, P, P, 32]
        block = ctx.enter_context(nc.Block())

        @block.sync
        def _(sp):
            for tile, at, src in loads:
                sp.dma_start(rows[at:at + src.shape[0], tile, :], src).then_inc(rows_in, 16)
            for t in range(NC):
                sp.dma_start(xrow[:, t, :], A["x_prompt"][0, t * L:(t + 1) * L, :]).then_inc(x_in, 16)
            sp.wait_ge(zeroed, 1)
            wi = A["w_in"][0].rearrange("(k p) n -> p k n", p=P)
            for at, col, n in ((0, IG0, 8), (32, IG0 + 8, 8), (64, DT0, 16)):
                sp.dma_start(S.wg[:, :, at:at + n], wi[:, :, col:col + n]).then_inc(small_in, 16)
            for row, src in enumerate((A["mlstm_gate_b"][0, 0], A["mlstm_gate_b"][0, 1])):
                sp.dma_start(S.col[0:H_A, row:row + 1], src.rearrange("(a b) -> a b", b=1)).then_inc(small_in, 16)
            for row, name in ((2, "dt_bias"), (3, "a_log"), (4, "d_skip")):
                sp.dma_start(S.col[0:H_B, row:row + 1], A[name][0].rearrange("(a b) -> a b", b=1)).then_inc(small_in, 16)
            sp.dma_start(S.m0T[:, :], A["state_mlstm_m"][0].rearrange("b h -> h b"), allow_slow_non_contiguous=True).then_inc(small_in, 16)
            sp.wait_ge(small_in, 16 * 9)

        @block.gpsimd
        def _(pool):
            own = Chain(pool, pool_own)
            own(nc.gpsimd.memset(S.ident[:, :], 0.0))
            nc.gpsimd.affine_select(out=S.ident[:, :], in_=S.ident[:, :], compare_op=ALU.not_equal, fill=1.0,
                                    base=0, pattern=[[-1, P]], channel_multiplier=1).then_inc(consts, 1)
            nc.gpsimd.iota(S.iota[:, :], [[1, P]], base=0, channel_multiplier=0,
                           allow_small_or_imprecise_dtypes=True)
            own(nc.gpsimd.memset(S.far[:, :], 0.0))
            own(nc.gpsimd.affine_select(out=S.far[:, :], in_=S.far[:, :], compare_op=ALU.is_ge, fill=FAR,
                                        base=0, pattern=[[1, P]], channel_multiplier=-1))
            own(nc.gpsimd.memset(S.pick[:, :, :], 0.0))
            own(nc.gpsimd.affine_select(out=S.pick[:, :, :], in_=S.pick[:, :, :], compare_op=ALU.not_equal, fill=1.0,
                                        base=0, pattern=[[-1, H_B], [0, P]], channel_multiplier=1))

        @block.vector
        def _(dve):
            nc.vector.memset(S.wg[:, :, :], 0.0).then_inc(zeroed, 1)
            nc.vector.memset(S.ones[:, :], 1.0)
            dve.wait_ge(turned, 3)
            nc.vector.tensor_copy(S.vec[:, 0:P], ps[0][:, 0:P])
            nc.vector.tensor_copy(S.vec[:, P:NVEC], ps[0][:, P:P + 100])
            nc.vector.tensor_copy(S.xT[:, :, T:N].rearrange("p k b -> p b k"),
                                  ps[0][:, 384:448].rearrange("p (b k) -> p b k", k=KD))
            nc.vector.tensor_copy(S.n0[:, :], ps[0][:, 448:512]).then_inc(moved, 1)
            nc.vector.tensor_copy(S.cbufa[:, 0:384], ps[1][:, 0:384])
            nc.vector.tensor_copy(S.cbufb[:, 0:128], ps[1][:, 384:512])
            nc.vector.tensor_copy(S.cbufb[:, 128:288], ps[2][:, 0:160]).then_inc(moved, 1)
            for k in range(KD):
                dve.wait_ge(turned, 4 + k)
                nc.vector.tensor_copy(S.xT[:, k, 0:T], ps[3 + k % 5][:, :]).then_inc(moved, 1)

        @block.scalar
        def _(act):
            act.wait_ge(moved, 1)
            nc.scalar.activation(S.silc[:, :, 0:1], ps[0][:, 256:264].rearrange("p (k a) -> p k a", a=1), ACT.Silu)
            nc.scalar.activation(S.silc[:, :, 1:9].rearrange("p k b -> p b k"),
                                 ps[0][:, 264:328].rearrange("p (b k) -> p b k", k=KD), ACT.Silu).then_inc(moved_c, 1)

        @block.tensor
        def _(pe):
            pe.wait_ge(consts, 1)
            pe.wait_ge(rows_in, 16 * len(loads))
            for t in range(10):
                h = height[t]
                mm = nc.tensor.transpose(ps[t // 4][:, t % 4 * P:t % 4 * P + h], rows[0:h, t, :], S.ident[0:h, 0:h])
                if t in (3, 7, 9):
                    mm.then_inc(turned, 1)
            pe.wait_ge(x_in, 16 * NC)
            for k in range(KD):
                if k >= 5:
                    pe.wait_ge(moved, 2 + k - 4)
                for t in range(NC):
                    mm = nc.tensor.transpose(ps[3 + k % 5][:, t * L:(t + 1) * L], xrow[:, t, k * P:(k + 1) * P], S.ident[:, :])
                mm.then_inc(turned, 1)


def project(nc, name, runs, w, K, X, width, evict, after=None):
    cols = 4096 // K
    per = cols // P
    wv = w.rearrange("(k p) n -> p k n", p=P)
    with Phase(nc) as ctx:
        wb = [ctx.enter_context(nc.sbuf_tensor(f"wb{i}_{name}", [P, K, cols], F32)) for i in range(2)]
        ps = [ctx.enter_context(nc.psum_tensor(f"ps{i}_{name}", [P, 2, 512], F32)) for i in range(2)]
        w_in = [ctx.sem(f"w_in{i}_{name}") for i in range(2)]
        product = ctx.sem(f"product_{name}")
        evicted = ctx.sem(f"evicted_{name}")
        block = ctx.enter_context(nc.Block())
        nh, hw = (2, HN) if width == N else (1, width)

        @block.sync
        def _(sp):
            pairs = 0
            for col, n, _ in runs:
                with sp.Fori(0, n) as i:
                    for j in range(2):
                        sp.wait_ge(product, 2 * per * i + per * (2 * pairs + j + 1))
                        sp.dma_start(wb[j][:, :, :], wv[:, :, bass.ds(i * (2 * cols) + (col + j * cols), cols)]).then_inc(w_in[j], 16)
                pairs += n

        @block.tensor
        def _(pe):
            pairs = 0
            pe.sem_inc(product, 2 * per)
            for _, n, _ in runs:
                with pe.Fori(0, n) as i:
                    for j in range(2):
                        pe.wait_ge(w_in[j], 16 * i + 16 * (pairs + 1))
                        for m in range(per):
                            c = j * per + m
                            pe.wait_ge(evicted, 2 * per * i + (2 * per * pairs + c + 1))
                            for h in range(nh):
                                for k in range(K):
                                    mm = nc.tensor.matmul(ps[c % 2][:, h, 0:hw], wb[j][:, k, m * P:(m + 1) * P],
                                                          X(k)[:, h * hw:(h + 1) * hw], start=(k == 0), stop=(k == K - 1))
                            mm.then_inc(product, 1)
                pairs += n

        def evictions(eng):
            eng.sem_inc(evicted, 2)
            pairs = 0
            for _, n, chunk in runs:
                with eng.Fori(0, n) as i:
                    for c in range(2 * per):
                        eng.wait_ge(product, 2 * per * i + (2 * per * (pairs + 1) + c + 1))
                        evict(2 * per * i + (chunk + c), ps[c % 2]).then_inc(evicted, 1)
                pairs += n

        block.scalar(evictions)
        if after:
            after(block)


def bcast(ap, dim, n):
    return ap.unsqueeze(dim).to_broadcast(ap.shape[:dim] + (n,) + ap.shape[dim:])


def norm_phase(nc, name, S, X, n_chunks, finish):
    with Phase(nc) as ctx:
        sq = ctx.enter_context(nc.sbuf_tensor(f"sq_{name}", [P, 2, N], F32))
        ps = ctx.enter_context(nc.psum_tensor(f"ps_{name}", [P, 2, 512], F32))
        squared, summed, scaled, rooted = (ctx.sem(f"{n}_{name}") for n in ("squared", "summed", "scaled", "rooted"))
        act_own = ctx.sem(f"act_own_{name}")
        dve_own = ctx.sem(f"dve_own_{name}")
        block = ctx.enter_context(nc.Block())

        @block.scalar
        def _(act):
            for k in range(n_chunks):
                if k >= 2:
                    act.wait_ge(summed, k - 1)
                nc.scalar.activation(sq[:, k % 2, :], X(k), ACT.Square).then_inc(squared, 1)
            act.wait_ge(scaled, 1)
            own = Chain(act, act_own)
            own(nc.scalar.activation(S.rb[:, :], S.rb[:, :], ACT.Ln))
            nc.scalar.activation(S.rb[:, :], S.rb[:, :], ACT.Exp, scale=-0.5).then_inc(rooted, 1)

        @block.tensor
        def _(pe):
            for k in range(n_chunks):
                pe.wait_ge(squared, k + 1)
                for h in range(2):
                    mm = nc.tensor.matmul(ps[:, h, 0:HN], S.ones[:, :], sq[:, k % 2, h * HN:(h + 1) * HN],
                                          start=(k == 0), stop=(k == n_chunks - 1))
                mm.then_inc(summed, 1)

        @block.vector
        def _(dve):
            dve.wait_ge(summed, n_chunks)
            nc.vector.tensor_scalar(halves(S.rb[:, :]), ps[:, :, 0:HN], 1.0 / (n_chunks * P), EPS, ALU.mult, ALU.add).then_inc(scaled, 1)
            dve.wait_ge(rooted, 1)
            finish(dve, Chain(dve, dve_own))


def modulate(nc, S, dst, gain, shift, scale):
    def finish(dve, own):
        own(nc.vector.tensor_scalar(S.gs[:, :, :], S.mod[:, scale:scale + KD, :], 1.0, None, ALU.add))
        own(nc.vector.tensor_tensor(S.gs[:, :, :], S.gs[:, :, :], bcast(S.vec[:, gain:gain + KD], 2, 9), ALU.mult))
        for k in range(KD):
            nc.vector.scalar_tensor_tensor(out=dst[:, k, 0:T], in0=S.xT[:, k, 0:T], scalar=S.gs[:, k, 0:1],
                                           in1=S.rb[:, 0:T], op0=ALU.mult, op1=ALU.mult)
        own(nc.vector.tensor_tensor(dst[:, :, T:N], S.xT[:, :, T:N], bcast(S.rb[:, T:N], 1, KD), ALU.mult))
        for k in range(KD):
            nc.vector.tensor_scalar(dst[:, k, 0:T], dst[:, k, 0:T], S.mod[:, shift + k, 0:1], None, ALU.add)
        own(nc.vector.tensor_tensor(dst[:, :, T:N], dst[:, :, T:N], S.gs[:, :, 1:9], ALU.mult))
        own(nc.vector.tensor_tensor(dst[:, :, T:N], dst[:, :, T:N], S.mod[:, shift:shift + KD, 1:9], ALU.add))
    return finish


def gates_phase(nc, A, S, R, O):
    with Phase(nc) as ctx:
        sem = ctx.sem
        sb = lambda n, s: ctx.enter_context(nc.sbuf_tensor(n, s, F32))
        ps = ctx.enter_context(nc.psum_tensor("ps_gate", [P, 2, 512], F32))
        pt = ctx.enter_context(nc.psum_tensor("pt_gate", [P, 2, 512], F32))
        pb = ctx.enter_context(nc.psum_tensor("pb_gate", [P, 4, 512], F32))
        fg, u, ef, lf, ig = (sb(f"{n}_gate", [H_A, N]) for n in ("fg", "u", "ef", "lf", "ig"))
        dx, du, de = (sb(f"{n}_gate", [H_B, N]) for n in ("dx", "du", "de"))
        bt = sb("bt_gate", [H_A, N])
        reset = sb("reset_gate", [H_B, T])
        mc = sb("mc_gate", [H_A, NC + 1])
        ml = sb("ml_gate", [H_A, NC + 1])
        va = sb("va_gate", [H_A, 28])
        vb = sb("vb_gate", [H_B, 21])
        xa = sb("xa_gate", [H_A, H_A, 28])
        xb = sb("xb_gate", [H_B, H_B, 21])
        row = {n: sb(f"row_{n}", [H_A, N]) for n in ("inter", "w", "em")}
        rw = sb("row_ws", [H_B, T])
        re = sb("row_ec", [H_B, T])
        gated, acted, dve_own, act_own = sem("gated"), sem("acted"), sem("dve_own_gate"), sem("act_own_gate")
        rowed, columned, expanded, spread, out_done = sem("rowed"), sem("columned"), sem("expanded"), sem("spread"), sem("gate_out")
        block = ctx.enter_context(nc.Block())

        @block.tensor
        def _(pe):
            for h in range(2):
                for k in range(KD):
                    mm = nc.tensor.matmul(ps[0:96, h, 0:HN], S.wg[:, k, :], S.hT[:, k, h * HN:(h + 1) * HN],
                                          start=(k == 0), stop=(k == KD - 1))
            mm.then_inc(gated, 1)
            pe.wait_ge(acted, 2)
            for q, r in enumerate((R.a, row["inter"], row["w"], row["em"], R.cum, R.dt, rw, re)):
                n = H_A if q < 4 else H_B
                for c in range(NC):
                    at = (c * 8 + q) * 16
                    mm = nc.tensor.transpose(pt[:, 0, at:at + n], r[0:n, c * L:(c + 1) * L], S.ident[0:n, 0:n])
            mm.then_inc(columned, 1)
            pe.wait_ge(expanded, 1)
            nc.tensor.matmul(pb[:, 0, 0:224], S.ones[0:H_A, :], xa[:, :, :].rearrange("p a b -> p (a b)"), start=True, stop=True)
            nc.tensor.matmul(pb[:, 1, 0:336], S.ones[0:H_B, :], xb[:, :, :].rearrange("p a b -> p (a b)"), start=True, stop=True).then_inc(columned, 1)

        @block.scalar
        def _(act):
            own = Chain(act, act_own)
            act.wait_ge(gated, 1)
            nc.scalar.activation(halves(ig[:, :]), ps[0:H_A, :, 0:HN], ACT.Identity, bias=S.col[0:H_A, 0:1])
            nc.scalar.activation(halves(fg[:, :]), ps[32:32 + H_A, :, 0:HN], ACT.Identity, bias=S.col[0:H_A, 1:2])
            own(nc.scalar.activation(halves(dx[:, :]), ps[64:64 + H_B, :, 0:HN], ACT.Identity, bias=S.col[0:H_B, 2:3]))
            nc.scalar.activation(ef[:, :], fg[:, :], ACT.Abs)
            own(nc.scalar.activation(de[:, :], dx[:, :], ACT.Abs))
            nc.scalar.activation(ef[:, :], ef[:, :], ACT.Exp, scale=-1.0)
            nc.scalar.activation(S.ea[:, :], S.col[0:H_B, 3:4], ACT.Exp)
            own(nc.scalar.activation(de[:, :], de[:, :], ACT.Exp, scale=-1.0))
            nc.scalar.activation(ef[:, :], ef[:, :], ACT.Ln, bias=1.0)
            nc.scalar.activation(de[:, :], de[:, :], ACT.Ln, bias=1.0).then_inc(acted, 1)
            act.wait_ge(rowed, 2)
            for t in (row["inter"][:, :], row["w"][:, :], row["em"][:, :], rw[:, :], re[:, :], va[:, :], vb[:, 0:12]):
                last = nc.scalar.activation(t, t, ACT.Exp, scale=-1.0)
            last.then_inc(acted, 1)

        @block.vector
        def _(dve):
            own = Chain(dve, dve_own)
            v = nc.vector
            v.memset(reset[:, :], 1.0)
            own(v.memset(mc[:, 0:1], 0.0))
            own(v.memset(reset[:, :].rearrange("p (c l) -> p c l", c=NC)[:, :, 0:1], 0.0))
            dve.wait_ge(acted, 1)
            v.scalar_tensor_tensor(out=lf[:, :], in0=fg[:, :], scalar=0.0, in1=ef[:, :], op0=ALU.min, op1=ALU.subtract)
            own(v.scalar_tensor_tensor(out=R.dt[:, :], in0=dx[:, :], scalar=0.0, in1=de[:, :], op0=ALU.max, op1=ALU.add))
            own(v.tensor_scalar(du[:, :], R.dt[:, :], S.ea[:, 0:1], None, ALU.mult))
            v.tensor_tensor_scan(bt[:, 0:T], reset[0:H_A, :], lf[:, 0:T], 0.0, ALU.mult, ALU.add)
            v.tensor_copy(bt[:, T:N], lf[:, T:N])
            v.tensor_tensor_scan(R.cum[:, 0:T], reset[:, :], du[:, 0:T], 0.0, ALU.mult, ALU.add)
            own(v.tensor_copy(R.cum[:, T:N], du[:, T:N]))
            own(v.tensor_tensor(R.a[:, :], ig[:, :], bt[:, :], ALU.subtract))
            for c in range(NC):
                at = slice(c * L, (c + 1) * L)
                own(v.tensor_tensor_scan(R.M[:, at], R.a[:, at], R.a[:, at], mc[:, c:c + 1], ALU.max, ALU.max))
                own(v.tensor_tensor(mc[:, c + 1:c + 2], R.M[:, (c + 1) * L - 1:(c + 1) * L], bt[:, (c + 1) * L - 1:(c + 1) * L], ALU.add))
            own(v.tensor_tensor(R.M[:, T:N], R.a[:, T:N], S.m0T[:, :], ALU.max))
            for c in range(NC):
                at = slice(c * L, (c + 1) * L)
                last = slice((c + 1) * L - 1, (c + 1) * L)
                v.tensor_scalar(row["inter"][:, at], R.M[:, at], mc[:, c:c + 1], None, ALU.subtract)
                v.tensor_scalar(row["w"][:, at], R.a[:, at], R.M[:, last], -1.0, ALU.subtract, ALU.mult)
                v.tensor_tensor(va[:, c:c + 1], R.M[:, last], mc[:, c:c + 1], ALU.subtract)
                v.tensor_scalar(rw[:, at], R.cum[:, at], R.cum[:, last], -1.0, ALU.subtract, ALU.mult)
                v.tensor_copy(vb[:, c:c + 1], R.cum[:, last])
            v.tensor_tensor(row["inter"][:, T:N], R.M[:, T:N], S.m0T[:, :], ALU.subtract)
            v.tensor_tensor(row["w"][:, T:N], R.M[:, T:N], R.a[:, T:N], ALU.subtract)
            v.tensor_copy(re[:, :], R.cum[:, 0:T])
            own(v.tensor_tensor(row["em"][:, :], R.M[:, :], bt[:, :], ALU.add))
            v.tensor_copy(va[:, 4:12], row["inter"][:, T:N])
            v.tensor_copy(va[:, 12:20], row["w"][:, T:N])
            v.tensor_copy(va[:, 20:28], row["em"][:, T:N])
            v.tensor_copy(vb[:, 4:12], R.cum[:, T:N])
            v.tensor_copy(vb[:, 12:20], R.dt[:, T:N])
            v.tensor_copy(S.mS[:, :], row["em"][:, T:N])
            own(v.tensor_copy(vb[:, 20:21], S.col[0:H_B, 4:5]))
            v.tensor_copy(S.mP[:, :], mc[:, NC:NC + 1]).then_inc(rowed, 2)
            dve.wait_ge(acted, 2)
            v.tensor_tensor(xa[:, :, :], bcast(va[:, :], 1, H_A), bcast(S.ident[0:H_A, 0:H_A], 2, 28), ALU.mult)
            v.tensor_tensor(xb[:, :, :], bcast(vb[:, :], 1, H_B), bcast(S.ident[0:H_B, 0:H_B], 2, 21), ALU.mult).then_inc(expanded, 1)
            dve.wait_ge(columned, 1)
            v.tensor_copy(S.cols[:, :, 0:4, 0:8], pt[:, 0, :].rearrange("p (c q n) -> p c q n", c=NC, q=8)[:, :, 0:4, 0:8])
            v.tensor_copy(S.cols[:, :, 4:8, :], pt[:, 0, :].rearrange("p (c q n) -> p c q n", c=NC, q=8)[:, :, 4:8, :])
            dve.wait_ge(columned, 2)
            v.tensor_copy(S.ba[:, :, :].rearrange("p a b -> p (a b)"), pb[:, 0, 0:224])
            v.tensor_copy(S.bb[:, :, :].rearrange("p a b -> p (a b)"), pb[:, 1, 0:336]).then_inc(spread, 1)

        @block.sync
        def _(sp):
            sp.wait_ge(rowed, 2)
            sp.dma_start(O["p_m"][0, 0].rearrange("(h a) -> h a", a=1), S.mP[:, :]).then_inc(out_done, 16)
            sp.dma_start(O["s_m"][0].rearrange("b h -> h b"), S.mS[:, :], allow_slow_non_contiguous=True).then_inc(out_done, 16)
            sp.wait_ge(out_done, 32)


def conv_phase(nc, A, S, O):
    with Phase(nc) as ctx:
        sem = ctx.sem
        sb = lambda n, s: ctx.enter_context(nc.sbuf_tensor(n, s, F32))
        y = sb("y_conv", [P, 4, T])
        ys = sb("ys_conv", [P, 28, B])
        ts = sb("ts_conv", [P, 28, B])
        raw = sb("raw_conv", [P, 28, 3 + B])
        tail = sb("tail_conv", [32, 28 * P])
        ps = [ctx.enter_context(nc.psum_tensor(f"ps_conv{i}", [P, 512], F32)) for i in range(7)]
        first, convd, used, dve_own, act_own = sem("first_tap"), sem("convd"), sem("silu_done"), sem("dve_own_conv"), sem("act_own_conv")
        kept, tailed, rowed, out_done = sem("raw_kept"), sem("tail_turned"), sem("tail_moved"), sem("conv_out")
        samples = sem("samples_convd")
        block = ctx.enter_context(nc.Block())
        slot = lambda i: i if i < 16 else NX + i - 16

        def tap(i, j):
            return S.vec[:, V_CAW + 16 * j + i:V_CAW + 16 * j + i + 1] if i < 16 else S.vec[:, V_CBW + 12 * j + i - 16:V_CBW + 12 * j + i - 15]

        def bias(i):
            return S.vec[:, V_CAB + i:V_CAB + i + 1] if i < 16 else S.vec[:, V_CBB + i - 16:V_CBB + i - 15]

        @block.scalar
        def _(act):
            for i in range(28 + 2):
                if i < 28:
                    if i >= 4:
                        act.wait_ge(used, i - 3)
                    nc.scalar.activation(y[:, i % 4, :], S.proj[:, slot(i), 0:T], ACT.Identity, bias=bias(i), scale=tap(i, 3)).then_inc(first, 1)
                if i >= 2:
                    act.wait_ge(convd, i - 1)
                    nc.scalar.activation(S.proj[:, slot(i - 2), 0:T], y[:, (i - 2) % 4, :], ACT.Silu).then_inc(used, 1)
            act.wait_ge(samples, 1)
            nc.scalar.activation(S.proj[:, 0:16, T:N], ys[:, 0:16, :], ACT.Silu)
            nc.scalar.activation(S.proj[:, NX:NX + 12, T:N], ys[:, 16:28, :], ACT.Silu)
            for k in range(KD):
                nc.scalar.activation(S.proj[:, NZ + k, :], S.proj[:, NZ + k, :], ACT.Silu)
            for k in range(KD):
                last = nc.scalar.activation(S.proj[:, NO + k, :], S.proj[:, NO + k, :], ACT.Sigmoid)
            last.then_inc(used, 1)

        @block.vector
        def _(dve):
            own = Chain(dve, dve_own)
            v = nc.vector
            v.tensor_copy(raw[:, 0:16, :], S.proj[:, 0:16, T - 3:N])
            v.tensor_copy(raw[:, 16:28, :], S.proj[:, NX:NX + 12, T - 3:N]).then_inc(kept, 1)
            dve.wait_ge(kept, 1)
            for lo, n, w, b, buf in ((0, 16, V_CAW, V_CAB, S.cbufa), (16, 12, V_CBW, V_CBB, S.cbufb)):
                o = ys[:, lo:lo + n, :]
                t = ts[:, lo:lo + n, :]
                bv = buf[:, :].rearrange("p (b j r) -> p j r b", b=B, j=3)
                own(v.tensor_tensor(o, raw[:, lo:lo + n, 3:11], bcast(S.vec[:, w + 3 * n:w + 4 * n], 2, B), ALU.mult))
                own(v.tensor_tensor(o, o, bcast(S.vec[:, b:b + n], 2, B), ALU.add))
                for j in range(3):
                    own(v.tensor_tensor(t, bv[:, j], bcast(S.vec[:, w + j * n:w + (j + 1) * n], 2, B), ALU.mult))
                    own(v.tensor_tensor(o, o, t, ALU.add))
            dve.sem_inc(samples, 1)
            for i in range(28):
                dve.wait_ge(first, i + 1)
                for j in (2, 1, 0):
                    d = 3 - j
                    ins = v.scalar_tensor_tensor(out=y[:, i % 4, d:T], in0=S.proj[:, slot(i), 0:T - d], scalar=tap(i, j),
                                                 in1=y[:, i % 4, d:T], op0=ALU.mult, op1=ALU.add)
                    if j:
                        own(ins)
                    else:
                        ins.then_inc(convd, 1)
            dve.wait_ge(used, 29)
            v.tensor_scalar(S.proj[:, NK:NK + 8, :], S.proj[:, NK:NK + 8, :], KSCALE, None, ALU.mult).then_inc(rowed, 1)

            for i in range(7):
                dve.wait_ge(tailed, i + 1)
                v.tensor_copy(tail[0:11, i * 512:(i + 1) * 512], ps[i][0:11, :]).then_inc(rowed, 1)

        @block.tensor
        def _(pe):
            pe.wait_ge(kept, 1)
            for i in range(28):
                mm = nc.tensor.transpose(ps[i // 4][0:11, i % 4 * P:i % 4 * P + P], raw[:, i, :], S.ident[:, :])
                if i % 4 == 3:
                    mm.then_inc(tailed, 1)

        @block.sync
        def _(sp):
            n = 0
            for key, src, cols, at in (("conva", A["state_mlstm_conv"], 2048, 0), ("convb", A["state_ssm_conv"], 1536, 2048)):
                sp.dma_start(O["s_" + key][0, :, 0:2, :], src[0, :, 1:3, :]).then_inc(out_done, 16)
            sp.wait_ge(rowed, 8)
            for key, cols, at in (("conva", 2048, 0), ("convb", 1536, 2048)):
                sp.dma_start(O["p_" + key][0, 0], tail[0:3, at:at + cols]).then_inc(out_done, 16)
                sp.dma_start(O["s_" + key][0, :, 2, :], tail[3:11, at:at + cols]).then_inc(out_done, 16)
            sp.wait_ge(out_done, 16 * 6)


def mlstm_phase(nc, S, R, O):
    with Phase(nc) as ctx:
        sem = ctx.sem
        sb = lambda n, s: ctx.enter_context(nc.sbuf_tensor(n, s, F32))
        V1 = P + 1
        num = sb("num_ml", [P, NC, H_A, V1])
        va = [sb(f"vaug{i}", [P, NC, V1]) for i in range(2)]
        kw = [sb(f"kw{i}", [P, NC, P]) for i in range(2)]
        X = [sb(f"x_ml{i}", [P, NC, L]) for i in range(2)]
        E = [sb(f"e_ml{i}", [P, NC, L]) for i in range(2)]
        C = sb("c_ml", [P, H_A, V1])
        ti = [sb(f"ti_ml{i}", [P, V1]) for i in range(2)]
        sq = sb("sq_ml", [P, H_A, P])
        den, r, mean, var = (sb(f"{n}_ml", [P, NC, H_A]) for n in ("den", "r", "mean", "var"))
        bank = lambda n: ctx.enter_context(nc.psum_tensor(n, [P, 512], F32))
        qk, mb, st = ([bank(f"{n}{i}_ml") for i in range(2)] for n in ("qk", "mb", "st"))
        trk, trv = bank("trk_ml"), bank("trv_ml")
        scored, turned, kv_ready, exps, xs, weighed, stepped, scaled_i, c_ready, num_ready = (
            sem(n + "_ml") for n in ("scored", "turned", "kv_ready", "exps", "xs", "weighed", "stepped", "scaled_i", "c_ready", "num_ready"))
        ones_set, squared, centred, var_ready, rooted, normed, hturned, hmoved, dve_own, act_own, n_out, o_done = (
            sem(n + "_ml") for n in ("ones_set", "squared", "centred", "var_ready", "rooted", "normed", "hturned", "hmoved", "dve_own", "act_own", "n_out", "out_done"))
        block = ctx.enter_context(nc.Block())
        q, k, v = (lambda h, c, s=s: S.proj[:, s + h, c * L:(c + 1) * L] for s in (NQ, NK, NV))
        col = lambda c, quantity, h: S.cols[:, c, quantity, h:h + 1]

        @block.tensor
        def _(pe):
            def scores(h):
                if h >= 2:
                    pe.wait_ge(weighed, h - 1)
                for c in range(NC):
                    nc.tensor.matmul(qk[h % 2][:, c * L:(c + 1) * L], k(h, c), q(h, c), start=True, stop=True)
                nc.tensor.matmul(mb[h % 2][:, :], S.pick[0:H_A, h, :], R.M[:, 0:T], start=True, stop=True).then_inc(scored, 1)
                if h >= 1:
                    pe.wait_ge(kv_ready, h)
                for c in range(NC):
                    nc.tensor.transpose(trk[:, c * L:(c + 1) * L], k(h, c), S.ident[:, :])
                    mm = nc.tensor.transpose(trv[:, c * L:(c + 1) * L], v(h, c), S.ident[:, :])
                mm.then_inc(turned, 1)

            def steps(h):
                pe.wait_ge(weighed, h + 1)
                pe.wait_ge(kv_ready, h + 1)
                for c in range(NC):
                    n = NC * h + c
                    if n >= 2:
                        pe.wait_ge(num_ready, n - 1)
                    nc.tensor.matmul(st[n % 2][:, 0:V1], X[h % 2][:, c, :], va[h % 2][:, c, :], start=True, stop=True)
                    if c:
                        pe.wait_ge(c_ready, n)
                        nc.tensor.matmul(st[n % 2][:, 130:130 + V1], q(h, c), C[:, h, :], start=True, stop=True)
                    nc.tensor.matmul(st[n % 2][:, 260:260 + V1], kw[h % 2][:, c, :], va[h % 2][:, c, :], start=True, stop=True).then_inc(stepped, 1)

            scores(0)
            for h in range(H_A):
                if h + 1 < H_A:
                    scores(h + 1)
                steps(h)
            pe.wait_ge(c_ready, NC * H_A)
            nc.tensor.transpose(mb[0][0:H_A, 0:P], C[:, :, P], S.ident[:, :]).then_inc(n_out, 1)
            pe.wait_ge(normed, 1)
            for h in range(H_A):
                if h >= 2:
                    pe.wait_ge(hmoved, h - 1)
                for c in range(NC):
                    mm = nc.tensor.transpose(qk[h % 2][:, c * L:(c + 1) * L], num[:, c, h, 0:P], S.ident[:, :])
                mm.then_inc(hturned, 1)

        @block.scalar
        def _(act):
            def prepare(h):
                act.wait_ge(turned, h + 1)
                if h >= 2:
                    act.wait_ge(stepped, NC * (h - 1))
                nc.scalar.activation(va[h % 2][:, :, 0:P], trv[:, :].rearrange("p (c l) -> p c l", c=NC), ACT.Copy)
                for c in range(NC):
                    last = nc.scalar.activation(kw[h % 2][:, c, :], trk[:, c * L:(c + 1) * L], ACT.Copy, scale=col(c, 2, h))
                last.then_inc(kv_ready, 1)
                act.wait_ge(xs, h + 1)
                nc.scalar.activation(E[h % 2][:, :, :], X[h % 2][:, :, :], ACT.Exp, scale=-1.0).then_inc(exps, 1)

            act.wait_ge(ones_set, 1)
            prepare(0)
            for h in range(H_A):
                if h + 1 < H_A:
                    prepare(h + 1)
                for c in range(1, NC):
                    n = NC * h + c
                    act.wait_ge(stepped, n + 1)
                    if n >= 2:
                        act.wait_ge(num_ready, n - 1)
                    nc.scalar.activation(ti[n % 2][:, :], st[n % 2][:, 130:130 + V1], ACT.Copy, scale=col(c, 1, h)).then_inc(scaled_i, 1)
            for c in range(NC):
                act.wait_ge(centred, c + 1)
                if c:
                    act.wait_ge(var_ready, c)
                nc.scalar.activation(sq[:, :, :], num[:, c, :, 0:P], ACT.Square).then_inc(squared, 1)
            act.wait_ge(var_ready, NC + 1)
            own = Chain(act, act_own)
            own(nc.scalar.activation(var[:, :, :], var[:, :, :], ACT.Ln))
            nc.scalar.activation(var[:, :, :], var[:, :, :], ACT.Exp, scale=-0.5).then_inc(rooted, 1)

        @block.vector
        def _(dve):
            own = Chain(dve, dve_own)
            V = nc.vector
            for i in range(2):
                last = V.memset(va[i][:, :, P:V1], 1.0)
            last.then_inc(ones_set, 1)

            def weigh(h):
                dve.wait_ge(scored, h + 1)
                if h >= 2:
                    dve.wait_ge(stepped, NC * (h - 1))
                for c in range(NC):
                    last = V.scalar_tensor_tensor(out=X[h % 2][:, c, :], in0=mb[h % 2][:, c * L:(c + 1) * L], scalar=col(c, 0, h),
                                                  in1=S.far[:, :], op0=ALU.subtract, op1=ALU.max)
                last.then_inc(xs, 1)
                dve.wait_ge(exps, h + 1)
                V.tensor_tensor(X[h % 2][:, :, :], E[h % 2][:, :, :], qk[h % 2][:, :].rearrange("p (c l) -> p c l", c=NC), ALU.mult).then_inc(weighed, 1)

            weigh(0)
            for h in range(H_A):
                if h + 1 < H_A:
                    weigh(h + 1)
                for c in range(NC):
                    n = NC * h + c
                    dve.wait_ge(stepped, n + 1)
                    if c:
                        dve.wait_ge(scaled_i, 3 * h + c)
                        V.scalar_tensor_tensor(out=C[:, h, :], in0=C[:, h, :], scalar=S.ba[:, h, c:c + 1],
                                               in1=st[n % 2][:, 260:260 + V1], op0=ALU.mult, op1=ALU.add).then_inc(c_ready, 1)
                        V.tensor_tensor(num[:, c, h, :], ti[n % 2][:, :], st[n % 2][:, 0:V1], ALU.add).then_inc(num_ready, 1)
                    else:
                        V.tensor_copy(C[:, h, :], st[n % 2][:, 260:260 + V1]).then_inc(c_ready, 1)
                        V.tensor_copy(num[:, c, h, :], st[n % 2][:, 0:V1]).then_inc(num_ready, 1)
            dve.wait_ge(n_out, 1)
            V.tensor_copy(S.nrow[:, :], mb[0][0:H_A, 0:P]).then_inc(n_out, 1)
            dve.wait_ge(num_ready, NC * H_A)
            own(V.scalar_tensor_tensor(out=den[:, :, :], in0=num[:, :, :, P], scalar=-1.0, in1=num[:, :, :, P], op0=ALU.mult, op1=ALU.max))
            own(V.tensor_tensor(den[:, :, :], den[:, :, :], S.cols[:, :, 3, 0:H_A], ALU.max))
            own(V.reciprocal(r[:, :, :], den[:, :, :]))
            for c in range(NC):
                h_c = num[:, c, :, 0:P]
                own(V.tensor_tensor(h_c, h_c, bcast(r[:, c, :], 2, P), ALU.mult))
                own(V.reduce_sum(mean[:, c, :], h_c, AX_X))
                own(V.tensor_scalar(mean[:, c, :], mean[:, c, :], 1.0 / P, None, ALU.mult))
                V.tensor_tensor(h_c, h_c, bcast(mean[:, c, :], 2, P), ALU.subtract).then_inc(centred, 1)
                dve.wait_ge(squared, c + 1)
                V.reduce_sum(var[:, c, :], sq[:, :, :], AX_X).then_inc(var_ready, 1)
            dve.wait_ge(var_ready, NC)
            V.tensor_scalar(var[:, :, :], var[:, :, :], 1.0 / P, EPS, ALU.mult, ALU.add).then_inc(var_ready, 1)
            dve.wait_ge(rooted, 1)
            for c in range(NC):
                last = V.tensor_tensor(num[:, c, :, 0:P], num[:, c, :, 0:P], bcast(var[:, c, :], 2, P), ALU.mult)
            last.then_inc(normed, 1)
            for h in range(H_A):
                dve.wait_ge(hturned, h + 1)
                V.scalar_tensor_tensor(out=S.proj[:, NQ + h, 0:T], in0=qk[h % 2][:, :], scalar=S.vec[:, V_GA + h:V_GA + h + 1],
                                       in1=S.proj[:, NO + h, 0:T], op0=ALU.mult, op1=ALU.mult).then_inc(hmoved, 1)

        @block.sync
        def _(sp):
            sp.wait_ge(c_ready, NC * H_A)
            sp.dma_start(O["p_c"][0, 0].rearrange("h d v -> d h v"), C[:, :, 0:P]).then_inc(o_done, 16)
            sp.wait_ge(n_out, 2)
            sp.dma_start(O["p_n"][0, 0], S.nrow[:, :]).then_inc(o_done, 16)
            sp.wait_ge(o_done, 32)


def ssd_phase(nc, S, R, O):
    with Phase(nc) as ctx:
        sem = ctx.sem
        sb = lambda n, s: ctx.enter_context(nc.sbuf_tensor(n, s, F32))
        HG = H_B // G_B
        BC = sb("bc_ssd", [P, NC, L])
        Bt = sb("bt_ssd", [P, NC, P])
        xdt, xw, Y = (sb(f"{n}_ssd", [P, NC, HG, P_B]) for n in ("xdt", "xw", "y"))
        ST = sb("st_ssd", [P, HG, P_B])
        tmp = sb("tmp_ssd", [P, HG, P_B])
        X = [sb(f"x_ssd{i}", [P, NC, L]) for i in range(2)]
        E = [sb(f"e_ssd{i}", [P, NC, L]) for i in range(2)]
        so = sb("so_ssd", [P, 4, P])
        bank = lambda n: ctx.enter_context(nc.psum_tensor(n, [P, 512], F32))
        a, cb, py = ([bank(f"{n}{i}_ssd") for i in range(2)] for n in ("a", "cb", "py"))
        pi, pu = bank("pi_ssd"), bank("pu_ssd")
        names = ("bc_in", "bc_out", "x_in", "x_out", "spread", "xs", "exps", "weighed", "y_in", "y_out", "inter_in", "state", "inter_out",
                 "t_in", "t_out", "so_in", "so_ready", "o_done", "dve_own")
        m = {n: sem(n + "_ssd") for n in names}
        block = ctx.enter_context(nc.Block())
        tok = lambda slot, c: S.proj[:, slot, c * L:(c + 1) * L]
        col = lambda c, quantity, h: S.cols[:, c, quantity, h:h + 1]

        @block.tensor
        def _(pe):
            for g in range(G_B):
                if g:
                    pe.wait_ge(m["t_out"], 4)
                    pe.wait_ge(m["so_ready"], 1)
                for c in range(NC):
                    nc.tensor.matmul(a[0][:, c * L:(c + 1) * L], tok(NX + 8 + g, c), tok(NX + 10 + g, c), start=True, stop=True)
                    mm = nc.tensor.transpose(a[1][:, c * L:(c + 1) * L], tok(NX + 8 + g, c), S.ident[:, :])
                mm.then_inc(m["bc_in"], 1)
                for c in range(NC):
                    if c >= 2:
                        pe.wait_ge(m["x_out"], NC * g + c - 1)
                    for f in range(4):
                        mm = nc.tensor.transpose(py[c % 2][:, f * P:(f + 1) * P], tok(NX + 4 * g + f, c), S.ident[:, :])
                    mm.then_inc(m["x_in"], 1)

                def spread(h):
                    n = HG * g + h
                    if n >= 2:
                        pe.wait_ge(m["xs"], n - 1)
                    nc.tensor.matmul(cb[n % 2][:, :], S.pick[0:H_B, n, :], R.cum[:, 0:T], start=True, stop=True).then_inc(m["spread"], 1)

                spread(0)
                for h in range(HG):
                    n = HG * g + h
                    if h + 1 < HG:
                        spread(h + 1)
                    pe.wait_ge(m["weighed"], n + 1)
                    pe.wait_ge(m["x_out"], NC * (g + 1))
                    if h >= 2:
                        pe.wait_ge(m["y_out"], n - 1)
                    for c in range(NC):
                        mm = nc.tensor.matmul(py[n % 2][:, c * P_B:(c + 1) * P_B], E[n % 2][:, c, :], xdt[:, c, h, :], start=True, stop=True)
                    mm.then_inc(m["y_in"], 1)
                for c in range(NC):
                    n = NC * g + c
                    if n:
                        pe.wait_ge(m["state"], n)
                        pe.wait_ge(m["inter_out"], n)
                    if c:
                        nc.tensor.matmul(pi[:, :], tok(NX + 10 + g, c), ST[:, :, :].rearrange("p h d -> p (h d)"), start=True, stop=True)
                    nc.tensor.matmul(pu[:, :], Bt[:, c, :], xw[:, c, :, :].rearrange("p h d -> p (h d)"), start=True, stop=True).then_inc(m["inter_in"], 1)
                pe.wait_ge(m["inter_out"], NC * (g + 1))
                pe.wait_ge(m["state"], NC * (g + 1))
                pe.wait_ge(m["y_out"], HG * (g + 1))
                for f in range(4):
                    if f >= 2:
                        pe.wait_ge(m["t_out"], 4 * g + f - 1)
                    for c in range(NC):
                        mm = nc.tensor.transpose(a[f % 2][:, c * L:(c + 1) * L], Y[:, c, 2 * f:2 * f + 2, :].rearrange("p h d -> p (h d)"), S.ident[:, :])
                    mm.then_inc(m["t_in"], 1)
                for f in range(4):
                    mm = nc.tensor.transpose(pi[:, f * P:(f + 1) * P], ST[:, 2 * f:2 * f + 2, :].rearrange("p h d -> p (h d)"), S.ident[:, :])
                mm.then_inc(m["so_in"], 1)

        @block.scalar
        def _(act):
            for g in range(G_B):
                act.wait_ge(m["bc_in"], g + 1)
                nc.scalar.activation(BC[:, :, :], a[0][:, :].rearrange("p (c l) -> p c l", c=NC), ACT.Copy)
                nc.scalar.activation(Bt[:, :, :], a[1][:, :].rearrange("p (c l) -> p c l", c=NC), ACT.Copy).then_inc(m["bc_out"], 1)
                for h in range(HG):
                    n = HG * g + h
                    act.wait_ge(m["xs"], n + 1)
                    nc.scalar.activation(X[n % 2][:, :, :], X[n % 2][:, :, :], ACT.Exp, scale=-1.0).then_inc(m["exps"], 1)

        @block.vector
        def _(dve):
            own = Chain(dve, m["dve_own"])
            V = nc.vector
            for g in range(G_B):
                hs = slice(HG * g, HG * (g + 1))
                for c in range(NC):
                    dve.wait_ge(m["x_in"], NC * g + c + 1)
                    px = py[c % 2][:, :].rearrange("p (h d) -> p h d", h=HG)
                    own(V.tensor_tensor(xdt[:, c], px, bcast(S.cols[:, c, 5, hs], 2, P_B), ALU.mult))
                    V.tensor_tensor(xw[:, c], xdt[:, c], bcast(S.cols[:, c, 6, hs], 2, P_B), ALU.mult)
                    V.tensor_tensor(Y[:, c], px, bcast(S.bb[:, hs, 20], 2, P_B), ALU.mult).then_inc(m["x_out"], 1)
                dve.wait_ge(m["x_out"], NC * (g + 1))

                def exponents(h):
                    n = HG * g + h
                    dve.wait_ge(m["spread"], n + 1)
                    for c in range(NC):
                        last = V.scalar_tensor_tensor(out=X[n % 2][:, c, :], in0=cb[n % 2][:, c * L:(c + 1) * L], scalar=col(c, 4, n),
                                                      in1=S.far[:, :], op0=ALU.subtract, op1=ALU.max)
                    last.then_inc(m["xs"], 1)

                def weigh(h):
                    n = HG * g + h
                    dve.wait_ge(m["exps"], n + 1)
                    dve.wait_ge(m["bc_out"], g + 1)
                    if n >= 2:
                        dve.wait_ge(m["y_in"], n - 1)
                    V.tensor_tensor(E[n % 2][:, :, :], X[n % 2][:, :, :], BC[:, :, :], ALU.mult).then_inc(m["weighed"], 1)

                exponents(0)
                weigh(0)
                for h in range(HG):
                    n = HG * g + h
                    if h + 1 < HG:
                        exponents(h + 1)
                        weigh(h + 1)
                    dve.wait_ge(m["y_in"], n + 1)
                    V.tensor_tensor(Y[:, :, h, :], Y[:, :, h, :], py[n % 2][:, 0:NC * P_B].rearrange("p (c d) -> p c d", c=NC), ALU.add).then_inc(m["y_out"], 1)
                for c in range(NC):
                    n = NC * g + c
                    dve.wait_ge(m["inter_in"], n + 1)
                    pu_v = pu[:, :].rearrange("p (h d) -> p h d", h=HG)
                    if c == 0:
                        V.tensor_copy(ST[:, :, :], pu_v).then_inc(m["state"], 1)
                        dve.sem_inc(m["inter_out"], 1)
                        continue
                    own(V.tensor_tensor(ST[:, :, :], ST[:, :, :], bcast(S.bb[:, hs, c], 2, P_B), ALU.mult))
                    V.tensor_tensor(ST[:, :, :], ST[:, :, :], pu_v, ALU.add).then_inc(m["state"], 1)
                    own(V.tensor_tensor(tmp[:, :, :], pi[:, :].rearrange("p (h d) -> p h d", h=HG), bcast(S.cols[:, c, 7, hs], 2, P_B), ALU.mult))
                    V.tensor_tensor(Y[:, c], Y[:, c], tmp[:, :, :], ALU.add).then_inc(m["inter_out"], 1)
                for f in range(4):
                    dve.wait_ge(m["t_in"], 4 * g + f + 1)
                    z = S.proj[:, NZ + 4 * g + f, 0:T]
                    V.tensor_tensor(z, a[f % 2][:, :], z, ALU.mult).then_inc(m["t_out"], 1)
                dve.wait_ge(m["so_in"], g + 1)
                if g:
                    dve.wait_ge(m["o_done"], 16 * g)
                V.tensor_copy(so[:, :, :], pi[:, :].rearrange("p (f n) -> p f n", f=4)).then_inc(m["so_ready"], 1)

        @block.sync
        def _(sp):
            for g in range(G_B):
                sp.wait_ge(m["so_ready"], g + 1)
                sp.dma_start(O["p_ssm"][0, 0, HG * g:HG * (g + 1)].rearrange("(f a) p n -> (a p) f n", a=2), so[:, :, :]).then_inc(m["o_done"], 16)
            sp.wait_ge(m["o_done"], 16 * G_B)


def sample_phase(nc, A, S, O):
    with Phase(nc) as ctx:
        sem = ctx.sem
        sb = lambda n, s: ctx.enter_context(nc.sbuf_tensor(n, s, F32))
        st = [sb(f"state{i}", [P, 4, 8, P]) for i in range(2)]
        vrow = sb("vrow", [B, D])
        brow = sb("brow", [B, 512])
        wk, qn, nd, hh, t1, t2 = (sb(f"{n}_sm", [P, B, H_A]) for n in ("wk", "qn", "nd", "hh", "t1", "t2"))
        dec, dt, yv, xd = (sb(f"{n}_sm", [P, KD, B]) for n in ("dec", "dt", "yv", "xd"))
        dsk = sb("dsk_sm", [P, KD])
        junk = sb("junk_sm", [P, P])
        nrow = sb("nrow_sm", [64, P])
        pr = ctx.enter_context(nc.psum_tensor("pr_sm", [P, 2, 512], F32))
        pv = [ctx.enter_context(nc.psum_tensor(f"pv{i}_sm", [P, 2, 512], F32)) for i in range(2)]
        ph = ctx.enter_context(nc.psum_tensor("ph_sm", [P, 512], F32))
        pm = ctx.enter_context(nc.psum_tensor("pm_sm", [P, 512], F32))
        m = {n: sem(n + "_sm") for n in ("in0", "in1", "turned", "rows", "spread", "updated", "read", "unit", "qn_in", "den_in", "num_in",
                                         "mean_in", "meant", "sq_in", "var_in", "var_out", "rooted", "n_in", "n_out", "o_done0", "o_done1", "o_done", "dve_own", "act_own")}
        block = ctx.enter_context(nc.Block())
        cv = A["state_mlstm_c"][0].rearrange("b h d v -> d b h v")
        sv = A["state_ssm"][0].rearrange("b (c a) p n -> (a p) b c n", a=2)
        oc = O["s_c"][0].rearrange("b h d v -> d b h v")
        os_ = O["s_ssm"][0].rearrange("b (c a) p n -> (a p) b c n", a=2)
        units = [(cv, oc, 0), (cv, oc, 4), (sv, os_, 0), (sv, os_, 4)]

        @block.sync
        def _(sp):
            for u, (src, _, b0) in enumerate(units):
                i = u % 2
                if u >= 2:
                    sp.wait_ge(m["unit"], u - 1)
                    for b in range(4):
                        sp.dma_start(units[u - 2][1][:, units[u - 2][2] + b], st[i][:, b]).then_inc(m[f"o_done{i}"], 16)
                    sp.wait_ge(m[f"o_done{i}"], 64)
                    if u - 2 < 2:
                        sp.wait_ge(m["num_in"], u - 1)
                for b in range(4):
                    sp.dma_start(st[i][:, b], src[:, b0 + b]).then_inc(m[f"in{i}"], 16)
            for u in (2, 3):
                sp.wait_ge(m["unit"], u + 1)
                for b in range(4):
                    sp.dma_start(units[u][1][:, units[u][2] + b], st[u % 2][:, b]).then_inc(m["o_done"], 16)
            sp.wait_ge(m["n_out"], 1)
            sp.dma_start(O["s_n"][0].rearrange("b h d -> (b h) d"), nrow[:, :]).then_inc(m["o_done"], 16)
            sp.wait_ge(m["o_done"], 16 * 9)

        @block.tensor
        def _(pe):
            for k in range(KD):
                nc.tensor.transpose(pr[0:B, k // 4, k % 4 * P:k % 4 * P + P], S.proj[:, NV + k, T:N], S.ident[:, :])
            for k in range(4):
                mm = nc.tensor.transpose(ph[0:B, k * P:(k + 1) * P], S.proj[:, NX + 8 + k, T:N], S.ident[:, :])
            mm.then_inc(m["turned"], 1)
            pe.wait_ge(m["rows"], 1)

            def spread(s):
                b = s % B
                if s >= 2:
                    pe.wait_ge(m["read"], s - 1)
                if s < B:
                    for j in range(2):
                        mm = nc.tensor.matmul(pv[s % 2][:, j, :], S.pick[0:B, b, :], vrow[:, j * 512:(j + 1) * 512], start=True, stop=True)
                else:
                    mm = nc.tensor.matmul(pv[s % 2][:, 0, :], S.pick[0:B, b, :], brow[:, :], start=True, stop=True)
                mm.then_inc(m["spread"], 1)

            for u in range(2):
                for b in range(4 * u, 4 * u + 4):
                    spread(b)
                pe.wait_ge(m["unit"], u + 1)
                for b in range(4 * u, 4 * u + 4):
                    for h in range(H_A):
                        mm = nc.tensor.matmul(pm[:, b * H_A + h:b * H_A + h + 1], st[u][:, b % 4, h, :], S.proj[:, NQ + h, T + b:T + b + 1],
                                              start=True, stop=True)
                mm.then_inc(m["num_in"], 1)
            pe.wait_ge(m["qn_in"], 1)
            nc.tensor.matmul(pm[:, 64:128], S.ones[:, :], qn[:, :, :].rearrange("p b h -> p (b h)"), start=True, stop=True).then_inc(m["den_in"], 1)
            nc.tensor.transpose(pr[0:64, 0, 0:P], S.n0[:, :], S.ident[:, :]).then_inc(m["n_in"], 1)
            pe.wait_ge(m["mean_in"], 1)
            nc.tensor.matmul(pm[:, 128:192], S.ones[:, :], hh[:, :, :].rearrange("p b h -> p (b h)"), start=True, stop=True).then_inc(m["meant"], 1)
            pe.wait_ge(m["sq_in"], 1)
            nc.tensor.matmul(pm[:, 192:256], S.ones[:, :], t1[:, :, :].rearrange("p b h -> p (b h)"), start=True, stop=True).then_inc(m["var_in"], 1)
            for s in range(B, 2 * B):
                spread(s)

        @block.scalar
        def _(act):
            own = Chain(act, m["act_own"])
            act.wait_ge(m["var_out"], 1)
            own(nc.scalar.activation(t2[:, :, :], t2[:, :, :], ACT.Ln))
            nc.scalar.activation(t2[:, :, :], t2[:, :, :], ACT.Exp, scale=-0.5).then_inc(m["rooted"], 1)

        @block.vector
        def _(dve):
            own = Chain(dve, m["dve_own"])
            V = nc.vector
            dve.wait_ge(m["turned"], 1)
            V.tensor_copy(vrow[:, :].rearrange("p (a n) -> p a n", a=2), pr[0:B, :, :])
            V.tensor_copy(brow[:, :], ph[0:B, :]).then_inc(m["rows"], 1)
            perm = lambda t: t.rearrange("p h b -> p b h")
            kT, qT = (perm(S.proj[:, s:s + 8, T:N]) for s in (NK, NQ))
            own(V.tensor_tensor(wk[:, :, :], kT, perm(S.ba[:, :, 12:20]), ALU.mult))
            n0 = S.n0[:, :].rearrange("p (b h) -> p b h", b=B)
            own(V.tensor_tensor(n0, n0, perm(S.ba[:, :, 4:12]), ALU.mult))
            own(V.tensor_tensor(n0, n0, wk[:, :, :], ALU.add))
            V.tensor_tensor(qn[:, :, :], n0, qT, ALU.mult).then_inc(m["qn_in"], 1)
            for a in range(2):
                ps = slice(64 * a, 64 * a + 64)
                V.tensor_copy(dec[ps], S.bb[ps, a::2, 4:12])
                V.tensor_copy(dt[ps], S.bb[ps, a::2, 12:20])
                V.tensor_copy(dsk[ps], S.bb[ps, a::2, 20])
            xs = S.proj[:, NX:NX + KD, T:N]
            dve.wait_ge(m["rows"], 1)
            own(V.memset(yv[:, :, :], 0.0))
            own(V.tensor_tensor(xd[:, :, :], dt[:, :, :], xs, ALU.mult))
            for u in range(2):
                dve.wait_ge(m[f"in{u}"], 64)
                for b in range(4):
                    last = V.tensor_tensor(st[u][:, b], st[u][:, b], bcast(S.ba[:, :, 4 + 4 * u + b], 2, P), ALU.mult)
                own(last)
                for b in range(4):
                    s = 4 * u + b
                    dve.wait_ge(m["spread"], s + 1)
                    for h in range(H_A):
                        last = V.scalar_tensor_tensor(out=st[u][:, b, h, :], in0=pv[s % 2][:, h // 4, h % 4 * P:h % 4 * P + P], scalar=wk[:, s, h:h + 1],
                                                      in1=st[u][:, b, h, :], op0=ALU.mult, op1=ALU.add)
                    last.then_inc(m["read"], 1)
                dve.wait_ge(m["read"], 4 * u + 4)
                dve.sem_inc(m["unit"], 1)
            dve.wait_ge(m["den_in"], 1)
            dve.wait_ge(m["num_in"], 2)
            flat = lambda t: t.rearrange("p b h -> p (b h)")
            own(V.tensor_copy(flat(nd[:, :, :]), pm[:, 64:128]))
            own(V.scalar_tensor_tensor(out=nd[:, :, :], in0=nd[:, :, :], scalar=-1.0, in1=nd[:, :, :], op0=ALU.mult, op1=ALU.max))
            own(V.tensor_tensor(nd[:, :, :], nd[:, :, :], perm(S.ba[:, :, 20:28]), ALU.max))
            own(V.reciprocal(nd[:, :, :], nd[:, :, :]))
            V.tensor_tensor(flat(hh[:, :, :]), pm[:, 0:64], flat(nd[:, :, :]), ALU.mult).then_inc(m["mean_in"], 1)
            dve.wait_ge(m["meant"], 1)
            own(V.scalar_tensor_tensor(out=flat(hh[:, :, :]), in0=pm[:, 128:192], scalar=-1.0 / P, in1=flat(hh[:, :, :]), op0=ALU.mult, op1=ALU.add))
            V.tensor_tensor(t1[:, :, :], hh[:, :, :], hh[:, :, :], ALU.mult).then_inc(m["sq_in"], 1)
            dve.wait_ge(m["var_in"], 1)
            V.tensor_scalar(flat(t2[:, :, :]), pm[:, 192:256], 1.0 / P, EPS, ALU.mult, ALU.add).then_inc(m["var_out"], 1)
            dve.wait_ge(m["rooted"], 1)
            own(V.tensor_tensor(hh[:, :, :], hh[:, :, :], t2[:, :, :], ALU.mult))
            own(V.tensor_tensor(hh[:, :, :], hh[:, :, :], bcast(S.vec[:, V_GA:V_GA + 8], 1, B), ALU.mult))
            V.tensor_tensor(qT, hh[:, :, :], perm(S.proj[:, NO:NO + 8, T:N]), ALU.mult)
            dve.wait_ge(m["n_in"], 1)
            V.tensor_copy(nrow[:, :], pr[0:64, 0, 0:P]).then_inc(m["n_out"], 1)
            for u in range(2):
                dve.wait_ge(m[f"in{u}"], 128)
                for b in range(4):
                    last = V.tensor_tensor(st[u][:, b], st[u][:, b], bcast(dec[:, :, 4 * u + b], 2, P), ALU.mult)
                own(last)
                for b in range(4):
                    s = 4 * u + b
                    dve.wait_ge(m["spread"], B + s + 1)
                    for c in range(KD):
                        g = c // 4
                        last = V.scalar_tensor_tensor(out=st[u][:, b, c, :], in0=pv[s % 2][:, 0, g * P:(g + 1) * P], scalar=xd[:, c, s:s + 1],
                                                      in1=st[u][:, b, c, :], op0=ALU.mult, op1=ALU.add)
                    own(last)
                    for c in range(KD):
                        g = c // 4
                        own(V.tensor_tensor_reduce(out=junk[:, :], in0=pv[s % 2][:, 0, 256 + g * P:256 + (g + 1) * P], in1=st[u][:, b, c, :],
                                                   scale=1.0, scalar=0.0, op0=ALU.mult, op1=ALU.add, accum_out=yv[:, c, s:s + 1]))
                    dve.sem_inc(m["read"], 1)
                dve.sem_inc(m["unit"], 1)
            own(V.tensor_tensor(xd[:, :, :], xs, bcast(dsk[:, :], 2, B), ALU.mult))
            own(V.tensor_tensor(yv[:, :, :], yv[:, :, :], xd[:, :, :], ALU.add))
            own(V.tensor_tensor(S.proj[:, NZ:NZ + KD, T:N], yv[:, :, :], S.proj[:, NZ:NZ + KD, T:N], ALU.mult))


NB = [TOPK // (a + 1) for a in range(TOPK)]
NCAND = sum(NB)
LOW = -3.0e38
TB = 40
NTB = N // TB
JG = 4
NG = NKEY // JG


def residual_phase(nc, name, S, src, gate):
    with Phase(nc) as ctx:
        own_s = ctx.sem(f"own_{name}")
        t = ctx.enter_context(nc.sbuf_tensor(f"t_{name}", [P, KD, B], F32))
        block = ctx.enter_context(nc.Block())

        @block.vector
        def _(dve):
            own = Chain(dve, own_s)
            for k in range(KD):
                nc.vector.scalar_tensor_tensor(out=S.xT[:, k, 0:T], in0=src[:, k, 0:T], scalar=S.mod[:, gate + k, 0:1],
                                               in1=S.xT[:, k, 0:T], op0=ALU.mult, op1=ALU.add)
            own(nc.vector.tensor_tensor(t[:, :, :], src[:, :, T:N], S.mod[:, gate:gate + KD, 1:9], ALU.mult))
            own(nc.vector.tensor_tensor(S.xT[:, :, T:N], S.xT[:, :, T:N], t[:, :, :], ALU.add))


def topk_phase(nc, A, S, qry):
    with Phase(nc) as ctx:
        sem = ctx.sem
        sb = lambda n, s, d=F32: ctx.enter_context(nc.sbuf_tensor(n, s, d))
        keys = sb("keys", [P, 2, P])
        keysT = sb("keysT", [P, 2, P])
        wk = sb("wk_tk", [P, 16, NKEY])
        top = sb("top_tk", [P, 16, TOPK])
        idx = sb("idx_tk", [P, 16, TOPK], U32)
        idf = sb("idf_tk", [P, 16, TOPK])
        cand = sb("cand_tk", [P, PH, NCAND])
        cidx = sb("cidx_tk", [P, PH, NCAND])
        cwk = sb("cwk_tk", [P, PH, NCAND])
        best = sb("best_tk", [P, PH, TOPK])
        pos = sb("pos_tk", [P, PH, TOPK], U32)
        posf = sb("posf_tk", [P, PH, TOPK])
        hit = sb("hit_tk", [P, PH * TOPK, NCAND])
        ei = sb("ei_tk", [P, PH * TOPK])
        eu = sb("eu_tk", [P, 2, PH * TOPK], U32)
        res = sb("res_tk", [P, 3, PH * TOPK])
        ssum = sb("ssum_tk", [P, PH])
        ps = [ctx.enter_context(nc.psum_tensor(f"ps_tk{i}", [P, 4, P], F32)) for i in range(5)]
        pk = ctx.enter_context(nc.psum_tensor("pk_tk", [P, 4, P], F32))
        m = {n: sem(n + "_tk") for n in ("keys_in", "keys_t", "keys_s", "scored", "read", "hit", "picked", "shifted", "gates", "res", "res_t", "res_s", "dve_own")}
        block = ctx.enter_context(nc.Block())
        tiles = [(t * L, L) for t in range(NC)] + [(T, B)]

        @block.sync
        def _(sp):
            sp.dma_start(keys[:, :, :], A["peer_sub_keys"][0].rearrange("j k d -> k j d")).then_inc(m["keys_in"], 16)
            sp.wait_ge(m["keys_in"], 16)

        @block.tensor
        def _(pe):
            pe.wait_ge(m["keys_in"], 16)
            nc.tensor.transpose(pk[:, 0, :], keys[:, 0, :], S.ident[:, :])
            nc.tensor.transpose(pk[:, 1, :], keys[:, 1, :], S.ident[:, :]).then_inc(m["keys_t"], 1)
            pe.wait_ge(m["keys_s"], 1)
            for t, (at, n) in enumerate(tiles):
                if t:
                    pe.wait_ge(m["read"], t)
                for q in range(4):
                    for i in range(4):
                        l = 4 * q + i
                        mm = nc.tensor.matmul(ps[q][0:n, i, :], qry[:, l, at:at + n], keysT[:, l % 2, :], start=True, stop=True)
                mm.then_inc(m["scored"], 1)
                pe.wait_ge(m["res"], t + 1)
                if t:
                    pe.wait_ge(m["res_s"], t)
                for q in range(3):
                    mm = nc.tensor.transpose(ps[4][:, q, 0:n], res[0:n, q, :], S.ident[0:n, 0:n])
                mm.then_inc(m["res_t"], 1)

        @block.scalar
        def _(act):
            act.wait_ge(m["keys_t"], 1)
            nc.scalar.activation(keysT[:, :, :], pk[:, 0:2, :], ACT.Copy).then_inc(m["keys_s"], 1)
            for t, (at, n) in enumerate(tiles):
                act.wait_ge(m["shifted"], t + 1)
                nc.scalar.activation(best[0:n, :, :], best[0:n, :, :], ACT.Exp).then_inc(m["gates"], 1)
                act.wait_ge(m["res_t"], t + 1)
                nc.scalar.activation(S.selT[:, :, at:at + n], ps[4][:, 0:3, 0:n], ACT.Copy).then_inc(m["res_s"], 1)

        @block.gpsimd
        def _(pool):
            for t, (at, n) in enumerate(tiles):
                pool.wait_ge(m["hit"], t + 1)
                h4 = hit[0:n, :, :].rearrange("p (h k) c -> p h k c", h=PH)
                for h in range(PH):
                    last = nc.gpsimd.tensor_tensor(h4[:, h], h4[:, h], bcast(cidx[0:n, h, :], 1, TOPK), ALU.mult)
                last.then_inc(m["picked"], 1)

        @block.vector
        def _(dve):
            own = Chain(dve, m["dve_own"])
            V = nc.vector
            for t, (at, n) in enumerate(tiles):
                dve.wait_ge(m["scored"], t + 1)
                for half in range(2):
                    src = [ps[l // 4][0:n, l % 4, :] if half == 0 else wk[0:n, l, :] for l in range(16)]
                    at8 = slice(8 * half, 8 * half + 8)
                    for l in range(16):
                        last = V.max(top[0:n, l, at8], src[l])
                    own(last)
                    for l in range(16):
                        last = V.max_index(idx[0:n, l, at8], top[0:n, l, at8], src[l])
                        if half == 0:
                            last = V.match_replace(wk[0:n, l, :], top[0:n, l, at8], src[l], LOW)
                    if half:
                        own(last)
                    else:
                        own(last)
                        dve.sem_inc(m["read"], 1)
                own(V.tensor_copy(idf[0:n, :, :], idx[0:n, :, :]))
                t4 = top[0:n, :, :].rearrange("p (h j) k -> p h j k", j=2)
                i4 = idf[0:n, :, :].rearrange("p (h j) k -> p h j k", j=2)
                own(V.tensor_scalar(i4[:, :, 0, :], i4[:, :, 0, :], float(NKEY), None, ALU.mult))
                off = 0
                for a in range(9):
                    if a < 8:
                        o = slice(off, off + NB[a])
                        V.tensor_tensor(cand[0:n, :, o], bcast(t4[:, :, 0, a], 2, NB[a]), t4[:, :, 1, 0:NB[a]], ALU.add)
                        last = V.tensor_tensor(cidx[0:n, :, o], bcast(i4[:, :, 0, a], 2, NB[a]), i4[:, :, 1, 0:NB[a]], ALU.add)
                        off += NB[a]
                    else:
                        o = slice(off, off + 8)
                        V.tensor_tensor(cand[0:n, :, o], t4[:, :, 0, 8:16], t4[:, :, 1, 0:1].to_broadcast((n, PH, 8)), ALU.add)
                        last = V.tensor_tensor(cidx[0:n, :, o], i4[:, :, 0, 8:16], i4[:, :, 1, 0:1].to_broadcast((n, PH, 8)), ALU.add)
                own(last)
                for half in range(2):
                    src = cand if half == 0 else cwk
                    at8 = slice(8 * half, 8 * half + 8)
                    for h in range(PH):
                        last = V.max(best[0:n, h, at8], src[0:n, h, :])
                    own(last)
                    for h in range(PH):
                        last = V.max_index(pos[0:n, h, at8], best[0:n, h, at8], src[0:n, h, :])
                        if half == 0:
                            last = V.match_replace(cwk[0:n, h, :], best[0:n, h, at8], src[0:n, h, :], LOW)
                    own(last)
                own(V.tensor_copy(posf[0:n, :, :], pos[0:n, :, :]))
                if t:
                    dve.wait_ge(m["picked"], t)
                V.tensor_tensor(hit[0:n, :, :], bcast(posf[0:n, :, :].rearrange("p h k -> p (h k)"), 2, NCAND),
                                bcast(S.iota[0:n, 0:NCAND], 1, PH * TOPK), ALU.is_equal).then_inc(m["hit"], 1)
                own(V.tensor_copy(ssum[0:n, :], best[0:n, :, 0]))
                V.tensor_tensor(best[0:n, :, :], best[0:n, :, :], bcast(ssum[0:n, :], 2, TOPK), ALU.subtract).then_inc(m["shifted"], 1)
                dve.wait_ge(m["gates"], t + 1)
                own(V.reduce_sum(ssum[0:n, :], best[0:n, :, :], AX_X))
                own(V.reciprocal(ssum[0:n, :], ssum[0:n, :]))
                if t:
                    dve.wait_ge(m["res_t"], t)
                V.tensor_tensor(res[0:n, 2, :].rearrange("p (h k) -> p h k", h=PH), best[0:n, :, :], bcast(ssum[0:n, :], 2, TOPK), ALU.mult)
                dve.wait_ge(m["picked"], t + 1)
                own(V.reduce_sum(ei[0:n, :], hit[0:n, :, :], AX_X))
                own(V.tensor_copy(eu[0:n, 0, :], ei[0:n, :]))
                V.tensor_scalar(eu[0:n, 1, :], eu[0:n, 0, :], NKEY - 1, None, ALU.bitwise_and)
                own(V.tensor_scalar(ei[0:n, :].bitcast(U32), eu[0:n, 0, :], 7, None, ALU.logical_shift_right))
                V.tensor_copy(res[0:n, 0, :], ei[0:n, :].bitcast(U32))
                V.tensor_copy(res[0:n, 1, :], eu[0:n, 1, :]).then_inc(m["res"], 1)


def gate_matrix_phase(nc, S, gates):
    with Phase(nc) as ctx:
        sem = ctx.sem
        sb = lambda n, s: ctx.enter_context(nc.sbuf_tensor(n, s, F32))
        pick = sb("pick_gm", [P, 2, 3, TB])
        oh = sb("oh_gm", [P, 2, 4, 2, P])
        stage = sb("stage_gm", [P, 2, NG, JG, TB])
        ps = [ctx.enter_context(nc.psum_tensor(f"ps_gm{i}", [P, 4, P], F32)) for i in range(2)]
        own_s, hot, multiplied, staged = sem("dve_own_gm"), sem("hot"), sem("multiplied_gm"), sem("staged")
        stored = [sem(f"stored{i}") for i in range(2)]
        block = ctx.enter_context(nc.Block())
        Q = TB // 4
        gv = gates.rearrange("g i b e -> i b g e")
        blocks = NTB + 1
        assert NTB % 2 == 1 and Q % 2 == 0

        def vec_block(dve, i, s):
            V = nc.vector
            V.tensor_copy(pick[:, s, :, :], S.selT[:, :, bass.ds(i * (2 * TB) + s * TB, TB)]).then_inc(own_s, 1)
            dve.wait_ge(own_s, 2 * i + (s + 1))
            for q in range(Q):
                dve.wait_ge(multiplied, 2 * Q * i + (Q * s + q + 1))
                for u in range(4):
                    k = 4 * q + u
                    V.tensor_scalar(oh[:, q % 2, u, 0, :], S.iota[:, :], pick[:, s, 0, k:k + 1], None, ALU.is_equal)
                    last = V.tensor_scalar(oh[:, q % 2, u, 1, :], S.iota[:, :], pick[:, s, 1, k:k + 1], pick[:, s, 2, k:k + 1], ALU.is_equal, ALU.mult)
                last.then_inc(hot, 1)

        def pe_block(pe, i, s):
            for q in range(Q):
                pe.wait_ge(hot, 2 * Q * i + (Q * s + q + 1))
                pe.wait_ge(staged, 2 * Q * i + (Q * s + q + 1))
                for u in range(4):
                    mm = nc.tensor.matmul(ps[q % 2][:, u, :], oh[:, q % 2, u, 0, :], oh[:, q % 2, u, 1, :], start=True, stop=True)
                mm.then_inc(multiplied, 1)

        def act_block(act, i, s):
            act.wait_ge(stored[s], 16 * i + 16)
            for q in range(Q):
                act.wait_ge(multiplied, 2 * Q * i + (Q * s + q + 3))
                nc.scalar.activation(stage[:, s, :, :, 4 * q:4 * q + 4].rearrange("p g j t -> p t (g j)"), ps[q % 2][:, :, :], ACT.Copy).then_inc(staged, 1)

        def sp_block(sp, i, s):
            sp.wait_ge(staged, 2 * Q * i + (Q * (s + 1) + 2))
            sp.dma_start(gv[:, bass.ds(2 * i + s, 1), :, :].rearrange("i b g e -> i (b g) e"),
                         stage[:, s, :, :, :].rearrange("p g j t -> p g (j t)")).then_inc(stored[s], 16)

        def whole(engine, body):
            with engine.Fori(0, NTB // 2) as i:
                for s in range(2):
                    body(engine, i, s)
            body(engine, NTB // 2, 0)

        @block.vector
        def _(dve):
            whole(dve, vec_block)

        @block.tensor
        def _(pe):
            pe.sem_inc(multiplied, 2)
            whole(pe, pe_block)

        @block.scalar
        def _(act):
            act.sem_inc(staged, 2)
            for s in range(2):
                act.sem_inc(stored[s], 16)
            whole(act, act_block)

        @block.sync
        def _(sp):
            whole(sp, sp_block)
            sp.wait_ge(stored[0], 16 * (NTB // 2 + 2))
            sp.wait_ge(stored[1], 16 * (NTB // 2 + 1))


def expert_phase(nc, A, S, gates):
    with Phase(nc) as ctx:
        sem = ctx.sem
        sb = lambda n, s: ctx.enter_context(nc.sbuf_tensor(n, s, F32))
        ub = [sb(f"u{i}", [P, JG, D]) for i in range(2)]
        vb = [sb(f"v{i}", [P, JG, D]) for i in range(2)]
        gb = [sb(f"g{i}", [P, NTB, JG, TB]) for i in range(2)]
        ut = [sb(f"ut{i}", [P, KD, P]) for i in range(2)]
        ge = [sb(f"ge{i}", [P, N]) for i in range(2)]
        W = sb("w_ex", [P, JG, N])
        pt = [ctx.enter_context(nc.psum_tensor(f"pt_ex{i}", [P, 4, P], F32)) for i in range(2)]
        pa = [ctx.enter_context(nc.psum_tensor(f"pa_ex{i}", [P, 512], F32)) for i in range(2)]
        po = [ctx.enter_context(nc.psum_tensor(f"po_ex{i}", [P, 2, 512], F32)) for i in range(2)]
        u_in, v_in, g_in = ([sem(f"{n}_in{i}") for i in range(2)] for n in "uvg")
        turned, moved_lo, moved_hi, hidden, gelued, weighted, mixed, added, used_v = (
            sem(n + "_ex") for n in ("turned", "moved_lo", "moved_hi", "hidden", "gelued", "weighted", "mixed", "added", "used_v"))
        zero = sem("zero_ex")
        block = ctx.enter_context(nc.Block())
        uv = A["peer_u"][0].rearrange("(i j) d -> i j d", j=NKEY)
        vv = A["peer_v"][0].rearrange("(i j) d -> i j d", j=NKEY)
        KP = KD // 2

        @block.sync
        def _(sp):
            with sp.Fori(0, NG // 2) as i:
                for s in range(2):
                    g = 2 * i + s
                    sp.wait_ge(turned, 4 * JG * i + 2 * JG * (s + 1))
                    sp.dma_start(ub[s][:, :, :], uv[:, bass.ds(8 * i + 4 * s, JG), :]).then_inc(u_in[s], 16)
                    sp.wait_ge(weighted, 2 * JG * i + JG * (s + 1))
                    sp.dma_start(gb[s][:, :, :, :].rearrange("p b j t -> p (b j t)"),
                                 gates[bass.ds(2 * i + s, 1)].rearrange("g i b e -> (g i) (b e)")).then_inc(g_in[s], 16)
                    sp.wait_ge(used_v, 2 * i + (s + 1))
                    sp.dma_start(vb[s][:, :, :], vv[:, bass.ds(8 * i + 4 * s, JG), :]).then_inc(v_in[s], 16)

        @block.tensor
        def _(pe):
            pe.sem_inc(turned, 4 * JG)
            pe.sem_inc(used_v, 2)
            pe.sem_inc(mixed, 1)
            with pe.Fori(0, NG // 2) as i:
                for s in range(2):
                    def turn(j):
                        for x in range(2):
                            pe.wait_ge((moved_lo, moved_hi)[x], 2 * JG * i + (JG * s + j + 1))
                            for k in range(4):
                                mm = nc.tensor.transpose(pt[x][:, k, :], ub[s][:, j, (4 * x + k) * P:(4 * x + k + 1) * P], S.ident[:, :])
                            mm.then_inc(turned, 1)

                    def hide(j):
                        pe.wait_ge(moved_lo, 2 * JG * i + (JG * s + j + 2))
                        pe.wait_ge(moved_hi, 2 * JG * i + (JG * s + j + 2))
                        for h in range(2):
                            pe.wait_ge(gelued, 4 * JG * i + (2 * (JG * s + j) + h + 1))
                            for k in range(KD):
                                mm = nc.tensor.matmul(pa[h][:, 0:HN], ut[j % 2][:, k, :], S.h2T[:, k, h * HN:(h + 1) * HN],
                                                      start=(k == 0), stop=(k == KD - 1))
                            mm.then_inc(hidden, 1)

                    pe.wait_ge(u_in[s], 16 * i + 16)
                    turn(0)
                    for j in range(JG):
                        if j + 1 < JG:
                            turn(j + 1)
                        hide(j)
                    pe.wait_ge(v_in[s], 16 * i + 16)
                    for kp in range(KP):
                        pe.wait_ge(added, 2 * KD * i + (KD * s + 2 * kp + 2))
                        for j in range(JG):
                            if kp == 0:
                                pe.wait_ge(weighted, 2 * JG * i + (JG * s + j + 1 + 2 * JG))
                            for x in range(2):
                                k = 2 * kp + x
                                for h in range(2):
                                    mm = nc.tensor.matmul(po[x][:, h, 0:HN], vb[s][:, j, k * P:(k + 1) * P], W[:, j, h * HN:(h + 1) * HN],
                                                          start=(j == 0), stop=(j == JG - 1))
                                if j == JG - 1:
                                    mm.then_inc(mixed, 1)

        @block.scalar
        def _(act):
            act.sem_inc(moved_lo, 1)
            act.sem_inc(gelued, 2)
            with act.Fori(0, NG // 2) as i:
                for s in range(2):
                    def move(j):
                        act.wait_ge(turned, 4 * JG * i + (2 * (JG * s + j) + 1 + 4 * JG))
                        act.wait_ge(hidden, 4 * JG * i + (2 * (JG * s + j) + 2))
                        nc.scalar.activation(ut[j % 2][:, 0:4, :], pt[0][:, :, :], ACT.Copy).then_inc(moved_lo, 1)

                    move(0)
                    for j in range(JG):
                        if j + 1 < JG:
                            move(j + 1)
                        for h in range(2):
                            n = 2 * (JG * s + j) + h
                            act.wait_ge(hidden, 4 * JG * i + (n + 1 + 4))
                            if h == 0:
                                act.wait_ge(weighted, 2 * JG * i + (JG * s + j + 2 * JG - 1))
                            nc.scalar.activation(ge[j % 2][:, h * HN:(h + 1) * HN], pa[h][:, 0:HN], ACT.Gelu).then_inc(gelued, 1)

        @block.vector
        def _(dve):
            V = nc.vector
            V.memset(S.acc[:, :, :], 0.0).then_inc(zero, 1)
            dve.wait_ge(zero, 1)
            dve.sem_inc(moved_hi, 1)
            dve.sem_inc(hidden, 4)
            dve.sem_inc(weighted, 2 * JG)
            dve.sem_inc(added, 2)
            with dve.Fori(0, NG // 2) as i:
                for s in range(2):
                    def move(j):
                        dve.wait_ge(turned, 4 * JG * i + (2 * (JG * s + j) + 2 + 4 * JG))
                        dve.wait_ge(hidden, 4 * JG * i + (2 * (JG * s + j) + 2))
                        V.tensor_copy(ut[j % 2][:, 4:8, :], pt[1][:, :, :]).then_inc(moved_hi, 1)

                    move(0)
                    for j in range(JG):
                        if j + 1 < JG:
                            move(j + 1)
                        if j == 0:
                            dve.wait_ge(g_in[s], 16 * i + 16)
                            dve.wait_ge(mixed, 2 * KD * i + (KD * s + 1))
                        dve.wait_ge(gelued, 4 * JG * i + (2 * (JG * s + j) + 4))
                        V.tensor_tensor(W[:, j, :].rearrange("p (b t) -> p b t", t=TB), ge[j % 2][:, :].rearrange("p (b t) -> p b t", t=TB),
                                        gb[s][:, :, j, :], ALU.mult).then_inc(weighted, 1)
                    for k in range(KD):
                        dve.wait_ge(mixed, 2 * KD * i + (KD * s + k + 2))
                        V.tensor_tensor(halves(S.acc[:, k, :]), halves(S.acc[:, k, :]), po[k % 2][:, :, 0:HN], ALU.add).then_inc(added, 1)
                    dve.sem_inc(used_v, 1)


def output_phase(nc, S, O, y):
    with Phase(nc) as ctx:
        st = [ctx.enter_context(nc.sbuf_tensor(f"st_out{i}", [P, 2, 512], F32)) for i in range(2)]
        ps = [ctx.enter_context(nc.psum_tensor(f"ps_out{i}", [P, 2, 512], F32)) for i in range(2)]
        turned, moved, done = (ctx.sem(n + "_out") for n in ("turned", "moved", "done"))
        block = ctx.enter_context(nc.Block())
        tiles = [(t * L, L, O["y_p"][0, t * L:(t + 1) * L, :]) for t in range(NC)] + [(T, B, O["y_s"].rearrange("b t d -> (b t) d"))]

        @block.tensor
        def _(pe):
            for t, (at, n, _) in enumerate(tiles):
                if t >= 2:
                    pe.wait_ge(moved, t - 1)
                for k in range(KD):
                    mm = nc.tensor.transpose(ps[t % 2][0:n, k // 4, k % 4 * P:k % 4 * P + P], y[:, k, at:at + n], S.ident[:, :])
                mm.then_inc(turned, 1)

        @block.scalar
        def _(act):
            for t, (_, n, _) in enumerate(tiles):
                act.wait_ge(turned, t + 1)
                if t >= 2:
                    act.wait_ge(done, 16 * (t - 1))
                nc.scalar.activation(st[t % 2][0:n], ps[t % 2][0:n], ACT.Copy).then_inc(moved, 1)

        @block.sync
        def _(sp):
            for t, (_, n, dst) in enumerate(tiles):
                sp.wait_ge(moved, t + 1)
                sp.dma_start(dst, st[t % 2][0:n].rearrange("p a b -> p (a b)")).then_inc(done, 16)
                sp.wait_ge(done, 16 * (t + 1))


class Buffers:
    pass


def program(nc, A, O, gates):
    S, R = Buffers(), Buffers()
    with ExitStack() as whole:
        def sb(ctx, name, shape, dt=F32):
            t = ctx.enter_context(nc.sbuf_tensor(name, shape, dt))
            return t

        S.ident = sb(whole, "ident", [P, P])
        S.ones = sb(whole, "ones", [P, P])
        S.iota = sb(whole, "iota", [P, P])
        S.vec = sb(whole, "vec", [P, NVEC])
        S.mod = sb(whole, "mod", [P, 48, 9])
        S.rb = sb(whole, "rb", [P, N])
        S.gs = sb(whole, "gs", [P, KD, 9])
        S.xT = sb(whole, "xT", [P, KD, N])
        with ExitStack() as mixers:
            S.far = sb(mixers, "far", [P, P])
            S.wg = sb(mixers, "wg", [P, KD, 96])
            S.col = sb(mixers, "col", [H_B, 5])
            S.m0T = sb(mixers, "m0T", [H_A, B])
            S.silc = sb(mixers, "silc", [P, KD, 9])
            S.n0 = sb(mixers, "n0", [P, 64])
            S.cbufa = sb(mixers, "cbufa", [P, 384])
            S.cbufb = sb(mixers, "cbufb", [P, 288])
            S.pick = sb(mixers, "pick", [H_B, H_B, P])
            S.ea = sb(mixers, "ea", [H_B, 1])
            S.mS = sb(mixers, "mS", [H_A, B])
            S.mP = sb(mixers, "mP", [H_A, 1])
            S.cols = sb(mixers, "cols", [P, NC, 8, H_B])
            S.ba = sb(mixers, "ba", [P, H_A, 28])
            S.bb = sb(mixers, "bb", [P, H_B, 21])
            S.nrow = sb(mixers, "nrow", [H_A, P])
            R.a = sb(mixers, "row_a", [H_A, N])
            R.M = sb(mixers, "row_M", [H_A, N])
            R.cum = sb(mixers, "row_cum", [H_B, N])
            R.dt = sb(mixers, "row_dt", [H_B, N])
            setup_phase(nc, A, S)
            project(nc, "ada", [(0, 6, 0)], A["w_ada"][0], KD, lambda k: S.silc[:, k, :], 9,
                    lambda c, bank: nc.scalar.activation(S.mod[:, bass.ds(c, 1), :], bank[:, 0:1, 0:9], ACT.Copy))
            with Phase(nc) as ctx:
                added = ctx.sem("bias_added")
                block = ctx.enter_context(nc.Block())

                @block.vector
                def _(dve):
                    nc.vector.tensor_tensor(S.mod[:, :, :], S.mod[:, :, :], bcast(S.vec[:, V_BADA:V_BADA + 48], 2, 9), ALU.add).then_inc(added, 1)
                    dve.wait_ge(added, 1)

            S.proj = sb(mixers, "proj", [P, SLOTS, N])
            with ExitStack() as ctx:
                S.hT = sb(ctx, "hT", [P, KD, N])
                norm_phase(nc, "n1", S, lambda k: S.xT[:, k, :], KD, modulate(nc, S, S.hT, V_N1, 0, 8))
                keep = lambda c, bank: nc.scalar.activation(S.proj[:, bass.ds(c, 1), :].rearrange("p c (a n) -> p (c a) n", a=2), bank[:, :, 0:HN], ACT.Copy)
                project(nc, "in", [(0, 4, 0), (Z0, 2, NZ)], A["w_in"][0], KD, lambda k: S.hT[:, k, :], N, keep)
                project(nc, "in2", [(Z0 + 4 * 512 - 512, 1, NZ + 12)], A["w_in"][0], KD, lambda k: S.hT[:, k, :], N, keep)
                gates_phase(nc, A, S, R, O)
            conv_phase(nc, A, S, O)
            mlstm_phase(nc, S, R, O)
            ssd_phase(nc, S, R, O)
            sample_phase(nc, A, S, O)

            def gain(dve, own):
                for k in range(KD):
                    last = nc.vector.scalar_tensor_tensor(out=S.proj[:, NZ + k, :], in0=S.proj[:, NZ + k, :], scalar=S.vec[:, V_GB + k:V_GB + k + 1],
                                                          in1=S.rb[:, :], op0=ALU.mult, op1=ALU.mult)
                own(last)
            norm_phase(nc, "ssm", S, lambda k: S.proj[:, NZ + k, :], KD, gain)
            mixed = lambda c, bank: nc.scalar.activation(S.proj[:, bass.ds(c + NK, 1), :].rearrange("p c (a n) -> p (c a) n", a=2), bank[:, :, 0:HN], ACT.Copy)
            project(nc, "out", [(0, 2, 0)], A["w_out"][0], 2 * KD, lambda k: S.proj[:, (NQ + k if k < KD else NZ + k - KD), :], N, mixed)
            residual_phase(nc, "r1", S, S.proj[:, NK:NK + KD, :], 16)
        S.h2T = sb(whole, "h2T", [P, KD, N])
        norm_phase(nc, "n2", S, lambda k: S.xT[:, k, :], KD, modulate(nc, S, S.h2T, V_N2, 24, 32))
        S.acc = sb(whole, "acc", [P, KD, N])
        with ExitStack() as ctx:
            S.selT = sb(ctx, "selT", [P, 3, N])
            with ExitStack() as ctx2:
                qry = sb(ctx2, "qry", [P, 16, N])
                project(nc, "query", [(0, 2, 0)], A["peer_w_query"][0], KD, lambda k: S.h2T[:, k, :], N,
                        lambda c, bank: nc.scalar.activation(qry[:, bass.ds(c, 1), :].rearrange("p c (a n) -> p (c a) n", a=2), bank[:, :, 0:HN], ACT.Copy))
                topk_phase(nc, A, S, qry)
            gate_matrix_phase(nc, S, gates)
        expert_phase(nc, A, S, gates)
        residual_phase(nc, "r2", S, S.acc, 40)

        def final(dve, own):
            for k in range(KD):
                last = nc.vector.scalar_tensor_tensor(out=S.acc[:, k, :], in0=S.xT[:, k, :], scalar=S.vec[:, V_GF + k:V_GF + k + 1],
                                                      in1=S.rb[:, :], op0=ALU.mult, op1=ALU.mult)
            own(last)
        norm_phase(nc, "nf", S, lambda k: S.xT[:, k, :], KD, final)
        output_phase(nc, S, O, S.acc)


_INS = ["x_prompt", "x_sample", "c_prompt", "c_sample", "state_mlstm_c", "state_mlstm_n", "state_mlstm_m", "state_mlstm_conv",
        "state_ssm", "state_ssm_conv", "w_ada", "b_ada", "norm1_g", "norm2_g", "w_in", "mlstm_gate_b", "conv_a_w", "conv_a_b",
        "mlstm_norm_g", "conv_b_w", "conv_b_b", "dt_bias", "a_log", "d_skip", "ssm_norm_g", "w_out", "peer_w_query",
        "peer_sub_keys", "peer_u", "peer_v", "final_norm_g"]
_OUTS = [("y_p", (1, T, D)), ("y_s", (B, 1, D)),
         ("p_c", (1, 1, H_A, P, P)), ("p_n", (1, 1, H_A, P)), ("p_m", (1, 1, H_A)), ("p_conva", (1, 1, 3, 2 * D)),
         ("p_ssm", (1, 1, H_B, P_B, P)), ("p_convb", (1, 1, 3, 1536)),
         ("s_c", (1, B, H_A, P, P)), ("s_n", (1, B, H_A, P)), ("s_m", (1, B, H_A)), ("s_conva", (1, B, 3, 2 * D)),
         ("s_ssm", (1, B, H_B, P_B, P)), ("s_convb", (1, B, 3, 1536))]


def kernel(**inputs):
    import numpy as _np
    import concourse.bacc as _bacc
    from concourse import mybir as _mybir
    from concourse.bass_utils import run_bass_kernel_spmd as _run

    nc = _bacc.Bacc("TRN2", target_bir_lowering=False, num_devices=1)
    arrays, ins, outs = {}, {}, {}
    for name in _INS:
        a = _np.ascontiguousarray(inputs[name])
        arrays[f"in_{name}_dram"] = a
        ins[name] = nc.dram_tensor(f"in_{name}_dram", a.shape, _mybir.dt.from_np(a.dtype), kind="ExternalInput").ap()
    for i, (name, shape) in enumerate(_OUTS):
        outs[name] = nc.dram_tensor(f"out_{i}_dram", shape, F32, kind="ExternalOutput").ap()
    gates = nc.dram_tensor("gates_dram", (NG, P, NTB, JG * TB), F32, kind="Internal").ap()
    program(nc, ins, outs, gates)
    r = _run(nc, [arrays], core_ids=[0])
    return tuple(r.results[0][f"out_{i}_dram"] for i in range(len(_OUTS)))
```

```python
from contextlib import ExitStack

import concourse.bass as bass
from concourse import mybir

F32 = mybir.dt.float32
F32R = mybir.dt.float32r
U32 = mybir.dt.uint32
ALU = mybir.AluOpType
ACT = mybir.ActivationFunctionType
AX_X = mybir.AxisListType.X

P = 128
D = 1024
KD = D // P
T = 512
B = 8
N = T + B
HN = N // 2
L = 128
NC = T // L
H_A = 8
H_B = 16
P_B = 64
G_B = 2
CONV = 4
NQ, NK, NV, NO, NZ, NX = 0, 8, 16, 24, 32, 40
SLOTS = 52
IG0, Z0, DT0 = 4096, 4112, 6672
PH = 8
NKEY = 128
TOPK = 16
EPS = 1e-6
FAR = 1e4
KSCALE = float(P) ** -0.5

V_BADA, V_N1, V_N2, V_CAW = 0, 48, 56, 64
V_CAB, V_CBW, V_CBB, V_GA, V_GB, V_GF = 128, 144, 192, 204, 212, 220
NVEC = 228


class Chain:

    def __init__(self, engine, sem):
        self.engine, self.sem, self.n = engine, sem, 0

    def __call__(self, instruction):
        self.n += 1
        instruction.then_inc(self.sem, 1)
        self.engine.wait_ge(self.sem, self.n)

    def take(self, vector):
        pass


class Phase(ExitStack):

    def __init__(self, nc):
        super().__init__()
        self.nc, self.semaphores = nc, []
        self.callback(self.clear)

    def sem(self, name):
        self.semaphores.append(self.nc.alloc_semaphore(name=name))
        return self.semaphores[-1]

    def clear(self):
        self.nc.all_engine_barrier()
        self.nc.clear_and_free_semaphores(self.semaphores)
        self.nc.all_engine_barrier()


def halves(t):
    return t.rearrange("p (a n) -> p a n", a=2)


def setup_phase(nc, A, S):
    with Phase(nc) as ctx:
        sem = ctx.sem
        rows = ctx.enter_context(nc.sbuf_tensor("rows", [P, 11, P], F32))
        xrow = ctx.enter_context(nc.sbuf_tensor("xrow", [P, NC, D], F32))
        ps = [ctx.enter_context(nc.psum_tensor(f"ps_set{i}", [P, 512], F32)) for i in range(8)]
        rows_in, x_in, small_in = sem("rows_in"), sem("x_in"), sem("small_in")
        zeroed, consts, turned, moved, moved_c = sem("zeroed"), sem("consts"), sem("turned"), sem("moved"), sem("moved_c")
        pool_own = sem("pool_own_set")
        loads = [
            (0, 0, A["b_ada"][0].rearrange("(r p) -> r p", p=P)),
            (0, 48, A["norm1_g"][0].rearrange("(r p) -> r p", p=P)),
            (0, 56, A["norm2_g"][0].rearrange("(r p) -> r p", p=P)),
            (0, 64, A["conv_a_w"][0].rearrange("j (r p) -> (j r) p", p=P)),
            (1, 0, A["conv_a_b"][0].rearrange("(r p) -> r p", p=P)),
            (1, 16, A["conv_b_w"][0].rearrange("j (r p) -> (j r) p", p=P)),
            (1, 64, A["conv_b_b"][0].rearrange("(r p) -> r p", p=P)),
            (1, 76, A["mlstm_norm_g"][0].rearrange("(r p) -> r p", p=P)),
            (1, 84, A["ssm_norm_g"][0].rearrange("(r p) -> r p", p=P)),
            (1, 92, A["final_norm_g"].rearrange("(r p) -> r p", p=P)),
            (2, 0, A["c_prompt"].rearrange("b (r p) -> (b r) p", p=P)),
            (2, 8, A["c_sample"].rearrange("b (r p) -> (b r) p", p=P)),
            (3, 0, A["x_sample"].rearrange("b t (r p) -> (b t r) p", p=P)),
            (3, 64, A["state_mlstm_n"][0].rearrange("b h d -> (b h) d")),
        ]
        ca = A["state_mlstm_conv"][0].rearrange("b j (r p) -> (b j r) p", p=P)
        cb = A["state_ssm_conv"][0].rearrange("b j (r p) -> (b j r) p", p=P)
        loads += [(4 + i, 0, ca[i * P:(i + 1) * P]) for i in range(3)]
        loads += [(7 + i, 0, cb[i * P:min((i + 1) * P, 288)]) for i in range(3)]
        height = [P, 100, 72, P, P, P, P, P, P, 32]
        block = ctx.enter_context(nc.Block())

        @block.sync
        def _(sp):
            for tile, at, src in loads:
                sp.dma_start(rows[at:at + src.shape[0], tile, :], src).then_inc(rows_in, 16)
            for t in range(NC):
                sp.dma_start(xrow[:, t, :], A["x_prompt"][0, t * L:(t + 1) * L, :]).then_inc(x_in, 16)
            sp.wait_ge(zeroed, 1)
            wi = A["w_in"][0].rearrange("(k p) n -> p k n", p=P)
            for at, col, n in ((0, IG0, 8), (32, IG0 + 8, 8), (64, DT0, 16)):
                sp.dma_start(S.wg[:, :, at:at + n], wi[:, :, col:col + n]).then_inc(small_in, 16)
            for row, src in enumerate((A["mlstm_gate_b"][0, 0], A["mlstm_gate_b"][0, 1])):
                sp.dma_start(S.col[0:H_A, row:row + 1], src.rearrange("(a b) -> a b", b=1)).then_inc(small_in, 16)
            for row, name in ((2, "dt_bias"), (3, "a_log"), (4, "d_skip")):
                sp.dma_start(S.col[0:H_B, row:row + 1], A[name][0].rearrange("(a b) -> a b", b=1)).then_inc(small_in, 16)
            sp.dma_start(S.m0T[:, :], A["state_mlstm_m"][0].rearrange("b h -> h b"), allow_slow_non_contiguous=True).then_inc(small_in, 16)
            sp.wait_ge(small_in, 16 * 9)

        @block.gpsimd
        def _(pool):
            own = Chain(pool, pool_own)
            own(nc.gpsimd.memset(S.ident[:, :], 0.0))
            nc.gpsimd.affine_select(out=S.ident[:, :], in_=S.ident[:, :], compare_op=ALU.not_equal, fill=1.0,
                                    base=0, pattern=[[-1, P]], channel_multiplier=1).then_inc(consts, 1)
            nc.gpsimd.iota(S.iota[:, :], [[1, P]], base=0, channel_multiplier=0,
                           allow_small_or_imprecise_dtypes=True)
            own(nc.gpsimd.memset(S.far[:, :], 0.0))
            own(nc.gpsimd.affine_select(out=S.far[:, :], in_=S.far[:, :], compare_op=ALU.is_ge, fill=FAR,
                                        base=0, pattern=[[1, P]], channel_multiplier=-1))
            own(nc.gpsimd.memset(S.pick[:, :, :], 0.0))
            own(nc.gpsimd.affine_select(out=S.pick[:, :, :], in_=S.pick[:, :, :], compare_op=ALU.not_equal, fill=1.0,
                                        base=0, pattern=[[-1, H_B], [0, P]], channel_multiplier=1))

        @block.vector
        def _(dve):
            nc.vector.memset(S.wg[:, :, :], 0.0).then_inc(zeroed, 1)
            nc.vector.memset(S.ones[:, :], 1.0)
            dve.wait_ge(turned, 3)
            nc.vector.tensor_copy(S.vec[:, 0:P], ps[0][:, 0:P])
            nc.vector.tensor_copy(S.vec[:, P:NVEC], ps[0][:, P:P + 100])
            nc.vector.tensor_copy(S.xT[:, :, T:N].rearrange("p k b -> p b k"),
                                  ps[0][:, 384:448].rearrange("p (b k) -> p b k", k=KD))
            nc.vector.tensor_copy(S.n0[:, :], ps[0][:, 448:512]).then_inc(moved, 1)
            nc.vector.tensor_copy(S.cbufa[:, 0:384], ps[1][:, 0:384])
            nc.vector.tensor_copy(S.cbufb[:, 0:128], ps[1][:, 384:512])
            nc.vector.tensor_copy(S.cbufb[:, 128:288], ps[2][:, 0:160]).then_inc(moved, 1)
            for k in range(KD):
                dve.wait_ge(turned, 4 + k)
                nc.vector.tensor_copy(S.xT[:, k, 0:T], ps[3 + k % 5][:, :]).then_inc(moved, 1)

        @block.scalar
        def _(act):
            act.wait_ge(moved, 1)
            nc.scalar.activation(S.silc[:, :, 0:1], ps[0][:, 256:264].rearrange("p (k a) -> p k a", a=1), ACT.Silu)
            nc.scalar.activation(S.silc[:, :, 1:9].rearrange("p k b -> p b k"),
                                 ps[0][:, 264:328].rearrange("p (b k) -> p b k", k=KD), ACT.Silu).then_inc(moved_c, 1)

        @block.tensor
        def _(pe):
            pe.wait_ge(consts, 1)
            pe.wait_ge(rows_in, 16 * len(loads))
            for t in range(10):
                h = height[t]
                mm = nc.tensor.transpose(ps[t // 4][:, t % 4 * P:t % 4 * P + h], rows[0:h, t, :], S.ident[0:h, 0:h])
                if t in (3, 7, 9):
                    mm.then_inc(turned, 1)
            pe.wait_ge(x_in, 16 * NC)
            for k in range(KD):
                if k >= 5:
                    pe.wait_ge(moved, 2 + k - 4)
                for t in range(NC):
                    mm = nc.tensor.transpose(ps[3 + k % 5][:, t * L:(t + 1) * L], xrow[:, t, k * P:(k + 1) * P], S.ident[:, :])
                mm.then_inc(turned, 1)


def project(nc, name, runs, w, K, X, width, evict, after=None):
    cols = 4096 // K
    per = cols // P
    wv = w.rearrange("(k p) n -> p k n", p=P)
    with Phase(nc) as ctx:
        wb = [ctx.enter_context(nc.sbuf_tensor(f"wb{i}_{name}", [P, K, cols], F32)) for i in range(2)]
        ps = [ctx.enter_context(nc.psum_tensor(f"ps{i}_{name}", [P, 2, 512], F32)) for i in range(2)]
        w_in = [ctx.sem(f"w_in{i}_{name}") for i in range(2)]
        product = ctx.sem(f"product_{name}")
        evicted = ctx.sem(f"evicted_{name}")
        block = ctx.enter_context(nc.Block())
        nh, hw = (2, HN) if width == N else (1, width)

        @block.sync
        def _(sp):
            pairs = 0
            for col, n, _ in runs:
                with sp.Fori(0, n) as i:
                    for j in range(2):
                        sp.wait_ge(product, 2 * per * i + per * (2 * pairs + j + 1))
                        sp.dma_start(wb[j][:, :, :], wv[:, :, bass.ds(i * (2 * cols) + (col + j * cols), cols)]).then_inc(w_in[j], 16)
                pairs += n

        @block.tensor
        def _(pe):
            pairs = 0
            pe.sem_inc(product, 2 * per)
            for _, n, _ in runs:
                with pe.Fori(0, n) as i:
                    for j in range(2):
                        pe.wait_ge(w_in[j], 16 * i + 16 * (pairs + 1))
                        for m in range(per):
                            c = j * per + m
                            pe.wait_ge(evicted, 2 * per * i + (2 * per * pairs + c + 1))
                            for h in range(nh):
                                for k in range(K):
                                    mm = nc.tensor.matmul(ps[c % 2][:, h, 0:hw], wb[j][:, k, m * P:(m + 1) * P],
                                                          X(k)[:, h * hw:(h + 1) * hw], start=(k == 0), stop=(k == K - 1))
                            mm.then_inc(product, 1)
                pairs += n

        def evictions(eng):
            eng.sem_inc(evicted, 2)
            pairs = 0
            for _, n, chunk in runs:
                with eng.Fori(0, n) as i:
                    for c in range(2 * per):
                        eng.wait_ge(product, 2 * per * i + (2 * per * (pairs + 1) + c + 1))
                        evict(2 * per * i + (chunk + c), ps[c % 2]).then_inc(evicted, 1)
                pairs += n

        block.scalar(evictions)
        if after:
            after(block)


def bcast(ap, dim, n):
    return ap.unsqueeze(dim).to_broadcast(ap.shape[:dim] + (n,) + ap.shape[dim:])


def norm_phase(nc, name, S, X, n_chunks, finish):
    with Phase(nc) as ctx:
        sq = ctx.enter_context(nc.sbuf_tensor(f"sq_{name}", [P, 2, N], F32))
        ps = ctx.enter_context(nc.psum_tensor(f"ps_{name}", [P, 2, 512], F32))
        squared, summed, scaled, rooted = (ctx.sem(f"{n}_{name}") for n in ("squared", "summed", "scaled", "rooted"))
        act_own = ctx.sem(f"act_own_{name}")
        dve_own = ctx.sem(f"dve_own_{name}")
        block = ctx.enter_context(nc.Block())

        @block.scalar
        def _(act):
            for k in range(n_chunks):
                if k >= 2:
                    act.wait_ge(summed, k - 1)
                nc.scalar.activation(sq[:, k % 2, :], X(k), ACT.Square).then_inc(squared, 1)
            act.wait_ge(scaled, 1)
            own = Chain(act, act_own)
            own(nc.scalar.activation(S.rb[:, :], S.rb[:, :], ACT.Ln))
            nc.scalar.activation(S.rb[:, :], S.rb[:, :], ACT.Exp, scale=-0.5).then_inc(rooted, 1)

        @block.tensor
        def _(pe):
            for k in range(n_chunks):
                pe.wait_ge(squared, k + 1)
                for h in range(2):
                    mm = nc.tensor.matmul(ps[:, h, 0:HN], S.ones[:, :], sq[:, k % 2, h * HN:(h + 1) * HN],
                                          start=(k == 0), stop=(k == n_chunks - 1))
                mm.then_inc(summed, 1)

        @block.vector
        def _(dve):
            dve.wait_ge(summed, n_chunks)
            nc.vector.tensor_scalar(halves(S.rb[:, :]), ps[:, :, 0:HN], 1.0 / (n_chunks * P), EPS, ALU.mult, ALU.add).then_inc(scaled, 1)
            dve.wait_ge(rooted, 1)
            finish(dve, Chain(dve, dve_own))


def modulate(nc, S, dst, gain, shift, scale):
    def finish(dve, own):
        own(nc.vector.tensor_scalar(S.gs[:, :, :], S.mod[:, scale:scale + KD, :], 1.0, None, ALU.add))
        own(nc.vector.tensor_tensor(S.gs[:, :, :], S.gs[:, :, :], bcast(S.vec[:, gain:gain + KD], 2, 9), ALU.mult))
        for k in range(KD):
            nc.vector.scalar_tensor_tensor(out=dst[:, k, 0:T], in0=S.xT[:, k, 0:T], scalar=S.gs[:, k, 0:1],
                                           in1=S.rb[:, 0:T], op0=ALU.mult, op1=ALU.mult)
        own(nc.vector.tensor_tensor(dst[:, :, T:N], S.xT[:, :, T:N], bcast(S.rb[:, T:N], 1, KD), ALU.mult))
        for k in range(KD):
            nc.vector.tensor_scalar(dst[:, k, 0:T], dst[:, k, 0:T], S.mod[:, shift + k, 0:1], None, ALU.add)
        own(nc.vector.tensor_tensor(dst[:, :, T:N], dst[:, :, T:N], S.gs[:, :, 1:9], ALU.mult))
        own(nc.vector.tensor_tensor(dst[:, :, T:N], dst[:, :, T:N], S.mod[:, shift:shift + KD, 1:9], ALU.add))
    return finish


def gates_phase(nc, A, S, R, O):
    with Phase(nc) as ctx:
        sem = ctx.sem
        sb = lambda n, s: ctx.enter_context(nc.sbuf_tensor(n, s, F32))
        ps = ctx.enter_context(nc.psum_tensor("ps_gate", [P, 2, 512], F32))
        pt = ctx.enter_context(nc.psum_tensor("pt_gate", [P, 2, 512], F32))
        pb = ctx.enter_context(nc.psum_tensor("pb_gate", [P, 4, 512], F32))
        fg, u, ef, lf, ig = (sb(f"{n}_gate", [H_A, N]) for n in ("fg", "u", "ef", "lf", "ig"))
        dx, du, de = (sb(f"{n}_gate", [H_B, N]) for n in ("dx", "du", "de"))
        bt = sb("bt_gate", [H_A, N])
        reset = sb("reset_gate", [H_B, T])
        mc = sb("mc_gate", [H_A, NC + 1])
        ml = sb("ml_gate", [H_A, NC + 1])
        va = sb("va_gate", [H_A, 28])
        vb = sb("vb_gate", [H_B, 21])
        xa = sb("xa_gate", [H_A, H_A, 28])
        xb = sb("xb_gate", [H_B, H_B, 21])
        row = {n: sb(f"row_{n}", [H_A, N]) for n in ("inter", "w", "em")}
        rw = sb("row_ws", [H_B, T])
        re = sb("row_ec", [H_B, T])
        gated, acted, dve_own, act_own = sem("gated"), sem("acted"), sem("dve_own_gate"), sem("act_own_gate")
        rowed, columned, expanded, spread, out_done = sem("rowed"), sem("columned"), sem("expanded"), sem("spread"), sem("gate_out")
        block = ctx.enter_context(nc.Block())

        @block.tensor
        def _(pe):
            for h in range(2):
                for k in range(KD):
                    mm = nc.tensor.matmul(ps[0:96, h, 0:HN], S.wg[:, k, :], S.hT[:, k, h * HN:(h + 1) * HN],
                                          start=(k == 0), stop=(k == KD - 1))
            mm.then_inc(gated, 1)
            pe.wait_ge(acted, 2)
            for q, r in enumerate((R.a, row["inter"], row["w"], row["em"], R.cum, R.dt, rw, re)):
                n = H_A if q < 4 else H_B
                for c in range(NC):
                    at = (c * 8 + q) * 16
                    mm = nc.tensor.transpose(pt[:, 0, at:at + n], r[0:n, c * L:(c + 1) * L], S.ident[0:n, 0:n])
            mm.then_inc(columned, 1)
            pe.wait_ge(expanded, 1)
            nc.tensor.matmul(pb[:, 0, 0:224], S.ones[0:H_A, :], xa[:, :, :].rearrange("p a b -> p (a b)"), start=True, stop=True)
            nc.tensor.matmul(pb[:, 1, 0:336], S.ones[0:H_B, :], xb[:, :, :].rearrange("p a b -> p (a b)"), start=True, stop=True).then_inc(columned, 1)

        @block.scalar
        def _(act):
            own = Chain(act, act_own)
            act.wait_ge(gated, 1)
            nc.scalar.activation(halves(ig[:, :]), ps[0:H_A, :, 0:HN], ACT.Identity, bias=S.col[0:H_A, 0:1])
            nc.scalar.activation(halves(fg[:, :]), ps[32:32 + H_A, :, 0:HN], ACT.Identity, bias=S.col[0:H_A, 1:2])
            own(nc.scalar.activation(halves(dx[:, :]), ps[64:64 + H_B, :, 0:HN], ACT.Identity, bias=S.col[0:H_B, 2:3]))
            nc.scalar.activation(ef[:, :], fg[:, :], ACT.Abs)
            own(nc.scalar.activation(de[:, :], dx[:, :], ACT.Abs))
            nc.scalar.activation(ef[:, :], ef[:, :], ACT.Exp, scale=-1.0)
            nc.scalar.activation(S.ea[:, :], S.col[0:H_B, 3:4], ACT.Exp)
            own(nc.scalar.activation(de[:, :], de[:, :], ACT.Exp, scale=-1.0))
            nc.scalar.activation(ef[:, :], ef[:, :], ACT.Ln, bias=1.0)
            nc.scalar.activation(de[:, :], de[:, :], ACT.Ln, bias=1.0).then_inc(acted, 1)
            act.wait_ge(rowed, 2)
            for t in (row["inter"][:, :], row["w"][:, :], row["em"][:, :], rw[:, :], re[:, :], va[:, :], vb[:, 0:12]):
                last = nc.scalar.activation(t, t, ACT.Exp, scale=-1.0)
            last.then_inc(acted, 1)

        @block.vector
        def _(dve):
            own = Chain(dve, dve_own)
            v = nc.vector
            v.memset(reset[:, :], 1.0)
            own(v.memset(mc[:, 0:1], 0.0))
            own(v.memset(reset[:, :].rearrange("p (c l) -> p c l", c=NC)[:, :, 0:1], 0.0))
            dve.wait_ge(acted, 1)
            v.scalar_tensor_tensor(out=lf[:, :], in0=fg[:, :], scalar=0.0, in1=ef[:, :], op0=ALU.min, op1=ALU.subtract)
            own(v.scalar_tensor_tensor(out=R.dt[:, :], in0=dx[:, :], scalar=0.0, in1=de[:, :], op0=ALU.max, op1=ALU.add))
            own(v.tensor_scalar(du[:, :], R.dt[:, :], S.ea[:, 0:1], None, ALU.mult))
            v.tensor_tensor_scan(bt[:, 0:T], reset[0:H_A, :], lf[:, 0:T], 0.0, ALU.mult, ALU.add)
            v.tensor_copy(bt[:, T:N], lf[:, T:N])
            v.tensor_tensor_scan(R.cum[:, 0:T], reset[:, :], du[:, 0:T], 0.0, ALU.mult, ALU.add)
            own(v.tensor_copy(R.cum[:, T:N], du[:, T:N]))
            own(v.tensor_tensor(R.a[:, :], ig[:, :], bt[:, :], ALU.subtract))
            for c in range(NC):
                at = slice(c * L, (c + 1) * L)
                own(v.tensor_tensor_scan(R.M[:, at], R.a[:, at], R.a[:, at], mc[:, c:c + 1], ALU.max, ALU.max))
                own(v.tensor_tensor(mc[:, c + 1:c + 2], R.M[:, (c + 1) * L - 1:(c + 1) * L], bt[:, (c + 1) * L - 1:(c + 1) * L], ALU.add))
            own(v.tensor_tensor(R.M[:, T:N], R.a[:, T:N], S.m0T[:, :], ALU.max))
            for c in range(NC):
                at = slice(c * L, (c + 1) * L)
                last = slice((c + 1) * L - 1, (c + 1) * L)
                v.tensor_scalar(row["inter"][:, at], R.M[:, at], mc[:, c:c + 1], None, ALU.subtract)
                v.tensor_scalar(row["w"][:, at], R.a[:, at], R.M[:, last], -1.0, ALU.subtract, ALU.mult)
                v.tensor_tensor(va[:, c:c + 1], R.M[:, last], mc[:, c:c + 1], ALU.subtract)
                v.tensor_scalar(rw[:, at], R.cum[:, at], R.cum[:, last], -1.0, ALU.subtract, ALU.mult)
                v.tensor_copy(vb[:, c:c + 1], R.cum[:, last])
            v.tensor_tensor(row["inter"][:, T:N], R.M[:, T:N], S.m0T[:, :], ALU.subtract)
            v.tensor_tensor(row["w"][:, T:N], R.M[:, T:N], R.a[:, T:N], ALU.subtract)
            v.tensor_copy(re[:, :], R.cum[:, 0:T])
            own(v.tensor_tensor(row["em"][:, :], R.M[:, :], bt[:, :], ALU.add))
            v.tensor_copy(va[:, 4:12], row["inter"][:, T:N])
            v.tensor_copy(va[:, 12:20], row["w"][:, T:N])
            v.tensor_copy(va[:, 20:28], row["em"][:, T:N])
            v.tensor_copy(vb[:, 4:12], R.cum[:, T:N])
            v.tensor_copy(vb[:, 12:20], R.dt[:, T:N])
            v.tensor_copy(S.mS[:, :], row["em"][:, T:N])
            own(v.tensor_copy(vb[:, 20:21], S.col[0:H_B, 4:5]))
            v.tensor_copy(S.mP[:, :], mc[:, NC:NC + 1]).then_inc(rowed, 2)
            dve.wait_ge(acted, 2)
            v.tensor_tensor(xa[:, :, :], bcast(va[:, :], 1, H_A), bcast(S.ident[0:H_A, 0:H_A], 2, 28), ALU.mult)
            v.tensor_tensor(xb[:, :, :], bcast(vb[:, :], 1, H_B), bcast(S.ident[0:H_B, 0:H_B], 2, 21), ALU.mult).then_inc(expanded, 1)
            dve.wait_ge(columned, 1)
            v.tensor_copy(S.cols[:, :, 0:4, 0:8], pt[:, 0, :].rearrange("p (c q n) -> p c q n", c=NC, q=8)[:, :, 0:4, 0:8])
            v.tensor_copy(S.cols[:, :, 4:8, :], pt[:, 0, :].rearrange("p (c q n) -> p c q n", c=NC, q=8)[:, :, 4:8, :])
            dve.wait_ge(columned, 2)
            v.tensor_copy(S.ba[:, :, :].rearrange("p a b -> p (a b)"), pb[:, 0, 0:224])
            v.tensor_copy(S.bb[:, :, :].rearrange("p a b -> p (a b)"), pb[:, 1, 0:336]).then_inc(spread, 1)

        @block.sync
        def _(sp):
            sp.wait_ge(rowed, 2)
            sp.dma_start(O["p_m"][0, 0].rearrange("(h a) -> h a", a=1), S.mP[:, :]).then_inc(out_done, 16)
            sp.dma_start(O["s_m"][0].rearrange("b h -> h b"), S.mS[:, :], allow_slow_non_contiguous=True).then_inc(out_done, 16)
            sp.wait_ge(out_done, 32)


def conv_phase(nc, A, S, O):
    with Phase(nc) as ctx:
        sem = ctx.sem
        sb = lambda n, s: ctx.enter_context(nc.sbuf_tensor(n, s, F32))
        y = sb("y_conv", [P, 4, T])
        ys = sb("ys_conv", [P, 28, B])
        ts = sb("ts_conv", [P, 28, B])
        raw = sb("raw_conv", [P, 28, 3 + B])
        tail = sb("tail_conv", [32, 28 * P])
        ps = [ctx.enter_context(nc.psum_tensor(f"ps_conv{i}", [P, 512], F32)) for i in range(7)]
        first, convd, used, dve_own, act_own = sem("first_tap"), sem("convd"), sem("silu_done"), sem("dve_own_conv"), sem("act_own_conv")
        kept, tailed, rowed, out_done = sem("raw_kept"), sem("tail_turned"), sem("tail_moved"), sem("conv_out")
        samples = sem("samples_convd")
        block = ctx.enter_context(nc.Block())
        slot = lambda i: i if i < 16 else NX + i - 16

        def tap(i, j):
            return S.vec[:, V_CAW + 16 * j + i:V_CAW + 16 * j + i + 1] if i < 16 else S.vec[:, V_CBW + 12 * j + i - 16:V_CBW + 12 * j + i - 15]

        def bias(i):
            return S.vec[:, V_CAB + i:V_CAB + i + 1] if i < 16 else S.vec[:, V_CBB + i - 16:V_CBB + i - 15]

        @block.scalar
        def _(act):
            for i in range(28 + 2):
                if i < 28:
                    if i >= 4:
                        act.wait_ge(used, i - 3)
                    nc.scalar.activation(y[:, i % 4, :], S.proj[:, slot(i), 0:T], ACT.Identity, bias=bias(i), scale=tap(i, 3)).then_inc(first, 1)
                if i >= 2:
                    act.wait_ge(convd, i - 1)
                    nc.scalar.activation(S.proj[:, slot(i - 2), 0:T], y[:, (i - 2) % 4, :], ACT.Silu).then_inc(used, 1)
            act.wait_ge(samples, 1)
            nc.scalar.activation(S.proj[:, 0:16, T:N], ys[:, 0:16, :], ACT.Silu)
            nc.scalar.activation(S.proj[:, NX:NX + 12, T:N], ys[:, 16:28, :], ACT.Silu)
            for k in range(KD):
                nc.scalar.activation(S.proj[:, NZ + k, :], S.proj[:, NZ + k, :], ACT.Silu)
            for k in range(KD):
                last = nc.scalar.activation(S.proj[:, NO + k, :], S.proj[:, NO + k, :], ACT.Sigmoid)
            last.then_inc(used, 1)

        @block.vector
        def _(dve):
            own = Chain(dve, dve_own)
            v = nc.vector
            v.tensor_copy(raw[:, 0:16, :], S.proj[:, 0:16, T - 3:N])
            v.tensor_copy(raw[:, 16:28, :], S.proj[:, NX:NX + 12, T - 3:N]).then_inc(kept, 1)
            dve.wait_ge(kept, 1)
            for lo, n, w, b, buf in ((0, 16, V_CAW, V_CAB, S.cbufa), (16, 12, V_CBW, V_CBB, S.cbufb)):
                o = ys[:, lo:lo + n, :]
                t = ts[:, lo:lo + n, :]
                bv = buf[:, :].rearrange("p (b j r) -> p j r b", b=B, j=3)
                own(v.tensor_tensor(o, raw[:, lo:lo + n, 3:11], bcast(S.vec[:, w + 3 * n:w + 4 * n], 2, B), ALU.mult))
                own(v.tensor_tensor(o, o, bcast(S.vec[:, b:b + n], 2, B), ALU.add))
                for j in range(3):
                    own(v.tensor_tensor(t, bv[:, j], bcast(S.vec[:, w + j * n:w + (j + 1) * n], 2, B), ALU.mult))
                    own(v.tensor_tensor(o, o, t, ALU.add))
            dve.sem_inc(samples, 1)
            for i in range(28):
                dve.wait_ge(first, i + 1)
                for j in (2, 1, 0):
                    d = 3 - j
                    ins = v.scalar_tensor_tensor(out=y[:, i % 4, d:T], in0=S.proj[:, slot(i), 0:T - d], scalar=tap(i, j),
                                                 in1=y[:, i % 4, d:T], op0=ALU.mult, op1=ALU.add)
                    if j:
                        own(ins)
                    else:
                        ins.then_inc(convd, 1)
            dve.wait_ge(used, 29)
            v.tensor_scalar(S.proj[:, NK:NK + 8, :], S.proj[:, NK:NK + 8, :], KSCALE, None, ALU.mult).then_inc(rowed, 1)

            for i in range(7):
                dve.wait_ge(tailed, i + 1)
                v.tensor_copy(tail[0:11, i * 512:(i + 1) * 512], ps[i][0:11, :]).then_inc(rowed, 1)

        @block.tensor
        def _(pe):
            pe.wait_ge(kept, 1)
            for i in range(28):
                mm = nc.tensor.transpose(ps[i // 4][0:11, i % 4 * P:i % 4 * P + P], raw[:, i, :], S.ident[:, :])
                if i % 4 == 3:
                    mm.then_inc(tailed, 1)

        @block.sync
        def _(sp):
            n = 0
            for key, src, cols, at in (("conva", A["state_mlstm_conv"], 2048, 0), ("convb", A["state_ssm_conv"], 1536, 2048)):
                sp.dma_start(O["s_" + key][0, :, 0:2, :], src[0, :, 1:3, :]).then_inc(out_done, 16)
            sp.wait_ge(rowed, 8)
            for key, cols, at in (("conva", 2048, 0), ("convb", 1536, 2048)):
                sp.dma_start(O["p_" + key][0, 0], tail[0:3, at:at + cols]).then_inc(out_done, 16)
                sp.dma_start(O["s_" + key][0, :, 2, :], tail[3:11, at:at + cols]).then_inc(out_done, 16)
            sp.wait_ge(out_done, 16 * 6)


def mlstm_phase(nc, S, R, O):
    with Phase(nc) as ctx:
        sem = ctx.sem
        sb = lambda n, s: ctx.enter_context(nc.sbuf_tensor(n, s, F32))
        V1 = P + 1
        num = sb("num_ml", [P, NC, H_A, V1])
        va = [sb(f"vaug{i}", [P, NC, V1]) for i in range(2)]
        kw = [sb(f"kw{i}", [P, NC, P]) for i in range(2)]
        X = [sb(f"x_ml{i}", [P, NC, L]) for i in range(2)]
        E = [sb(f"e_ml{i}", [P, NC, L]) for i in range(2)]
        C = sb("c_ml", [P, H_A, V1])
        ti = [sb(f"ti_ml{i}", [P, V1]) for i in range(2)]
        sq = sb("sq_ml", [P, H_A, P])
        den, r, mean, var = (sb(f"{n}_ml", [P, NC, H_A]) for n in ("den", "r", "mean", "var"))
        bank = lambda n: ctx.enter_context(nc.psum_tensor(n, [P, 512], F32))
        qk, mb, st = ([bank(f"{n}{i}_ml") for i in range(2)] for n in ("qk", "mb", "st"))
        trk, trv = bank("trk_ml"), bank("trv_ml")
        scored, turned, kv_ready, exps, xs, weighed, stepped, scaled_i, c_ready, num_ready = (
            sem(n + "_ml") for n in ("scored", "turned", "kv_ready", "exps", "xs", "weighed", "stepped", "scaled_i", "c_ready", "num_ready"))
        ones_set, squared, centred, var_ready, rooted, normed, hturned, hmoved, dve_own, act_own, n_out, o_done = (
            sem(n + "_ml") for n in ("ones_set", "squared", "centred", "var_ready", "rooted", "normed", "hturned", "hmoved", "dve_own", "act_own", "n_out", "out_done"))
        block = ctx.enter_context(nc.Block())
        q, k, v = (lambda h, c, s=s: S.proj[:, s + h, c * L:(c + 1) * L] for s in (NQ, NK, NV))
        col = lambda c, quantity, h: S.cols[:, c, quantity, h:h + 1]

        @block.tensor
        def _(pe):
            def scores(h):
                if h >= 2:
                    pe.wait_ge(weighed, h - 1)
                for c in range(NC):
                    nc.tensor.matmul(qk[h % 2][:, c * L:(c + 1) * L], k(h, c), q(h, c), start=True, stop=True)
                nc.tensor.matmul(mb[h % 2][:, :], S.pick[0:H_A, h, :], R.M[:, 0:T], start=True, stop=True).then_inc(scored, 1)
                if h >= 1:
                    pe.wait_ge(kv_ready, h)
                for c in range(NC):
                    nc.tensor.transpose(trk[:, c * L:(c + 1) * L], k(h, c), S.ident[:, :])
                    mm = nc.tensor.transpose(trv[:, c * L:(c + 1) * L], v(h, c), S.ident[:, :])
                mm.then_inc(turned, 1)

            def steps(h):
                pe.wait_ge(weighed, h + 1)
                pe.wait_ge(kv_ready, h + 1)
                for c in range(NC):
                    n = NC * h + c
                    if n >= 2:
                        pe.wait_ge(num_ready, n - 1)
                    nc.tensor.matmul(st[n % 2][:, 0:V1], X[h % 2][:, c, :], va[h % 2][:, c, :], start=True, stop=True)
                    if c:
                        pe.wait_ge(c_ready, n)
                        nc.tensor.matmul(st[n % 2][:, 130:130 + V1], q(h, c), C[:, h, :], start=True, stop=True)
                    nc.tensor.matmul(st[n % 2][:, 260:260 + V1], kw[h % 2][:, c, :], va[h % 2][:, c, :], start=True, stop=True).then_inc(stepped, 1)

            scores(0)
            for h in range(H_A):
                if h + 1 < H_A:
                    scores(h + 1)
                steps(h)
            pe.wait_ge(c_ready, NC * H_A)
            nc.tensor.transpose(mb[0][0:H_A, 0:P], C[:, :, P], S.ident[:, :]).then_inc(n_out, 1)
            pe.wait_ge(normed, 1)
            for h in range(H_A):
                if h >= 2:
                    pe.wait_ge(hmoved, h - 1)
                for c in range(NC):
                    mm = nc.tensor.transpose(qk[h % 2][:, c * L:(c + 1) * L], num[:, c, h, 0:P], S.ident[:, :])
                mm.then_inc(hturned, 1)

        @block.scalar
        def _(act):
            def prepare(h):
                act.wait_ge(turned, h + 1)
                if h >= 2:
                    act.wait_ge(stepped, NC * (h - 1))
                nc.scalar.activation(va[h % 2][:, :, 0:P], trv[:, :].rearrange("p (c l) -> p c l", c=NC), ACT.Copy)
                for c in range(NC):
                    last = nc.scalar.activation(kw[h % 2][:, c, :], trk[:, c * L:(c + 1) * L], ACT.Copy, scale=col(c, 2, h))
                last.then_inc(kv_ready, 1)
                act.wait_ge(xs, h + 1)
                nc.scalar.activation(E[h % 2][:, :, :], X[h % 2][:, :, :], ACT.Exp, scale=-1.0).then_inc(exps, 1)

            act.wait_ge(ones_set, 1)
            prepare(0)
            for h in range(H_A):
                if h + 1 < H_A:
                    prepare(h + 1)
                for c in range(1, NC):
                    n = NC * h + c
                    act.wait_ge(stepped, n + 1)
                    if n >= 2:
                        act.wait_ge(num_ready, n - 1)
                    nc.scalar.activation(ti[n % 2][:, :], st[n % 2][:, 130:130 + V1], ACT.Copy, scale=col(c, 1, h)).then_inc(scaled_i, 1)
            for c in range(NC):
                act.wait_ge(centred, c + 1)
                if c:
                    act.wait_ge(var_ready, c)
                nc.scalar.activation(sq[:, :, :], num[:, c, :, 0:P], ACT.Square).then_inc(squared, 1)
            act.wait_ge(var_ready, NC + 1)
            own = Chain(act, act_own)
            own(nc.scalar.activation(var[:, :, :], var[:, :, :], ACT.Ln))
            nc.scalar.activation(var[:, :, :], var[:, :, :], ACT.Exp, scale=-0.5).then_inc(rooted, 1)

        @block.vector
        def _(dve):
            own = Chain(dve, dve_own)
            V = nc.vector
            for i in range(2):
                last = V.memset(va[i][:, :, P:V1], 1.0)
            last.then_inc(ones_set, 1)

            def weigh(h):
                dve.wait_ge(scored, h + 1)
                if h >= 2:
                    dve.wait_ge(stepped, NC * (h - 1))
                for c in range(NC):
                    last = V.scalar_tensor_tensor(out=X[h % 2][:, c, :], in0=mb[h % 2][:, c * L:(c + 1) * L], scalar=col(c, 0, h),
                                                  in1=S.far[:, :], op0=ALU.subtract, op1=ALU.max)
                last.then_inc(xs, 1)
                dve.wait_ge(exps, h + 1)
                V.tensor_tensor(X[h % 2][:, :, :], E[h % 2][:, :, :], qk[h % 2][:, :].rearrange("p (c l) -> p c l", c=NC), ALU.mult).then_inc(weighed, 1)

            weigh(0)
            for h in range(H_A):
                if h + 1 < H_A:
                    weigh(h + 1)
                for c in range(NC):
                    n = NC * h + c
                    dve.wait_ge(stepped, n + 1)
                    if c:
                        dve.wait_ge(scaled_i, 3 * h + c)
                        V.scalar_tensor_tensor(out=C[:, h, :], in0=C[:, h, :], scalar=S.ba[:, h, c:c + 1],
                                               in1=st[n % 2][:, 260:260 + V1], op0=ALU.mult, op1=ALU.add).then_inc(c_ready, 1)
                        V.tensor_tensor(num[:, c, h, :], ti[n % 2][:, :], st[n % 2][:, 0:V1], ALU.add).then_inc(num_ready, 1)
                    else:
                        V.tensor_copy(C[:, h, :], st[n % 2][:, 260:260 + V1]).then_inc(c_ready, 1)
                        V.tensor_copy(num[:, c, h, :], st[n % 2][:, 0:V1]).then_inc(num_ready, 1)
            dve.wait_ge(n_out, 1)
            V.tensor_copy(S.nrow[:, :], mb[0][0:H_A, 0:P]).then_inc(n_out, 1)
            dve.wait_ge(num_ready, NC * H_A)
            own(V.scalar_tensor_tensor(out=den[:, :, :], in0=num[:, :, :, P], scalar=-1.0, in1=num[:, :, :, P], op0=ALU.mult, op1=ALU.max))
            own(V.tensor_tensor(den[:, :, :], den[:, :, :], S.cols[:, :, 3, 0:H_A], ALU.max))
            own(V.reciprocal(r[:, :, :], den[:, :, :]))
            for c in range(NC):
                h_c = num[:, c, :, 0:P]
                own(V.tensor_tensor(h_c, h_c, bcast(r[:, c, :], 2, P), ALU.mult))
                own(V.reduce_sum(mean[:, c, :], h_c, AX_X))
                own(V.tensor_scalar(mean[:, c, :], mean[:, c, :], 1.0 / P, None, ALU.mult))
                V.tensor_tensor(h_c, h_c, bcast(mean[:, c, :], 2, P), ALU.subtract).then_inc(centred, 1)
                dve.wait_ge(squared, c + 1)
                V.reduce_sum(var[:, c, :], sq[:, :, :], AX_X).then_inc(var_ready, 1)
            dve.wait_ge(var_ready, NC)
            V.tensor_scalar(var[:, :, :], var[:, :, :], 1.0 / P, EPS, ALU.mult, ALU.add).then_inc(var_ready, 1)
            dve.wait_ge(rooted, 1)
            for c in range(NC):
                last = V.tensor_tensor(num[:, c, :, 0:P], num[:, c, :, 0:P], bcast(var[:, c, :], 2, P), ALU.mult)
            last.then_inc(normed, 1)
            for h in range(H_A):
                dve.wait_ge(hturned, h + 1)
                V.scalar_tensor_tensor(out=S.proj[:, NQ + h, 0:T], in0=qk[h % 2][:, :], scalar=S.vec[:, V_GA + h:V_GA + h + 1],
                                       in1=S.proj[:, NO + h, 0:T], op0=ALU.mult, op1=ALU.mult).then_inc(hmoved, 1)

        @block.sync
        def _(sp):
            sp.wait_ge(c_ready, NC * H_A)
            sp.dma_start(O["p_c"][0, 0].rearrange("h d v -> d h v"), C[:, :, 0:P]).then_inc(o_done, 16)
            sp.wait_ge(n_out, 2)
            sp.dma_start(O["p_n"][0, 0], S.nrow[:, :]).then_inc(o_done, 16)
            sp.wait_ge(o_done, 32)


def ssd_phase(nc, S, R, O):
    with Phase(nc) as ctx:
        sem = ctx.sem
        sb = lambda n, s: ctx.enter_context(nc.sbuf_tensor(n, s, F32))
        HG = H_B // G_B
        BC = sb("bc_ssd", [P, NC, L])
        Bt = sb("bt_ssd", [P, NC, P])
        xdt, xw, Y = (sb(f"{n}_ssd", [P, NC, HG, P_B]) for n in ("xdt", "xw", "y"))
        ST = sb("st_ssd", [P, HG, P_B])
        tmp = sb("tmp_ssd", [P, HG, P_B])
        X = [sb(f"x_ssd{i}", [P, NC, L]) for i in range(2)]
        E = [sb(f"e_ssd{i}", [P, NC, L]) for i in range(2)]
        so = sb("so_ssd", [P, 4, P])
        bank = lambda n: ctx.enter_context(nc.psum_tensor(n, [P, 512], F32))
        a, cb, py = ([bank(f"{n}{i}_ssd") for i in range(2)] for n in ("a", "cb", "py"))
        pi, pu = bank("pi_ssd"), bank("pu_ssd")
        names = ("bc_in", "bc_out", "x_in", "x_out", "spread", "xs", "exps", "weighed", "y_in", "y_out", "inter_in", "state", "inter_out",
                 "t_in", "t_out", "so_in", "so_ready", "o_done", "dve_own")
        m = {n: sem(n + "_ssd") for n in names}
        block = ctx.enter_context(nc.Block())
        tok = lambda slot, c: S.proj[:, slot, c * L:(c + 1) * L]
        col = lambda c, quantity, h: S.cols[:, c, quantity, h:h + 1]

        @block.tensor
        def _(pe):
            for g in range(G_B):
                if g:
                    pe.wait_ge(m["t_out"], 4)
                    pe.wait_ge(m["so_ready"], 1)
                for c in range(NC):
                    nc.tensor.matmul(a[0][:, c * L:(c + 1) * L], tok(NX + 8 + g, c), tok(NX + 10 + g, c), start=True, stop=True)
                    mm = nc.tensor.transpose(a[1][:, c * L:(c + 1) * L], tok(NX + 8 + g, c), S.ident[:, :])
                mm.then_inc(m["bc_in"], 1)
                for c in range(NC):
                    if c >= 2:
                        pe.wait_ge(m["x_out"], NC * g + c - 1)
                    for f in range(4):
                        mm = nc.tensor.transpose(py[c % 2][:, f * P:(f + 1) * P], tok(NX + 4 * g + f, c), S.ident[:, :])
                    mm.then_inc(m["x_in"], 1)

                def spread(h):
                    n = HG * g + h
                    if n >= 2:
                        pe.wait_ge(m["xs"], n - 1)
                    nc.tensor.matmul(cb[n % 2][:, :], S.pick[0:H_B, n, :], R.cum[:, 0:T], start=True, stop=True).then_inc(m["spread"], 1)

                spread(0)
                for h in range(HG):
                    n = HG * g + h
                    if h + 1 < HG:
                        spread(h + 1)
                    pe.wait_ge(m["weighed"], n + 1)
                    pe.wait_ge(m["x_out"], NC * (g + 1))
                    if h >= 2:
                        pe.wait_ge(m["y_out"], n - 1)
                    for c in range(NC):
                        mm = nc.tensor.matmul(py[n % 2][:, c * P_B:(c + 1) * P_B], E[n % 2][:, c, :], xdt[:, c, h, :], start=True, stop=True)
                    mm.then_inc(m["y_in"], 1)
                for c in range(NC):
                    n = NC * g + c
                    if n:
                        pe.wait_ge(m["state"], n)
                        pe.wait_ge(m["inter_out"], n)
                    if c:
                        nc.tensor.matmul(pi[:, :], tok(NX + 10 + g, c), ST[:, :, :].rearrange("p h d -> p (h d)"), start=True, stop=True)
                    nc.tensor.matmul(pu[:, :], Bt[:, c, :], xw[:, c, :, :].rearrange("p h d -> p (h d)"), start=True, stop=True).then_inc(m["inter_in"], 1)
                pe.wait_ge(m["inter_out"], NC * (g + 1))
                pe.wait_ge(m["state"], NC * (g + 1))
                pe.wait_ge(m["y_out"], HG * (g + 1))
                for f in range(4):
                    if f >= 2:
                        pe.wait_ge(m["t_out"], 4 * g + f - 1)
                    for c in range(NC):
                        mm = nc.tensor.transpose(a[f % 2][:, c * L:(c + 1) * L], Y[:, c, 2 * f:2 * f + 2, :].rearrange("p h d -> p (h d)"), S.ident[:, :])
                    mm.then_inc(m["t_in"], 1)
                for f in range(4):
                    mm = nc.tensor.transpose(pi[:, f * P:(f + 1) * P], ST[:, 2 * f:2 * f + 2, :].rearrange("p h d -> p (h d)"), S.ident[:, :])
                mm.then_inc(m["so_in"], 1)

        @block.scalar
        def _(act):
            for g in range(G_B):
                act.wait_ge(m["bc_in"], g + 1)
                nc.scalar.activation(BC[:, :, :], a[0][:, :].rearrange("p (c l) -> p c l", c=NC), ACT.Copy)
                nc.scalar.activation(Bt[:, :, :], a[1][:, :].rearrange("p (c l) -> p c l", c=NC), ACT.Copy).then_inc(m["bc_out"], 1)
                for h in range(HG):
                    n = HG * g + h
                    act.wait_ge(m["xs"], n + 1)
                    nc.scalar.activation(X[n % 2][:, :, :], X[n % 2][:, :, :], ACT.Exp, scale=-1.0).then_inc(m["exps"], 1)

        @block.vector
        def _(dve):
            own = Chain(dve, m["dve_own"])
            V = nc.vector
            for g in range(G_B):
                hs = slice(HG * g, HG * (g + 1))
                for c in range(NC):
                    dve.wait_ge(m["x_in"], NC * g + c + 1)
                    px = py[c % 2][:, :].rearrange("p (h d) -> p h d", h=HG)
                    own(V.tensor_tensor(xdt[:, c], px, bcast(S.cols[:, c, 5, hs], 2, P_B), ALU.mult))
                    V.tensor_tensor(xw[:, c], xdt[:, c], bcast(S.cols[:, c, 6, hs], 2, P_B), ALU.mult)
                    V.tensor_tensor(Y[:, c], px, bcast(S.bb[:, hs, 20], 2, P_B), ALU.mult).then_inc(m["x_out"], 1)
                dve.wait_ge(m["x_out"], NC * (g + 1))

                def exponents(h):
                    n = HG * g + h
                    dve.wait_ge(m["spread"], n + 1)
                    for c in range(NC):
                        last = V.scalar_tensor_tensor(out=X[n % 2][:, c, :], in0=cb[n % 2][:, c * L:(c + 1) * L], scalar=col(c, 4, n),
                                                      in1=S.far[:, :], op0=ALU.subtract, op1=ALU.max)
                    last.then_inc(m["xs"], 1)

                def weigh(h):
                    n = HG * g + h
                    dve.wait_ge(m["exps"], n + 1)
                    dve.wait_ge(m["bc_out"], g + 1)
                    if n >= 2:
                        dve.wait_ge(m["y_in"], n - 1)
                    V.tensor_tensor(E[n % 2][:, :, :], X[n % 2][:, :, :], BC[:, :, :], ALU.mult).then_inc(m["weighed"], 1)

                exponents(0)
                weigh(0)
                for h in range(HG):
                    n = HG * g + h
                    if h + 1 < HG:
                        exponents(h + 1)
                        weigh(h + 1)
                    dve.wait_ge(m["y_in"], n + 1)
                    V.tensor_tensor(Y[:, :, h, :], Y[:, :, h, :], py[n % 2][:, 0:NC * P_B].rearrange("p (c d) -> p c d", c=NC), ALU.add).then_inc(m["y_out"], 1)
                for c in range(NC):
                    n = NC * g + c
                    dve.wait_ge(m["inter_in"], n + 1)
                    pu_v = pu[:, :].rearrange("p (h d) -> p h d", h=HG)
                    if c == 0:
                        V.tensor_copy(ST[:, :, :], pu_v).then_inc(m["state"], 1)
                        dve.sem_inc(m["inter_out"], 1)
                        continue
                    own(V.tensor_tensor(ST[:, :, :], ST[:, :, :], bcast(S.bb[:, hs, c], 2, P_B), ALU.mult))
                    V.tensor_tensor(ST[:, :, :], ST[:, :, :], pu_v, ALU.add).then_inc(m["state"], 1)
                    own(V.tensor_tensor(tmp[:, :, :], pi[:, :].rearrange("p (h d) -> p h d", h=HG), bcast(S.cols[:, c, 7, hs], 2, P_B), ALU.mult))
                    V.tensor_tensor(Y[:, c], Y[:, c], tmp[:, :, :], ALU.add).then_inc(m["inter_out"], 1)
                for f in range(4):
                    dve.wait_ge(m["t_in"], 4 * g + f + 1)
                    z = S.proj[:, NZ + 4 * g + f, 0:T]
                    V.tensor_tensor(z, a[f % 2][:, :], z, ALU.mult).then_inc(m["t_out"], 1)
                dve.wait_ge(m["so_in"], g + 1)
                if g:
                    dve.wait_ge(m["o_done"], 16 * g)
                V.tensor_copy(so[:, :, :], pi[:, :].rearrange("p (f n) -> p f n", f=4)).then_inc(m["so_ready"], 1)

        @block.sync
        def _(sp):
            for g in range(G_B):
                sp.wait_ge(m["so_ready"], g + 1)
                sp.dma_start(O["p_ssm"][0, 0, HG * g:HG * (g + 1)].rearrange("(f a) p n -> (a p) f n", a=2), so[:, :, :]).then_inc(m["o_done"], 16)
            sp.wait_ge(m["o_done"], 16 * G_B)


def sample_phase(nc, A, S, O):
    with Phase(nc) as ctx:
        sem = ctx.sem
        sb = lambda n, s: ctx.enter_context(nc.sbuf_tensor(n, s, F32))
        st = [sb(f"state{i}", [P, 4, 8, P]) for i in range(2)]
        vrow = sb("vrow", [B, D])
        brow = sb("brow", [B, 512])
        wk, qn, nd, hh, t1, t2 = (sb(f"{n}_sm", [P, B, H_A]) for n in ("wk", "qn", "nd", "hh", "t1", "t2"))
        dec, dt, yv, xd = (sb(f"{n}_sm", [P, KD, B]) for n in ("dec", "dt", "yv", "xd"))
        dsk = sb("dsk_sm", [P, KD])
        junk = sb("junk_sm", [P, P])
        nrow = sb("nrow_sm", [64, P])
        pr = ctx.enter_context(nc.psum_tensor("pr_sm", [P, 2, 512], F32))
        pv = [ctx.enter_context(nc.psum_tensor(f"pv{i}_sm", [P, 2, 512], F32)) for i in range(2)]
        ph = ctx.enter_context(nc.psum_tensor("ph_sm", [P, 512], F32))
        pm = ctx.enter_context(nc.psum_tensor("pm_sm", [P, 512], F32))
        m = {n: sem(n + "_sm") for n in ("in0", "in1", "turned", "rows", "spread", "updated", "read", "unit", "qn_in", "den_in", "num_in",
                                         "mean_in", "meant", "sq_in", "var_in", "var_out", "rooted", "n_in", "n_out", "o_done0", "o_done1", "o_done", "dve_own", "act_own")}
        block = ctx.enter_context(nc.Block())
        cv = A["state_mlstm_c"][0].rearrange("b h d v -> d b h v")
        sv = A["state_ssm"][0].rearrange("b (c a) p n -> (a p) b c n", a=2)
        oc = O["s_c"][0].rearrange("b h d v -> d b h v")
        os_ = O["s_ssm"][0].rearrange("b (c a) p n -> (a p) b c n", a=2)
        units = [(cv, oc, 0), (cv, oc, 4), (sv, os_, 0), (sv, os_, 4)]

        @block.sync
        def _(sp):
            for u, (src, _, b0) in enumerate(units):
                i = u % 2
                if u >= 2:
                    sp.wait_ge(m["unit"], u - 1)
                    for b in range(4):
                        sp.dma_start(units[u - 2][1][:, units[u - 2][2] + b], st[i][:, b]).then_inc(m[f"o_done{i}"], 16)
                    sp.wait_ge(m[f"o_done{i}"], 64)
                    if u - 2 < 2:
                        sp.wait_ge(m["num_in"], u - 1)
                for b in range(4):
                    sp.dma_start(st[i][:, b], src[:, b0 + b]).then_inc(m[f"in{i}"], 16)
            for u in (2, 3):
                sp.wait_ge(m["unit"], u + 1)
                for b in range(4):
                    sp.dma_start(units[u][1][:, units[u][2] + b], st[u % 2][:, b]).then_inc(m["o_done"], 16)
            sp.wait_ge(m["n_out"], 1)
            sp.dma_start(O["s_n"][0].rearrange("b h d -> (b h) d"), nrow[:, :]).then_inc(m["o_done"], 16)
            sp.wait_ge(m["o_done"], 16 * 9)

        @block.tensor
        def _(pe):
            for k in range(KD):
                nc.tensor.transpose(pr[0:B, k // 4, k % 4 * P:k % 4 * P + P], S.proj[:, NV + k, T:N], S.ident[:, :])
            for k in range(4):
                mm = nc.tensor.transpose(ph[0:B, k * P:(k + 1) * P], S.proj[:, NX + 8 + k, T:N], S.ident[:, :])
            mm.then_inc(m["turned"], 1)
            pe.wait_ge(m["rows"], 1)

            def spread(s):
                b = s % B
                if s >= 2:
                    pe.wait_ge(m["read"], s - 1)
                if s < B:
                    for j in range(2):
                        mm = nc.tensor.matmul(pv[s % 2][:, j, :], S.pick[0:B, b, :], vrow[:, j * 512:(j + 1) * 512], start=True, stop=True)
                else:
                    mm = nc.tensor.matmul(pv[s % 2][:, 0, :], S.pick[0:B, b, :], brow[:, :], start=True, stop=True)
                mm.then_inc(m["spread"], 1)

            for u in range(2):
                for b in range(4 * u, 4 * u + 4):
                    spread(b)
                pe.wait_ge(m["unit"], u + 1)
                for b in range(4 * u, 4 * u + 4):
                    for h in range(H_A):
                        mm = nc.tensor.matmul(pm[:, b * H_A + h:b * H_A + h + 1], st[u][:, b % 4, h, :], S.proj[:, NQ + h, T + b:T + b + 1],
                                              start=True, stop=True)
                mm.then_inc(m["num_in"], 1)
            pe.wait_ge(m["qn_in"], 1)
            nc.tensor.matmul(pm[:, 64:128], S.ones[:, :], qn[:, :, :].rearrange("p b h -> p (b h)"), start=True, stop=True).then_inc(m["den_in"], 1)
            nc.tensor.transpose(pr[0:64, 0, 0:P], S.n0[:, :], S.ident[:, :]).then_inc(m["n_in"], 1)
            pe.wait_ge(m["mean_in"], 1)
            nc.tensor.matmul(pm[:, 128:192], S.ones[:, :], hh[:, :, :].rearrange("p b h -> p (b h)"), start=True, stop=True).then_inc(m["meant"], 1)
            pe.wait_ge(m["sq_in"], 1)
            nc.tensor.matmul(pm[:, 192:256], S.ones[:, :], t1[:, :, :].rearrange("p b h -> p (b h)"), start=True, stop=True).then_inc(m["var_in"], 1)
            for s in range(B, 2 * B):
                spread(s)

        @block.scalar
        def _(act):
            own = Chain(act, m["act_own"])
            act.wait_ge(m["var_out"], 1)
            own(nc.scalar.activation(t2[:, :, :], t2[:, :, :], ACT.Ln))
            nc.scalar.activation(t2[:, :, :], t2[:, :, :], ACT.Exp, scale=-0.5).then_inc(m["rooted"], 1)

        @block.vector
        def _(dve):
            own = Chain(dve, m["dve_own"])
            V = nc.vector
            dve.wait_ge(m["turned"], 1)
            V.tensor_copy(vrow[:, :].rearrange("p (a n) -> p a n", a=2), pr[0:B, :, :])
            V.tensor_copy(brow[:, :], ph[0:B, :]).then_inc(m["rows"], 1)
            perm = lambda t: t.rearrange("p h b -> p b h")
            kT, qT = (perm(S.proj[:, s:s + 8, T:N]) for s in (NK, NQ))
            own(V.tensor_tensor(wk[:, :, :], kT, perm(S.ba[:, :, 12:20]), ALU.mult))
            n0 = S.n0[:, :].rearrange("p (b h) -> p b h", b=B)
            own(V.tensor_tensor(n0, n0, perm(S.ba[:, :, 4:12]), ALU.mult))
            own(V.tensor_tensor(n0, n0, wk[:, :, :], ALU.add))
            V.tensor_tensor(qn[:, :, :], n0, qT, ALU.mult).then_inc(m["qn_in"], 1)
            for a in range(2):
                ps = slice(64 * a, 64 * a + 64)
                V.tensor_copy(dec[ps], S.bb[ps, a::2, 4:12])
                V.tensor_copy(dt[ps], S.bb[ps, a::2, 12:20])
                V.tensor_copy(dsk[ps], S.bb[ps, a::2, 20])
            xs = S.proj[:, NX:NX + KD, T:N]
            dve.wait_ge(m["rows"], 1)
            own(V.memset(yv[:, :, :], 0.0))
            own(V.tensor_tensor(xd[:, :, :], dt[:, :, :], xs, ALU.mult))
            for u in range(2):
                dve.wait_ge(m[f"in{u}"], 64)
                for b in range(4):
                    last = V.tensor_tensor(st[u][:, b], st[u][:, b], bcast(S.ba[:, :, 4 + 4 * u + b], 2, P), ALU.mult)
                own(last)
                for b in range(4):
                    s = 4 * u + b
                    dve.wait_ge(m["spread"], s + 1)
                    for h in range(H_A):
                        last = V.scalar_tensor_tensor(out=st[u][:, b, h, :], in0=pv[s % 2][:, h // 4, h % 4 * P:h % 4 * P + P], scalar=wk[:, s, h:h + 1],
                                                      in1=st[u][:, b, h, :], op0=ALU.mult, op1=ALU.add)
                    last.then_inc(m["read"], 1)
                dve.wait_ge(m["read"], 4 * u + 4)
                dve.sem_inc(m["unit"], 1)
            dve.wait_ge(m["den_in"], 1)
            dve.wait_ge(m["num_in"], 2)
            flat = lambda t: t.rearrange("p b h -> p (b h)")
            own(V.tensor_copy(flat(nd[:, :, :]), pm[:, 64:128]))
            own(V.scalar_tensor_tensor(out=nd[:, :, :], in0=nd[:, :, :], scalar=-1.0, in1=nd[:, :, :], op0=ALU.mult, op1=ALU.max))
            own(V.tensor_tensor(nd[:, :, :], nd[:, :, :], perm(S.ba[:, :, 20:28]), ALU.max))
            own(V.reciprocal(nd[:, :, :], nd[:, :, :]))
            V.tensor_tensor(flat(hh[:, :, :]), pm[:, 0:64], flat(nd[:, :, :]), ALU.mult).then_inc(m["mean_in"], 1)
            dve.wait_ge(m["meant"], 1)
            own(V.scalar_tensor_tensor(out=flat(hh[:, :, :]), in0=pm[:, 128:192], scalar=-1.0 / P, in1=flat(hh[:, :, :]), op0=ALU.mult, op1=ALU.add))
            V.tensor_tensor(t1[:, :, :], hh[:, :, :], hh[:, :, :], ALU.mult).then_inc(m["sq_in"], 1)
            dve.wait_ge(m["var_in"], 1)
            V.tensor_scalar(flat(t2[:, :, :]), pm[:, 192:256], 1.0 / P, EPS, ALU.mult, ALU.add).then_inc(m["var_out"], 1)
            dve.wait_ge(m["rooted"], 1)
            own(V.tensor_tensor(hh[:, :, :], hh[:, :, :], t2[:, :, :], ALU.mult))
            own(V.tensor_tensor(hh[:, :, :], hh[:, :, :], bcast(S.vec[:, V_GA:V_GA + 8], 1, B), ALU.mult))
            V.tensor_tensor(qT, hh[:, :, :], perm(S.proj[:, NO:NO + 8, T:N]), ALU.mult)
            dve.wait_ge(m["n_in"], 1)
            V.tensor_copy(nrow[:, :], pr[0:64, 0, 0:P]).then_inc(m["n_out"], 1)
            for u in range(2):
                dve.wait_ge(m[f"in{u}"], 128)
                for b in range(4):
                    last = V.tensor_tensor(st[u][:, b], st[u][:, b], bcast(dec[:, :, 4 * u + b], 2, P), ALU.mult)
                own(last)
                for b in range(4):
                    s = 4 * u + b
                    dve.wait_ge(m["spread"], B + s + 1)
                    for c in range(KD):
                        g = c // 4
                        last = V.scalar_tensor_tensor(out=st[u][:, b, c, :], in0=pv[s % 2][:, 0, g * P:(g + 1) * P], scalar=xd[:, c, s:s + 1],
                                                      in1=st[u][:, b, c, :], op0=ALU.mult, op1=ALU.add)
                    own(last)
                    for c in range(KD):
                        g = c // 4
                        own(V.tensor_tensor_reduce(out=junk[:, :], in0=pv[s % 2][:, 0, 256 + g * P:256 + (g + 1) * P], in1=st[u][:, b, c, :],
                                                   scale=1.0, scalar=0.0, op0=ALU.mult, op1=ALU.add, accum_out=yv[:, c, s:s + 1]))
                    dve.sem_inc(m["read"], 1)
                dve.sem_inc(m["unit"], 1)
            own(V.tensor_tensor(xd[:, :, :], xs, bcast(dsk[:, :], 2, B), ALU.mult))
            own(V.tensor_tensor(yv[:, :, :], yv[:, :, :], xd[:, :, :], ALU.add))
            own(V.tensor_tensor(S.proj[:, NZ:NZ + KD, T:N], yv[:, :, :], S.proj[:, NZ:NZ + KD, T:N], ALU.mult))


NB = [TOPK // (a + 1) for a in range(TOPK)]
NCAND = sum(NB)
LOW = -3.0e38
TB = 52
NTB = N // TB
JG = 4
NG = NKEY // JG
PAIRS_TK = 6
PAIRS_GM = 4


def residual_phase(nc, name, S, src, gate):
    with Phase(nc) as ctx:
        own_s = ctx.sem(f"own_{name}")
        t = ctx.enter_context(nc.sbuf_tensor(f"t_{name}", [P, KD, B], F32))
        block = ctx.enter_context(nc.Block())

        @block.vector
        def _(dve):
            own = Chain(dve, own_s)
            for k in range(KD):
                nc.vector.scalar_tensor_tensor(out=S.xT[:, k, 0:T], in0=src[:, k, 0:T], scalar=S.mod[:, gate + k, 0:1],
                                               in1=S.xT[:, k, 0:T], op0=ALU.mult, op1=ALU.add)
            own(nc.vector.tensor_tensor(t[:, :, :], src[:, :, T:N], S.mod[:, gate:gate + KD, 1:9], ALU.mult))
            own(nc.vector.tensor_tensor(S.xT[:, :, T:N], S.xT[:, :, T:N], t[:, :, :], ALU.add))


def split_phase(nc, S):
    with Phase(nc) as ctx:
        high, low = ctx.sem("high"), ctx.sem("low")
        block = ctx.enter_context(nc.Block())

        @block.scalar
        def _(act):
            for k in range(KD):
                nc.scalar.activation(S.hH[:, k, :], S.h2T[:, k, :], ACT.Copy).then_inc(high, 1)

        @block.vector
        def _(dve):
            for k in range(KD):
                dve.wait_ge(high, k + 1)
                nc.vector.tensor_tensor(S.hL[:, k, :], S.h2T[:, k, :], S.hH[:, k, :].bitcast(F32), ALU.subtract).then_inc(low, 1)
            dve.wait_ge(low, KD)


def score_phase(nc, A, S, qry):
    with Phase(nc) as ctx:
        keys = ctx.enter_context(nc.sbuf_tensor("keys", [P, 2, P], F32))
        keysT = ctx.enter_context(nc.sbuf_tensor("keysT", [P, 2, P], F32))
        qs = ctx.enter_context(nc.sbuf_tensor("qs", [P, 2, PH, B], F32))
        ps = [ctx.enter_context(nc.psum_tensor(f"ps_sc{i}", [P, 4, P], F32)) for i in range(4)]
        pk = ctx.enter_context(nc.psum_tensor("pk_sc", [P, 4, P], F32))
        keys_in, keys_t, keys_s, gathered, scored, kept = (ctx.sem(n + "_sc") for n in ("keys_in", "keys_t", "keys_s", "gathered", "scored", "kept"))
        block = ctx.enter_context(nc.Block())

        @block.sync
        def _(sp):
            sp.dma_start(keys[:, :, :], A["peer_sub_keys"][0].rearrange("j k d -> k j d")).then_inc(keys_in, 16)
            sp.wait_ge(keys_in, 16)

        @block.vector
        def _(dve):
            nc.vector.tensor_copy(qs[:, :, :, :].rearrange("p j h b -> p h j b"),
                                  qry[:, :, T:N].rearrange("p (h j) b -> p h j b", j=2)).then_inc(gathered, 1)

        @block.tensor
        def _(pe):
            pe.wait_ge(keys_in, 16)
            nc.tensor.transpose(pk[:, 0, :], keys[:, 0, :], S.ident[:, :])
            nc.tensor.transpose(pk[:, 1, :], keys[:, 1, :], S.ident[:, :]).then_inc(keys_t, 1)
            pe.wait_ge(keys_s, 1)
            pe.wait_ge(gathered, 1)
            for j in range(2):
                mm = nc.tensor.matmul(pk[0:PH * B, j, :], qs[:, j, :, :].rearrange("p h b -> p (h b)"), keysT[:, j, :], start=True, stop=True)
            mm.then_inc(scored, 1)
            for t in range(NC):
                for q in range(4):
                    n = 4 * t + q
                    if n >= 4:
                        pe.wait_ge(kept, n - 2)
                    for i in range(4):
                        l = 4 * q + i
                        mm = nc.tensor.matmul(ps[q][:, i, :], qry[:, l, t * L:(t + 1) * L], keysT[:, l % 2, :], start=True, stop=True)
                    mm.then_inc(scored, 1)

        @block.scalar
        def _(act):
            act.wait_ge(keys_t, 1)
            nc.scalar.activation(keysT[:, :, :], pk[:, 0:2, :], ACT.Copy).then_inc(keys_s, 1)
            act.wait_ge(scored, 1)
            nc.scalar.activation(S.scS[:, :, :], pk[0:PH * B, 0:2, :], ACT.Copy).then_inc(kept, 1)
            for n in range(16):
                act.wait_ge(scored, n + 2)
                nc.scalar.activation(S.sc[:, n // 4, 4 * (n % 4):4 * (n % 4) + 4, :], ps[n % 4][:, :, :], ACT.Copy).then_inc(kept, 1)


class TopK:

    LINKS = 19

    def __init__(self, nc, S, name, ctx, rows, H, lists=None):
        sb = lambda n, s, d=F32: ctx.enter_context(nc.sbuf_tensor(f"{n}_{name}", s, d))
        self.nc, self.S, self.H, self.rows = nc, S, H, rows
        self.lists = lists if lists is not None else sb("lists", [rows, 2 * H, NKEY])
        self.top = sb("top", [rows, 2 * H, TOPK])
        self.idx = sb("idx", [rows, 2 * H, TOPK], U32)
        self.idf = sb("idf", [rows, 2 * H, TOPK])
        self.cand, self.cidx, self.cwk = (sb(n, [rows, H, NCAND]) for n in ("cand", "cidx", "cwk"))
        self.best = sb("best", [rows, H, TOPK])
        self.pos = sb("pos", [rows, H, TOPK], U32)
        self.posf = sb("posf", [rows, H, TOPK])
        self.hit = sb("hit", [rows, H * TOPK, NCAND])
        self.wk = self.hit[:, :, :].rearrange("p a b -> p (a b)")[:, 0:2 * H * NKEY].rearrange("p (l k) -> p l k", k=NKEY)
        self.ei = sb("ei", [rows, H * TOPK])
        self.eu = sb("eu", [rows, 2, H * TOPK], U32)
        self.eh = sb("eh", [rows, H * TOPK], U32)
        self.sum = sb("sum", [rows, H])

    def best_of(self, own, half, values, work, top, idx, n):
        V = self.nc.vector
        at = slice(8 * half, 8 * half + 8)
        src = work if half else values
        own.take(V)
        for l in range(n):
            last = V.max(top[:, l, at], src[:, l, :])
        own(last)
        own.take(V)
        for l in range(n):
            last = V.max_index(idx[:, l, at], top[:, l, at], src[:, l, :])
            if not half:
                last = V.match_replace(work[:, l, :], top[:, l, at], src[:, l, :], LOW)
        own(last)

    def lists_first(self, own):
        self.best_of(own, 0, self.lists, self.wk, self.top, self.idx, 2 * self.H)

    def lists_second(self, own):
        self.best_of(own, 1, self.lists, self.wk, self.top, self.idx, 2 * self.H)

    def candidates(self, own):
        V, n, H = self.nc.vector, self.rows, self.H
        own(V.tensor_copy(self.idf[:, :, :], self.idx[:, :, :]))
        t4 = self.top[:, :, :].rearrange("p (h j) k -> p h j k", j=2)
        i4 = self.idf[:, :, :].rearrange("p (h j) k -> p h j k", j=2)
        own(V.tensor_scalar(i4[:, :, 0, :], i4[:, :, 0, :], float(NKEY), None, ALU.mult))
        off = 0
        for a in range(8):
            o = slice(off, off + NB[a])
            V.tensor_tensor(self.cand[:, :, o], bcast(t4[:, :, 0, a], 2, NB[a]), t4[:, :, 1, 0:NB[a]], ALU.add)
            V.tensor_tensor(self.cidx[:, :, o], bcast(i4[:, :, 0, a], 2, NB[a]), i4[:, :, 1, 0:NB[a]], ALU.add)
            off += NB[a]
        o = slice(off, off + 8)
        V.tensor_tensor(self.cand[:, :, o], t4[:, :, 0, 8:16], t4[:, :, 1, 0:1].to_broadcast((n, H, 8)), ALU.add)
        own(V.tensor_tensor(self.cidx[:, :, o], i4[:, :, 0, 8:16], i4[:, :, 1, 0:1].to_broadcast((n, H, 8)), ALU.add))

    def sums(self, own):
        for half in range(2):
            self.best_of(own, half, self.cand, self.cwk, self.best, self.pos, self.H)
        own(self.nc.vector.tensor_copy(self.posf[:, :, :], self.pos[:, :, :]))

    def find(self):
        n = self.rows
        return self.nc.vector.tensor_tensor(self.hit[:, :, :], bcast(self.posf[:, :, :].rearrange("p h k -> p (h k)"), 2, NCAND),
                                            bcast(self.S.iota[0:n, 0:NCAND], 1, self.H * TOPK), ALU.is_equal)

    def shift(self, own):
        V = self.nc.vector
        own(V.tensor_copy(self.sum[:, :], self.best[:, :, 0]))
        return V.tensor_tensor(self.best[:, :, :], self.best[:, :, :], bcast(self.sum[:, :], 2, TOPK), ALU.subtract)

    def gates(self, own, out):
        V = self.nc.vector
        own(V.reduce_sum(self.sum[:, :], self.best[:, :, :], AX_X))
        own(V.reciprocal(self.sum[:, :], self.sum[:, :]))
        own(V.tensor_tensor(out.rearrange("p (h k) -> p h k", h=self.H), self.best[:, :, :], bcast(self.sum[:, :], 2, TOPK), ALU.mult))

    def experts(self, own, row, column):
        V = self.nc.vector
        own(V.reduce_sum(self.ei[:, :], self.hit[:, :, :], AX_X))
        own(V.tensor_copy(self.eu[:, 0, :], self.ei[:, :]))
        V.tensor_scalar(self.eu[:, 1, :], self.eu[:, 0, :], NKEY - 1, None, ALU.bitwise_and)
        own(V.tensor_scalar(self.eh[:, :], self.eu[:, 0, :], 7, None, ALU.logical_shift_right))
        V.tensor_copy(row, self.eh[:, :])
        return V.tensor_copy(column, self.eu[:, 1, :])


class LoopChain:

    def __init__(self, engine, sem, i, links, target, source):
        self.engine, self.sem, self.i, self.links, self.n = engine, sem, i, links, 0
        self.target, self.source = target, source

    def take(self, vector):
        vector.tensor_copy(self.target, self.source)

    def __call__(self, instruction):
        self.n += 1
        assert self.n <= self.links
        instruction.then_inc(self.sem, 1)
        self.engine.wait_ge(self.sem, self.links * self.i + self.n)


class Hidden:

    def __init__(self, nc, A, S, name, ctx, base, pairs, bufs, hidden_dram):
        sb = lambda n, s, d=F32: ctx.enter_context(nc.sbuf_tensor(f"{n}_{name}", s, d))
        self.nc, self.S, self.base, self.pairs, self.bufs, self.dram = nc, S, base, pairs, bufs, hidden_dram
        self.units = 2 * pairs
        self.u = [sb(f"u{i}", [P, 2, D]) for i in range(bufs)]
        self.ge = [sb(f"ge{i}", [P, 2, N]) for i in range(bufs)]
        self.utH = [sb(f"utH{i}", [P, KD, P], F32R) for i in range(2)]
        self.utL = [sb(f"utL{i}", [P, KD, P], F32R) for i in range(2)]
        self.pt = [ctx.enter_context(nc.psum_tensor(f"pt{i}_{name}", [P, 4, P], F32)) for i in range(2)]
        self.pa = [ctx.enter_context(nc.psum_tensor(f"pa{i}_{name}", [P, 512], F32)) for i in range(2)]
        self.uv = A["peer_u"][0].rearrange("(i j) d -> i j d", j=NKEY)
        self.u_in = [ctx.sem(f"u_in{i}_{name}") for i in range(bufs)]
        self.stored = [ctx.sem(f"ge_stored{i}_{name}") for i in range(bufs)]
        self.turned, self.high, self.low, self.hidden, self.gelued = (ctx.sem(f"{n}_{name}") for n in ("turned", "high", "low", "hidden", "gelued"))

    def load(self, sp, i, p):
        b, per = p % self.bufs, self.pairs // self.bufs
        sp.wait_ge(self.turned, 4 * self.pairs * i + 4 * (p + 1))
        sp.dma_start(self.u[b][:, :, :], self.uv[:, bass.ds(i * (2 * self.pairs) + 2 * (self.base + p), 2), :]).then_inc(self.u_in[b], 16)

    def start(self, pe):
        pe.sem_inc(self.turned, 4 * self.bufs)

    def turn(self, pe, i, u):
        p, b, per = u // 2, u // 2 % self.bufs, self.pairs // self.bufs
        if u % 2 == 0:
            pe.wait_ge(self.u_in[b], 16 * per * i + 16 * (p // self.bufs + 1))
        for x in range(2):
            pe.wait_ge(self.low, 2 * self.units * i + (2 * u + x + 1))
            for k in range(4):
                mm = self.nc.tensor.transpose(self.pt[x][:, k, :], self.u[b][:, u % 2, (4 * x + k) * P:(4 * x + k + 1) * P], self.S.ident[:, :])
            mm.then_inc(self.turned, 1)

    def hide(self, pe, i, u):
        S = self.S
        pe.wait_ge(self.low, 2 * self.units * i + (2 * u + 2 + 2))
        for h in range(2):
            tok = slice(h * HN, (h + 1) * HN)
            pe.wait_ge(self.gelued, 2 * self.units * i + (2 * u + h + 1))
            n = 0
            for k in range(KD):
                for w, x in ((self.utH, S.hH), (self.utH, S.hL), (self.utL, S.hH)):
                    mm = self.nc.tensor.matmul(self.pa[h][:, 0:HN], w[u % 2][:, k, :], x[:, k, tok], start=(n == 0), stop=(n == 3 * KD - 1))
                    n += 1
            mm.then_inc(self.hidden, 1)

    def move_high(self, act, i, u):
        for x in range(2):
            act.wait_ge(self.turned, 2 * self.units * i + (2 * u + x + 1 + 4 * self.bufs))
            if x == 0:
                act.wait_ge(self.hidden, 2 * self.units * i + (2 * u + 2))
            self.nc.scalar.activation(self.utH[u % 2][:, 4 * x:4 * x + 4, :], self.pt[x][:, :, :], ACT.Copy).then_inc(self.high, 1)

    def gelu(self, act, i, u):
        b, per = u // 2 % self.bufs, self.pairs // self.bufs
        if u % 2 == 0:
            act.wait_ge(self.stored[b], 16 * per * i + 16 * (u // 2 // self.bufs + 1))
        for h in range(2):
            act.wait_ge(self.hidden, 2 * self.units * i + (2 * u + h + 1 + 4))
            self.nc.scalar.activation(self.ge[b][:, u % 2, h * HN:(h + 1) * HN], self.pa[h][:, 0:HN], ACT.Gelu).then_inc(self.gelued, 1)
        if u % 2:
            act.wait_ge(self.gelued, 2 * self.units * i + (2 * u + 2 + 2))
            act.dma_start(self.dram[bass.ds(i * self.pairs + (self.base + u // 2), 1)].rearrange("q i e -> (q i) e"),
                          self.ge[b][:, :, :].rearrange("p j n -> p (j n)")).then_inc(self.stored[b], 16)

    def start_act(self, act):
        act.sem_inc(self.gelued, 2)
        for s in self.stored:
            act.sem_inc(s, 16)

    def finish_act(self, act, iterations):
        for s in self.stored:
            act.wait_ge(s, 16 * (self.pairs // self.bufs * iterations + 1))

    def start_dve(self, dve):
        dve.sem_inc(self.low, 2)
        dve.sem_inc(self.hidden, 4)

    def move_low(self, dve, i, u):
        for x in range(2):
            dve.wait_ge(self.high, 2 * self.units * i + (2 * u + x + 1))
            self.nc.vector.tensor_tensor(self.utL[u % 2][:, 4 * x:4 * x + 4, :], self.pt[x][:, :, :],
                                         self.utH[u % 2][:, 4 * x:4 * x + 4, :].bitcast(F32), ALU.subtract).then_inc(self.low, 1)


def topk_phase(nc, A, S, hidden_dram):
    with Phase(nc) as ctx:
        H = Hidden(nc, A, S, "tk", ctx, 0, PAIRS_TK, 3, hidden_dram)
        K = TopK(nc, S, "tk", ctx, P, PH)
        KS = TopK(nc, S, "ts", ctx, PH * B, 1, S.scS)
        res = ctx.enter_context(nc.sbuf_tensor("res_tk", [P, 3, P], F32))
        rs = ctx.enter_context(nc.sbuf_tensor("rs_tk", [PH * B, 3, TOPK], F32))
        rt = ctx.enter_context(nc.sbuf_tensor("rt_tk", [B, 3, P], F32))
        taken = ctx.enter_context(nc.sbuf_tensor("taken_tk", [1, 1], F32))
        pr = ctx.enter_context(nc.psum_tensor("pr_tk", [P, 4, P], F32))
        m = {n: ctx.sem(n + "_tk") for n in ("s_shifted", "s_gates", "s_res", "s_moved", "lists", "hit", "picked", "shifted",
                                             "gates", "res", "res_t", "res_s", "own", "s_own")}
        block = ctx.enter_context(nc.Block())
        U = H.units

        @block.sync
        def _(sp):
            with sp.Fori(0, NC) as i:
                for p in range(PAIRS_TK):
                    H.load(sp, i, p)
            sp.wait_ge(m["s_res"], 1)
            for h in range(PH):
                sp.dma_start(rt[:, :, h * TOPK:(h + 1) * TOPK], rs[h * B:(h + 1) * B, :, :]).then_inc(m["s_moved"], 16)
            sp.wait_ge(m["s_moved"], 16 * PH)

        @block.tensor
        def _(pe):
            H.start(pe)

            def tile(i, last=False):
                for u in range(U):
                    if not (last and u == U - 1):
                        H.turn(pe, i, u + 1)
                    H.hide(pe, i, u)
                    if u == 8:
                        pe.wait_ge(m["res"], 1 * i + 1)
                        pe.wait_ge(m["res_s"], 1 * i + 1)
                        for q in range(3):
                            mm = nc.tensor.transpose(pr[:, q, :], res[:, q, :], S.ident[:, :])
                        mm.then_inc(m["res_t"], 1)

            H.turn(pe, 0, 0)
            with pe.Fori(0, NC - 1) as i:
                tile(i)
            tile(NC - 1, last=True)
            pe.wait_ge(m["s_moved"], 16 * PH)
            pe.wait_ge(m["res_s"], NC + 1)
            for q in range(3):
                mm = nc.tensor.transpose(pr[:, q, 0:B], rt[:, q, :], S.ident[0:B, 0:B])
            mm.then_inc(m["res_t"], 1)

        @block.scalar
        def _(act):
            H.start_act(act)
            act.sem_inc(m["res_s"], 1)

            def tile(i, last=False):
                act.wait_ge(m["shifted"], 1 * i + 1)
                nc.scalar.activation(K.lists[:, :, :], S.sc[:, bass.ds(i, 1), :, :].rearrange("p a l k -> p (a l) k"), ACT.Copy).then_inc(m["lists"], 1)
                for u in range(U):
                    if not (last and u == U - 1):
                        H.move_high(act, i, u + 1)
                    H.gelu(act, i, u)
                    if u == 4:
                        act.wait_ge(m["shifted"], 1 * i + 2)
                        nc.scalar.activation(K.best[:, :, :], K.best[:, :, :], ACT.Exp).then_inc(m["gates"], 1)
                    if last and u == 6:
                        act.wait_ge(m["s_shifted"], 1)
                        nc.scalar.activation(KS.best[:, :, :], KS.best[:, :, :], ACT.Exp).then_inc(m["s_gates"], 1)
                    if u == 9:
                        act.wait_ge(m["res_t"], 1 * i + 1)
                        nc.scalar.activation(S.sel[:, :, bass.ds(i * L, L)], pr[:, 0:3, :], ACT.Copy).then_inc(m["res_s"], 1)

            H.move_high(act, 0, 0)
            with act.Fori(0, NC - 1) as i:
                tile(i)
            tile(NC - 1, last=True)
            act.wait_ge(m["res_t"], NC + 1)
            nc.scalar.activation(S.sel[:, :, T:N], pr[:, 0:3, 0:B], ACT.Copy).then_inc(m["res_s"], 1)
            H.finish_act(act, NC)

        @block.gpsimd
        def _(pool):
            with pool.Fori(0, NC) as i:
                pool.wait_ge(m["hit"], 1 * i + 1)
                for h in range(PH):
                    k = slice(h * TOPK, (h + 1) * TOPK)
                    last = nc.gpsimd.tensor_tensor(K.hit[:, k, :], K.hit[:, k, :], bcast(K.cidx[:, h, :], 1, TOPK), ALU.mult)
                last.then_inc(m["picked"], 1)

        @block.vector
        def _(dve):
            V = nc.vector
            H.start_dve(dve)
            dve.sem_inc(m["shifted"], 1)

            def tile(i, last=False):
                own = LoopChain(dve, m["own"], i, TopK.LINKS, taken[:, :], S.ones[0:1, 0:1])
                s_own = Chain(dve, m["s_own"])
                for u in range(U):
                    if not (last and u == U - 1):
                        H.move_low(dve, i, u + 1)
                    if u == 0:
                        dve.wait_ge(m["lists"], 1 * i + 1)
                        K.lists_first(own)
                    elif u == 1:
                        K.lists_second(own)
                    elif u == 2:
                        K.candidates(own)
                        K.sums(own)
                        K.shift(own).then_inc(m["shifted"], 1)
                    elif u == 3:
                        K.find().then_inc(m["hit"], 1)
                    elif u == 6:
                        dve.wait_ge(m["gates"], 1 * i + 1)
                        dve.wait_ge(m["res_s"], 1 * i + 1)
                        K.gates(own, res[:, 2, :])
                        dve.wait_ge(m["picked"], 1 * i + 1)
                        K.experts(own, res[:, 0, :], res[:, 1, :]).then_inc(m["res"], 1)
                    if last and u == 4:
                        KS.lists_first(s_own)
                        KS.lists_second(s_own)
                        KS.candidates(s_own)
                    elif last and u == 5:
                        KS.sums(s_own)
                        s_own(KS.find())
                        KS.shift(s_own).then_inc(m["s_shifted"], 1)
                    elif last and u == 7:
                        s_own(V.tensor_tensor(KS.hit[:, :, :], KS.hit[:, :, :], bcast(KS.cidx[:, 0, :], 1, TOPK), ALU.mult))
                        dve.wait_ge(m["s_gates"], 1)
                        KS.gates(s_own, rs[:, 2, :])
                        KS.experts(s_own, rs[:, 0, :], rs[:, 1, :]).then_inc(m["s_res"], 1)
                assert own.n == TopK.LINKS, own.n

            H.move_low(dve, 0, 0)
            with dve.Fori(0, NC - 1) as i:
                tile(i)
            tile(NC - 1, last=True)


def gate_matrix_phase(nc, A, S, gates, hidden_dram):
    QUADS = (0, 1, 2, 2, 2, 2, 2, 2)
    Q = TB // 4
    BANKS = 4
    assert sum(QUADS) == Q and NTB * PAIRS_GM + NC * PAIRS_TK == NKEY // 2
    with Phase(nc) as ctx:
        H = Hidden(nc, A, S, "gm", ctx, NC * PAIRS_TK, PAIRS_GM, 2, hidden_dram)
        sb = lambda n, s: ctx.enter_context(nc.sbuf_tensor(n, s, F32))
        pick = sb("pick_gm", [P, 3, TB])
        oh = sb("oh_gm", [P, 2, 4, 2, P])
        stage = sb("stage_gm", [P, NG, JG, TB])
        ps = [ctx.enter_context(nc.psum_tensor(f"ps_gm{i}", [P, 4, P], F32)) for i in range(BANKS)]
        picks, hot, multiplied, staged, stored = (ctx.sem(n + "_gm") for n in ("picks", "hot", "multiplied", "staged", "stored"))
        block = ctx.enter_context(nc.Block())
        gv = gates.rearrange("g i b e -> i b g e")
        U = H.units
        first = [sum(QUADS[:u]) for u in range(U + 1)]

        @block.sync
        def _(sp):
            with sp.Fori(0, NTB) as i:
                for p in range(PAIRS_GM):
                    H.load(sp, i, p)

        @block.vector
        def _(dve):
            V = nc.vector
            H.start_dve(dve)

            def tokens(i, last=False):
                dve.wait_ge(multiplied, Q * i + 2)
                V.tensor_copy(pick[:, :, :], S.sel[:, :, bass.ds(i * TB, TB)]).then_inc(picks, 1)
                for u in range(U):
                    if not (last and u == U - 1):
                        H.move_low(dve, i, u + 1)
                    if u == 0:
                        dve.wait_ge(picks, 1 * i + 1)
                    for q in range(first[u], first[u + 1]):
                        dve.wait_ge(multiplied, Q * i + (max(q, 1) + 1))
                        for t in range(4):
                            k = 4 * q + t
                            V.tensor_scalar(oh[:, q % 2, t, 0, :], S.iota[:, :], pick[:, 0, k:k + 1], None, ALU.is_equal)
                            hot_t = V.tensor_scalar(oh[:, q % 2, t, 1, :], S.iota[:, :], pick[:, 1, k:k + 1], pick[:, 2, k:k + 1], ALU.is_equal, ALU.mult)
                        hot_t.then_inc(hot, 1)

            H.move_low(dve, 0, 0)
            with dve.Fori(0, NTB - 1) as i:
                tokens(i)
            tokens(NTB - 1, last=True)

        @block.tensor
        def _(pe):
            H.start(pe)
            pe.sem_inc(multiplied, 2)

            def tokens(i, last=False):
                for u in range(U):
                    if not (last and u == U - 1):
                        H.turn(pe, i, u + 1)
                    H.hide(pe, i, u)
                    for q in range(first[u], first[u + 1]):
                        pe.wait_ge(hot, Q * i + (q + 1))
                        pe.wait_ge(staged, Q * i + max(q + 1, BANKS))
                        for t in range(4):
                            mm = nc.tensor.matmul(ps[q % BANKS][:, t, :], oh[:, q % 2, t, 0, :], oh[:, q % 2, t, 1, :], start=True, stop=True)
                        mm.then_inc(multiplied, 1)

            H.turn(pe, 0, 0)
            with pe.Fori(0, NTB - 1) as i:
                tokens(i)
            tokens(NTB - 1, last=True)

        @block.scalar
        def _(act):
            H.start_act(act)
            act.sem_inc(staged, BANKS)
            act.sem_inc(stored, 16)

            def tokens(i, last=False):
                for u in range(U + 1):
                    if u < U:
                        if not (last and u == U - 1):
                            H.move_high(act, i, u + 1)
                        H.gelu(act, i, u)
                    for q in range(first[max(u, 1) - 1], first[u]):
                        if q == 0:
                            act.wait_ge(stored, 16 * i + 16)
                        act.wait_ge(multiplied, Q * i + (q + 3))
                        nc.scalar.activation(stage[:, :, :, 4 * q:4 * q + 4].rearrange("p g j t -> p t (g j)"), ps[q % BANKS][:, :, :], ACT.Copy).then_inc(staged, 1)
                act.wait_ge(staged, Q * i + (Q + BANKS))
                act.dma_start(gv[:, bass.ds(i, 1), :, :].rearrange("i b g e -> i (b g) e"),
                              stage[:, :, :, :].rearrange("p g j t -> p g (j t)")).then_inc(stored, 16)

            H.move_high(act, 0, 0)
            with act.Fori(0, NTB - 1) as i:
                tokens(i)
            tokens(NTB - 1, last=True)
            act.wait_ge(stored, 16 * (NTB + 1))
            H.finish_act(act, NTB)


def value_phase(nc, A, S, gates, hidden_dram):
    with Phase(nc) as ctx:
        sem = ctx.sem
        sb = lambda n, s, d=F32: ctx.enter_context(nc.sbuf_tensor(n, s, d))
        vs = [sb(f"vs{i}", [P, 2, D]) for i in range(2)]
        vH = [sb(f"vH{i}", [P, JG, D], F32R) for i in range(2)]
        vL = [sb(f"vL{i}", [P, JG, D], F32R) for i in range(2)]
        ab = [sb(f"ab{i}", [P, JG, N]) for i in range(2)]
        gb = [sb(f"gb{i}", [P, NTB, JG, TB]) for i in range(2)]
        wH = [sb(f"wH{i}", [P, JG, N], F32R) for i in range(2)]
        wL = [sb(f"wL{i}", [P, JG, N], F32R) for i in range(2)]
        po = [ctx.enter_context(nc.psum_tensor(f"po_v{i}", [P, 2, 512], F32)) for i in range(4)]
        v_in, a_in, g_in = ([sem(f"{n}_in{i}_v") for i in range(2)] for n in "vag")
        high, low, weighted, w_high, w_low, mixed, added, zero = (
            sem(n + "_v") for n in ("high", "low", "weighted", "w_high", "w_low", "mixed", "added", "zero"))
        block = ctx.enter_context(nc.Block())
        vv = A["peer_v"][0].rearrange("(i j) d -> i j d", j=NKEY)
        blocked = lambda t: t.rearrange("p (b t) -> p b t", t=TB)

        @block.sync
        def _(sp):
            with sp.Fori(0, NG // 2) as i:
                for s in range(2):
                    sp.wait_ge(w_low, 2 * JG * i + JG * (s + 1))
                    sp.dma_start(ab[s][:, :, :].rearrange("p (q j) n -> p q (j n)", q=2),
                                 hidden_dram[bass.ds(4 * i + 2 * s, 2)].rearrange("q i e -> i q e")).then_inc(a_in[s], 16)
                    sp.dma_start(gb[s][:, :, :, :].rearrange("p b j t -> p (b j t)"),
                                 gates[bass.ds(2 * i + s, 1)].rearrange("g i b e -> (g i) (b e)")).then_inc(g_in[s], 16)
                    for q in range(2):
                        sp.wait_ge(low, 2 * JG * i + (JG * s + 2 * q + 2))
                        sp.dma_start(vs[q][:, :, :], vv[:, bass.ds(8 * i + (4 * s + 2 * q), 2), :]).then_inc(v_in[q], 16)

        @block.gpsimd
        def _(pool):
            pool.sem_inc(low, 4)
            with pool.Fori(0, NG // 2) as i:
                for s in range(2):
                    for j in range(JG):
                        pool.wait_ge(high, 2 * JG * i + (JG * s + j + 1))
                        nc.gpsimd.tensor_tensor(vL[s][:, j, :], vs[j // 2][:, j % 2, :], vH[s][:, j, :].bitcast(F32), ALU.subtract).then_inc(low, 1)

        @block.scalar
        def _(act):
            with act.Fori(0, NG // 2) as i:
                for s in range(2):
                    act.wait_ge(mixed, 2 * KD * i + KD * (s + 1))
                    for j in range(JG):
                        if j % 2 == 0:
                            act.wait_ge(v_in[j // 2], 32 * i + 16 * (s + 1))
                        nc.scalar.activation(vH[s][:, j, :], vs[j // 2][:, j % 2, :], ACT.Copy).then_inc(high, 1)
                        act.wait_ge(weighted, 2 * JG * i + (JG * s + j + 1))
                        nc.scalar.activation(wH[s][:, j, :], ab[s][:, j, :], ACT.Copy).then_inc(w_high, 1)

        @block.vector
        def _(dve):
            V = nc.vector
            V.memset(S.acc[:, :, :], 0.0).then_inc(zero, 1)
            dve.wait_ge(zero, 1)
            dve.sem_inc(w_low, 2 * JG)
            dve.sem_inc(added, 4 + KD)

            def weigh(i, s, j):
                if j == 0:
                    dve.wait_ge(a_in[s], 16 * i + 16)
                    dve.wait_ge(g_in[s], 16 * i + 16)
                V.tensor_tensor(blocked(ab[s][:, j, :]), blocked(ab[s][:, j, :]), gb[s][:, :, j, :], ALU.mult).then_inc(weighted, 1)
                dve.wait_ge(w_high, 2 * JG * i + (JG * s + j + 1))
                V.tensor_tensor(wL[s][:, j, :], ab[s][:, j, :], wH[s][:, j, :].bitcast(F32), ALU.subtract).then_inc(w_low, 1)

            def add(i, s, k):
                dve.wait_ge(mixed, 2 * KD * i + (KD * s + k + 1 + 2 * KD))
                V.tensor_tensor(halves(S.acc[:, k, :]), halves(S.acc[:, k, :]), po[k % 4][:, :, 0:HN], ALU.add).then_inc(added, 1)

            def two_groups(i, last=False):
                for s in range(2):
                    for j in range(JG):
                        if not (last and s == 1):
                            weigh(i if s == 0 else i + 1, 1 - s, j)
                        add(i, s, 2 * j)
                        add(i, s, 2 * j + 1)

            for j in range(JG):
                weigh(0, 0, j)
            with dve.Fori(0, NG // 2 - 1) as i:
                two_groups(i)
            two_groups(NG // 2 - 1, last=True)

        @block.tensor
        def _(pe):
            pe.sem_inc(mixed, 2 * KD)
            with pe.Fori(0, NG // 2) as i:
                for s in range(2):
                    for kp in range(KD // 2):
                        pe.wait_ge(added, 2 * KD * i + (KD * s + 2 * kp + 2 + KD))
                        for j in range(JG):
                            if kp == 0:
                                pe.wait_ge(low, 2 * JG * i + (JG * s + j + 1 + 4))
                                pe.wait_ge(w_low, 2 * JG * i + (JG * s + j + 1 + 2 * JG))
                            for x in range(2):
                                k = 2 * kp + x
                                cols = slice(k * P, (k + 1) * P)
                                for h in range(2):
                                    tok = slice(h * HN, (h + 1) * HN)
                                    for n, (v, w) in enumerate(((vH, wH), (vH, wL), (vL, wH))):
                                        mm = nc.tensor.matmul(po[k % 4][:, h, 0:HN], v[s][:, j, cols], w[s][:, j, tok],
                                                              start=(j == 0 and n == 0), stop=(j == JG - 1 and n == 2))
                                if j == JG - 1:
                                    mm.then_inc(mixed, 1)


def output_phase(nc, S, O, y):
    with Phase(nc) as ctx:
        st = [ctx.enter_context(nc.sbuf_tensor(f"st_out{i}", [P, 2, 512], F32)) for i in range(2)]
        ps = [ctx.enter_context(nc.psum_tensor(f"ps_out{i}", [P, 2, 512], F32)) for i in range(2)]
        turned, moved, done = (ctx.sem(n + "_out") for n in ("turned", "moved", "done"))
        block = ctx.enter_context(nc.Block())
        tiles = [(t * L, L, O["y_p"][0, t * L:(t + 1) * L, :]) for t in range(NC)] + [(T, B, O["y_s"].rearrange("b t d -> (b t) d"))]

        @block.tensor
        def _(pe):
            for t, (at, n, _) in enumerate(tiles):
                if t >= 2:
                    pe.wait_ge(moved, t - 1)
                for k in range(KD):
                    mm = nc.tensor.transpose(ps[t % 2][0:n, k // 4, k % 4 * P:k % 4 * P + P], y[:, k, at:at + n], S.ident[:, :])
                mm.then_inc(turned, 1)

        @block.scalar
        def _(act):
            for t, (_, n, _) in enumerate(tiles):
                act.wait_ge(turned, t + 1)
                if t >= 2:
                    act.wait_ge(done, 16 * (t - 1))
                nc.scalar.activation(st[t % 2][0:n], ps[t % 2][0:n], ACT.Copy).then_inc(moved, 1)

        @block.sync
        def _(sp):
            for t, (_, n, dst) in enumerate(tiles):
                sp.wait_ge(moved, t + 1)
                sp.dma_start(dst, st[t % 2][0:n].rearrange("p a b -> p (a b)")).then_inc(done, 16)
                sp.wait_ge(done, 16 * (t + 1))


class Buffers:
    pass


def program(nc, A, O, gates, hidden_dram):
    S, R = Buffers(), Buffers()
    with ExitStack() as whole:
        def sb(ctx, name, shape, dt=F32):
            t = ctx.enter_context(nc.sbuf_tensor(name, shape, dt))
            return t

        S.ident = sb(whole, "ident", [P, P])
        S.ones = sb(whole, "ones", [P, P])
        S.iota = sb(whole, "iota", [P, P])
        S.vec = sb(whole, "vec", [P, NVEC])
        S.mod = sb(whole, "mod", [P, 48, 9])
        S.rb = sb(whole, "rb", [P, N])
        S.gs = sb(whole, "gs", [P, KD, 9])
        S.xT = sb(whole, "xT", [P, KD, N])
        with ExitStack() as mixers:
            S.far = sb(mixers, "far", [P, P])
            S.wg = sb(mixers, "wg", [P, KD, 96])
            S.col = sb(mixers, "col", [H_B, 5])
            S.m0T = sb(mixers, "m0T", [H_A, B])
            S.silc = sb(mixers, "silc", [P, KD, 9])
            S.n0 = sb(mixers, "n0", [P, 64])
            S.cbufa = sb(mixers, "cbufa", [P, 384])
            S.cbufb = sb(mixers, "cbufb", [P, 288])
            S.pick = sb(mixers, "pick", [H_B, H_B, P])
            S.ea = sb(mixers, "ea", [H_B, 1])
            S.mS = sb(mixers, "mS", [H_A, B])
            S.mP = sb(mixers, "mP", [H_A, 1])
            S.cols = sb(mixers, "cols", [P, NC, 8, H_B])
            S.ba = sb(mixers, "ba", [P, H_A, 28])
            S.bb = sb(mixers, "bb", [P, H_B, 21])
            S.nrow = sb(mixers, "nrow", [H_A, P])
            R.a = sb(mixers, "row_a", [H_A, N])
            R.M = sb(mixers, "row_M", [H_A, N])
            R.cum = sb(mixers, "row_cum", [H_B, N])
            R.dt = sb(mixers, "row_dt", [H_B, N])
            setup_phase(nc, A, S)
            project(nc, "ada", [(0, 6, 0)], A["w_ada"][0], KD, lambda k: S.silc[:, k, :], 9,
                    lambda c, bank: nc.scalar.activation(S.mod[:, bass.ds(c, 1), :], bank[:, 0:1, 0:9], ACT.Copy))
            with Phase(nc) as ctx:
                added = ctx.sem("bias_added")
                block = ctx.enter_context(nc.Block())

                @block.vector
                def _(dve):
                    nc.vector.tensor_tensor(S.mod[:, :, :], S.mod[:, :, :], bcast(S.vec[:, V_BADA:V_BADA + 48], 2, 9), ALU.add).then_inc(added, 1)
                    dve.wait_ge(added, 1)

            S.proj = sb(mixers, "proj", [P, SLOTS, N])
            with ExitStack() as ctx:
                S.hT = sb(ctx, "hT", [P, KD, N])
                norm_phase(nc, "n1", S, lambda k: S.xT[:, k, :], KD, modulate(nc, S, S.hT, V_N1, 0, 8))
                keep = lambda c, bank: nc.scalar.activation(S.proj[:, bass.ds(c, 1), :].rearrange("p c (a n) -> p (c a) n", a=2), bank[:, :, 0:HN], ACT.Copy)
                project(nc, "in", [(0, 4, 0), (Z0, 2, NZ)], A["w_in"][0], KD, lambda k: S.hT[:, k, :], N, keep)
                project(nc, "in2", [(Z0 + 4 * 512 - 512, 1, NZ + 12)], A["w_in"][0], KD, lambda k: S.hT[:, k, :], N, keep)
                gates_phase(nc, A, S, R, O)
            conv_phase(nc, A, S, O)
            mlstm_phase(nc, S, R, O)
            ssd_phase(nc, S, R, O)
            sample_phase(nc, A, S, O)

            def gain(dve, own):
                for k in range(KD):
                    last = nc.vector.scalar_tensor_tensor(out=S.proj[:, NZ + k, :], in0=S.proj[:, NZ + k, :], scalar=S.vec[:, V_GB + k:V_GB + k + 1],
                                                          in1=S.rb[:, :], op0=ALU.mult, op1=ALU.mult)
                own(last)
            norm_phase(nc, "ssm", S, lambda k: S.proj[:, NZ + k, :], KD, gain)
            mixed = lambda c, bank: nc.scalar.activation(S.proj[:, bass.ds(c + NK, 1), :].rearrange("p c (a n) -> p (c a) n", a=2), bank[:, :, 0:HN], ACT.Copy)
            project(nc, "out", [(0, 2, 0)], A["w_out"][0], 2 * KD, lambda k: S.proj[:, (NQ + k if k < KD else NZ + k - KD), :], N, mixed)
            residual_phase(nc, "r1", S, S.proj[:, NK:NK + KD, :], 16)
        with ExitStack() as experts:
            S.sel = sb(experts, "sel", [P, 3, N])
            S.hH = sb(experts, "hH", [P, KD, N], F32R)
            S.hL = sb(experts, "hL", [P, KD, N], F32R)
            with ExitStack() as scores:
                S.sc = sb(scores, "sc", [P, NC, 16, NKEY])
                S.scS = sb(scores, "scS", [PH * B, 2, NKEY])
                with ExitStack() as ctx:
                    S.h2T = sb(ctx, "h2T", [P, KD, N])
                    qry = sb(ctx, "qry", [P, 16, N])
                    norm_phase(nc, "n2", S, lambda k: S.xT[:, k, :], KD, modulate(nc, S, S.h2T, V_N2, 24, 32))
                    project(nc, "query", [(0, 2, 0)], A["peer_w_query"][0], KD, lambda k: S.h2T[:, k, :], N,
                            lambda c, bank: nc.scalar.activation(qry[:, bass.ds(c, 1), :].rearrange("p c (a n) -> p (c a) n", a=2), bank[:, :, 0:HN], ACT.Copy))
                    split_phase(nc, S)
                    score_phase(nc, A, S, qry)
                topk_phase(nc, A, S, hidden_dram)
            gate_matrix_phase(nc, A, S, gates, hidden_dram)
        S.acc = sb(whole, "acc", [P, KD, N])
        value_phase(nc, A, S, gates, hidden_dram)
        residual_phase(nc, "r2", S, S.acc, 40)

        def final(dve, own):
            for k in range(KD):
                last = nc.vector.scalar_tensor_tensor(out=S.acc[:, k, :], in0=S.xT[:, k, :], scalar=S.vec[:, V_GF + k:V_GF + k + 1],
                                                      in1=S.rb[:, :], op0=ALU.mult, op1=ALU.mult)
            own(last)
        norm_phase(nc, "nf", S, lambda k: S.xT[:, k, :], KD, final)
        output_phase(nc, S, O, S.acc)


_INS = ["x_prompt", "x_sample", "c_prompt", "c_sample", "state_mlstm_c", "state_mlstm_n", "state_mlstm_m", "state_mlstm_conv",
        "state_ssm", "state_ssm_conv", "w_ada", "b_ada", "norm1_g", "norm2_g", "w_in", "mlstm_gate_b", "conv_a_w", "conv_a_b",
        "mlstm_norm_g", "conv_b_w", "conv_b_b", "dt_bias", "a_log", "d_skip", "ssm_norm_g", "w_out", "peer_w_query",
        "peer_sub_keys", "peer_u", "peer_v", "final_norm_g"]
_OUTS = [("y_p", (1, T, D)), ("y_s", (B, 1, D)),
         ("p_c", (1, 1, H_A, P, P)), ("p_n", (1, 1, H_A, P)), ("p_m", (1, 1, H_A)), ("p_conva", (1, 1, 3, 2 * D)),
         ("p_ssm", (1, 1, H_B, P_B, P)), ("p_convb", (1, 1, 3, 1536)),
         ("s_c", (1, B, H_A, P, P)), ("s_n", (1, B, H_A, P)), ("s_m", (1, B, H_A)), ("s_conva", (1, B, 3, 2 * D)),
         ("s_ssm", (1, B, H_B, P_B, P)), ("s_convb", (1, B, 3, 1536))]


def kernel(**inputs):
    import numpy as _np
    import concourse.bacc as _bacc
    from concourse import mybir as _mybir
    from concourse.bass_utils import run_bass_kernel_spmd as _run

    nc = _bacc.Bacc("TRN2", target_bir_lowering=False, num_devices=1)
    arrays, ins, outs = {}, {}, {}
    for name in _INS:
        a = _np.ascontiguousarray(inputs[name])
        arrays[f"in_{name}_dram"] = a
        ins[name] = nc.dram_tensor(f"in_{name}_dram", a.shape, _mybir.dt.from_np(a.dtype), kind="ExternalInput").ap()
    for i, (name, shape) in enumerate(_OUTS):
        outs[name] = nc.dram_tensor(f"out_{i}_dram", shape, F32, kind="ExternalOutput").ap()
    gates = nc.dram_tensor("gates_dram", (NG, P, NTB, JG * TB), F32, kind="Internal").ap()
    hidden = nc.dram_tensor("hidden_dram", (NKEY // 2, P, 2 * N), F32, kind="Internal").ap()
    program(nc, ins, outs, gates, hidden)
    r = _run(nc, [arrays], core_ids=[0])
    return tuple(r.results[0][f"out_{i}_dram"] for i in range(len(_OUTS)))
```

```python
from contextlib import ExitStack

import concourse.bass as bass
from concourse import mybir

F32 = mybir.dt.float32
F32R = mybir.dt.float32r
BF16 = mybir.dt.bfloat16
U32 = mybir.dt.uint32
ALU = mybir.AluOpType
ACT = mybir.ActivationFunctionType
AX_X = mybir.AxisListType.X

P = 128
D = 1024
KD = D // P
T = 512
B = 8
N = T + B
HN = N // 2
L = 128
NC = T // L
H_A = 8
H_B = 16
P_B = 64
G_B = 2
CONV = 4
NQ, NK, NV, NO, NZ, NX = 0, 8, 16, 24, 32, 40
SLOTS = 52
IG0, Z0, DT0 = 4096, 4112, 6672
PH = 8
NKEY = 128
TOPK = 16
EPS = 1e-6
FAR = 1e4
SPLIT = 64
KSCALE = float(P) ** -0.5

V_BADA, V_N1, V_N2, V_CAW = 0, 48, 56, 64
V_CAB, V_CBW, V_CBB, V_GA, V_GB, V_GF = 128, 144, 192, 204, 212, 220
NVEC = 228


class Chain:

    def __init__(self, engine, sem):
        self.engine, self.sem, self.n = engine, sem, 0

    def __call__(self, instruction):
        self.n += 1
        instruction.then_inc(self.sem, 1)
        self.engine.wait_ge(self.sem, self.n)

    def take(self, vector):
        pass


class Phase(ExitStack):

    def __init__(self, nc):
        super().__init__()
        self.nc, self.semaphores = nc, []
        self.callback(self.clear)

    def sem(self, name):
        self.semaphores.append(self.nc.alloc_semaphore(name=name))
        return self.semaphores[-1]

    def clear(self):
        self.nc.all_engine_barrier()
        self.nc.clear_and_free_semaphores(self.semaphores)
        self.nc.all_engine_barrier()


def halves(t):
    return t.rearrange("p (a n) -> p a n", a=2)


def setup_phase(nc, A, S):
    with Phase(nc) as ctx:
        sem = ctx.sem
        rows = ctx.enter_context(nc.sbuf_tensor("rows", [P, 11, P], F32))
        xrow = ctx.enter_context(nc.sbuf_tensor("xrow", [P, NC, D], F32))
        ps = [ctx.enter_context(nc.psum_tensor(f"ps_set{i}", [P, 512], F32)) for i in range(8)]
        rows_in, x_in, small_in = sem("rows_in"), sem("x_in"), sem("small_in")
        zeroed, consts, turned, moved, moved_c = sem("zeroed"), sem("consts"), sem("turned"), sem("moved"), sem("moved_c")
        pool_own = sem("pool_own_set")
        loads = [
            (0, 0, A["b_ada"][0].rearrange("(r p) -> r p", p=P)),
            (0, 48, A["norm1_g"][0].rearrange("(r p) -> r p", p=P)),
            (0, 56, A["norm2_g"][0].rearrange("(r p) -> r p", p=P)),
            (0, 64, A["conv_a_w"][0].rearrange("j (r p) -> (j r) p", p=P)),
            (1, 0, A["conv_a_b"][0].rearrange("(r p) -> r p", p=P)),
            (1, 16, A["conv_b_w"][0].rearrange("j (r p) -> (j r) p", p=P)),
            (1, 64, A["conv_b_b"][0].rearrange("(r p) -> r p", p=P)),
            (1, 76, A["mlstm_norm_g"][0].rearrange("(r p) -> r p", p=P)),
            (1, 84, A["ssm_norm_g"][0].rearrange("(r p) -> r p", p=P)),
            (1, 92, A["final_norm_g"].rearrange("(r p) -> r p", p=P)),
            (2, 0, A["c_prompt"].rearrange("b (r p) -> (b r) p", p=P)),
            (2, 8, A["c_sample"].rearrange("b (r p) -> (b r) p", p=P)),
            (3, 0, A["x_sample"].rearrange("b t (r p) -> (b t r) p", p=P)),
            (3, 64, A["state_mlstm_n"][0].rearrange("b h d -> (b h) d")),
        ]
        ca = A["state_mlstm_conv"][0].rearrange("b j (r p) -> (b j r) p", p=P)
        cb = A["state_ssm_conv"][0].rearrange("b j (r p) -> (b j r) p", p=P)
        loads += [(4 + i, 0, ca[i * P:(i + 1) * P]) for i in range(3)]
        loads += [(7 + i, 0, cb[i * P:min((i + 1) * P, 288)]) for i in range(3)]
        height = [P, 100, 72, P, P, P, P, P, P, 32]
        block = ctx.enter_context(nc.Block())

        @block.sync
        def _(sp):
            for tile, at, src in loads:
                sp.dma_start(rows[at:at + src.shape[0], tile, :], src).then_inc(rows_in, 16)
            for t in range(NC):
                sp.dma_start(xrow[:, t, :], A["x_prompt"][0, t * L:(t + 1) * L, :]).then_inc(x_in, 16)
            sp.wait_ge(zeroed, 1)
            wi = A["w_in"][0].rearrange("(k p) n -> p k n", p=P)
            for at, col, n in ((0, IG0, 8), (32, IG0 + 8, 8), (64, DT0, 16)):
                sp.dma_start(S.wg[:, :, at:at + n], wi[:, :, col:col + n]).then_inc(small_in, 16)
            for row, src in enumerate((A["mlstm_gate_b"][0, 0], A["mlstm_gate_b"][0, 1])):
                sp.dma_start(S.col[0:H_A, row:row + 1], src.rearrange("(a b) -> a b", b=1)).then_inc(small_in, 16)
            for row, name in ((2, "dt_bias"), (3, "a_log"), (4, "d_skip")):
                sp.dma_start(S.col[0:H_B, row:row + 1], A[name][0].rearrange("(a b) -> a b", b=1)).then_inc(small_in, 16)
            sp.dma_start(S.m0T[:, :], A["state_mlstm_m"][0].rearrange("b h -> h b"), allow_slow_non_contiguous=True).then_inc(small_in, 16)
            sp.wait_ge(small_in, 16 * 9)

        @block.gpsimd
        def _(pool):
            own = Chain(pool, pool_own)
            own(nc.gpsimd.memset(S.ident[:, :], 0.0))
            nc.gpsimd.affine_select(out=S.ident[:, :], in_=S.ident[:, :], compare_op=ALU.not_equal, fill=1.0,
                                    base=0, pattern=[[-1, P]], channel_multiplier=1).then_inc(consts, 1)
            nc.gpsimd.iota(S.iota[:, :], [[1, P]], base=0, channel_multiplier=0,
                           allow_small_or_imprecise_dtypes=True)
            own(nc.gpsimd.memset(S.far[:, :], 0.0))
            own(nc.gpsimd.affine_select(out=S.far[:, :], in_=S.far[:, :], compare_op=ALU.is_ge, fill=FAR,
                                        base=0, pattern=[[1, P]], channel_multiplier=-1))

        @block.vector
        def _(dve):
            nc.vector.memset(S.wg[:, :, :], 0.0).then_inc(zeroed, 1)
            nc.vector.memset(S.ones[:, :], 1.0)
            dve.wait_ge(turned, 3)
            nc.vector.tensor_copy(S.vec[:, 0:P], ps[0][:, 0:P])
            nc.vector.tensor_copy(S.vec[:, P:NVEC], ps[0][:, P:P + 100])
            nc.vector.tensor_copy(S.xT[:, :, T:N].rearrange("p k b -> p b k"),
                                  ps[0][:, 384:448].rearrange("p (b k) -> p b k", k=KD))
            nc.vector.tensor_copy(S.n0[:, :], ps[0][:, 448:512]).then_inc(moved, 1)
            nc.vector.tensor_copy(S.cbufa[:, 0:384], ps[1][:, 0:384])
            nc.vector.tensor_copy(S.cbufb[:, 0:128], ps[1][:, 384:512])
            nc.vector.tensor_copy(S.cbufb[:, 128:288], ps[2][:, 0:160]).then_inc(moved, 1)
            for k in range(KD):
                dve.wait_ge(turned, 4 + k)
                nc.vector.tensor_copy(S.xT[:, k, 0:T], ps[3 + k % 5][:, :]).then_inc(moved, 1)

        @block.scalar
        def _(act):
            act.wait_ge(moved, 1)
            nc.scalar.activation(S.silc[:, :, 0:1], ps[0][:, 256:264].rearrange("p (k a) -> p k a", a=1), ACT.Silu)
            nc.scalar.activation(S.silc[:, :, 1:9].rearrange("p k b -> p b k"),
                                 ps[0][:, 264:328].rearrange("p (b k) -> p b k", k=KD), ACT.Silu).then_inc(moved_c, 1)

        @block.tensor
        def _(pe):
            pe.wait_ge(consts, 1)
            pe.wait_ge(rows_in, 16 * len(loads))
            for t in range(10):
                h = height[t]
                mm = nc.tensor.transpose(ps[t // 4][:, t % 4 * P:t % 4 * P + h], rows[0:h, t, :], S.ident[0:h, 0:h])
                if t in (3, 7, 9):
                    mm.then_inc(turned, 1)
            pe.wait_ge(x_in, 16 * NC)
            for k in range(KD):
                if k >= 5:
                    pe.wait_ge(moved, 2 + k - 4)
                for t in range(NC):
                    mm = nc.tensor.transpose(ps[3 + k % 5][:, t * L:(t + 1) * L], xrow[:, t, k * P:(k + 1) * P], S.ident[:, :])
                mm.then_inc(turned, 1)


def project(nc, name, runs, w, K, X, evict):
    cols = 4096 // K
    per = cols // P
    wv = w.rearrange("(k p) n -> p k n", p=P)
    with Phase(nc) as ctx:
        wb = [ctx.enter_context(nc.sbuf_tensor(f"wb{i}_{name}", [P, K, cols], F32)) for i in range(2)]
        ps = [ctx.enter_context(nc.psum_tensor(f"ps{i}_{name}", [P, 2, 512], F32)) for i in range(2)]
        w_in = [ctx.sem(f"w_in{i}_{name}") for i in range(2)]
        product = ctx.sem(f"product_{name}")
        evicted = ctx.sem(f"evicted_{name}")
        block = ctx.enter_context(nc.Block())

        def over_runs(engine, step):
            pairs = 0
            for col, n, chunk in runs:
                with engine.Fori(0, n) as i:
                    for j in range(2):
                        step(i, pairs, j, col, chunk)
                pairs += n

        @block.sync
        def _(sp):
            def load(i, pairs, j, col, _):
                sp.wait_ge(product, 2 * per * i + per * (2 * pairs + j + 1))
                sp.dma_start(wb[j][:, :, :], wv[:, :, bass.ds(i * (2 * cols) + (col + j * cols), cols)]).then_inc(w_in[j], 16)
            over_runs(sp, load)

        @block.tensor
        def _(pe):
            pe.sem_inc(product, 2 * per)

            def multiply(i, pairs, j, *_):
                pe.wait_ge(w_in[j], 16 * i + 16 * (pairs + 1))
                for m in range(per):
                    c = j * per + m
                    pe.wait_ge(evicted, 2 * per * i + (2 * per * pairs + c + 1))
                    for h in range(2):
                        for k in range(K):
                            mm = nc.tensor.matmul(ps[c % 2][:, h, 0:HN], wb[j][:, k, m * P:(m + 1) * P],
                                                  X(k)[:, h * HN:(h + 1) * HN], start=(k == 0), stop=(k == K - 1))
                    mm.then_inc(product, 1)
            over_runs(pe, multiply)

        @block.scalar
        def _(act):
            act.sem_inc(evicted, 2)

            def move(i, pairs, j, _, chunk):
                for m in range(per):
                    c = j * per + m
                    act.wait_ge(product, 2 * per * i + (2 * per * (pairs + 1) + c + 1))
                    evict(2 * per * i + (chunk + c), ps[c % 2]).then_inc(evicted, 1)
            over_runs(act, move)


def project_split(nc, name, runs, w, XH, XL, out):
    per = 2
    cols = per * P
    wv = w.rearrange("(k p) n -> p k n", p=P)
    with Phase(nc) as ctx:
        sb = lambda n, s, d=F32: ctx.enter_context(nc.sbuf_tensor(f"{n}_{name}", s, d))
        wb = [sb(f"wb{i}", [P, KD, cols]) for i in range(2)]
        wH = [sb(f"wH{i}", [P, KD, P], F32R) for i in range(2)]
        wL = [sb(f"wL{i}", [P, KD, P], F32R) for i in range(2)]
        ps = [ctx.enter_context(nc.psum_tensor(f"ps{i}_{name}", [P, 2, 512], F32)) for i in range(2)]
        w_in = [ctx.sem(f"w_in{i}_{name}") for i in range(2)]
        high, low, product, evicted = (ctx.sem(f"{n}_{name}") for n in ("high", "low", "product", "evicted"))
        block = ctx.enter_context(nc.Block())

        def over_runs(engine, step):
            pairs = 0
            for col, n, chunk in runs:
                with engine.Fori(0, n) as i:
                    for j in range(2):
                        step(i, pairs, j, col, chunk)
                pairs += n

        @block.sync
        def _(sp):
            def load(i, pairs, j, col, _):
                sp.wait_ge(low, 2 * per * i + per * (2 * pairs + j + 1))
                sp.dma_start(wb[j][:, :, :], wv[:, :, bass.ds(i * (2 * cols) + (col + j * cols), cols)]).then_inc(w_in[j], 16)
            over_runs(sp, load)

        @block.scalar
        def _(act):
            def move_high(i, pairs, j, *_):
                act.wait_ge(w_in[j], 16 * i + 16 * (pairs + 1))
                for m in range(per):
                    act.wait_ge(product, 2 * per * i + (2 * per * pairs + j * per + m + 1))
                    nc.scalar.activation(wH[m][:, :, :], wb[j][:, :, m * P:(m + 1) * P], ACT.Copy).then_inc(high, 1)
            over_runs(act, move_high)

        @block.gpsimd
        def _(pool):
            pool.sem_inc(low, 2 * per)

            def move_low(i, pairs, j, *_):
                for m in range(per):
                    pool.wait_ge(high, 2 * per * i + (2 * per * pairs + j * per + m + 1))
                    nc.gpsimd.tensor_tensor(wL[m][:, :, :], wb[j][:, :, m * P:(m + 1) * P], wH[m][:, :, :].bitcast(F32), ALU.subtract).then_inc(low, 1)
            over_runs(pool, move_low)

        @block.tensor
        def _(pe):
            pe.sem_inc(product, 2)

            def multiply(i, pairs, j, *_):
                for m in range(per):
                    c = 2 * per * pairs + j * per + m
                    pe.wait_ge(low, 2 * per * i + (c + 1 + 2 * per))
                    pe.wait_ge(evicted, 2 * per * i + (c + 1))
                    for h in range(2):
                        tok = slice(h * HN, (h + 1) * HN)
                        for k in range(KD):
                            for n, (a, b) in enumerate(((wH, XH), (wH, XL), (wL, XH))):
                                mm = nc.tensor.matmul(ps[m][:, h, 0:HN], a[m][:, k, :], b[:, k, tok],
                                                      start=(k == 0 and n == 0), stop=(k == KD - 1 and n == 2))
                    mm.then_inc(product, 1)
            over_runs(pe, multiply)

        @block.vector
        def _(dve):
            dve.sem_inc(evicted, 2)

            def move(i, pairs, j, _, chunk):
                for m in range(per):
                    c = j * per + m
                    dve.wait_ge(product, 2 * per * i + (2 * per * pairs + c + 1 + 2))
                    nc.vector.tensor_copy(out[:, bass.ds(2 * per * i + (chunk + c), 1), :].rearrange("p c (a n) -> p (c a) n", a=2),
                                          ps[m][:, :, 0:HN]).then_inc(evicted, 1)
            over_runs(dve, move)


def input_phase(nc, A, S, XH, XL):
    per = 2
    cols = per * P
    wv = A["w_in"][0].rearrange("(k p) n -> p k n", p=P)
    conv_b, conv_a = (16, V_CBW, 12, V_CBB), (0, V_CAW, 16, V_CAB)
    runs = [(Z0 + D, 3, NX, conv_b), (0, 4, NQ, conv_a), (2 * D, 2, NV, None), (3 * D, 2, NO, ACT.Sigmoid), (Z0, 2, NZ, ACT.Silu)]
    with Phase(nc) as ctx:
        sb = lambda n, s, d=F32: ctx.enter_context(nc.sbuf_tensor(f"{n}_in", s, d))
        wb = [sb(f"wb{i}", [P, KD, cols]) for i in range(2)]
        wH = [sb(f"wH{i}", [P, KD, P], F32R) for i in range(2)]
        wL = [sb(f"wL{i}", [P, KD, P], F32R) for i in range(2)]
        y = sb("y", [P, 2, T])
        columns = sb("columns", [P, 2, CONV + 1])
        ps = [ctx.enter_context(nc.psum_tensor(f"ps{i}_in", [P, 2, 512], F32)) for i in range(2)]
        w_in = [ctx.sem(f"w_in{i}_in") for i in range(2)]
        high, low, product, evicted, own, convd, used = (ctx.sem(f"{n}_in") for n in ("high", "low", "product", "evicted", "dve_own", "convd", "used"))
        block = ctx.enter_context(nc.Block())
        slot = lambda i, first: S.proj[:, bass.ds(2 * per * i + first, 1), :]
        split = lambda t: t.rearrange("p c (a n) -> p (c a) n", a=2)

        def over_runs(engine, step, peel=False):
            chunks = 0
            for r, run in enumerate(runs):
                n = run[1] - (peel and r == len(runs) - 1)
                with engine.Fori(0, n) as i:
                    for c in range(2 * per):
                        step(i, chunks + c, c, run, False)
                chunks += 2 * per * run[1]
            if peel:
                for c in range(2 * per):
                    step(run[1] - 1, chunks - 2 * per * run[1] + c, c, run, c >= 2 * per - 2)

        @block.sync
        def _(sp):
            def load(i, n, c, run, _):
                if c % per == 0:
                    sp.wait_ge(low, 2 * per * i + (n + per))
                    sp.dma_start(wb[c // per][:, :, :], wv[:, :, bass.ds(i * (2 * cols) + (run[0] + c * P), cols)]).then_inc(w_in[c // per], 16)
            over_runs(sp, load)

        @block.scalar
        def _(act):
            def move_high(i, n, c):
                j = c // per % 2
                if c % per == 0:
                    act.wait_ge(w_in[j], 16 * i + 16 * (n // (2 * per) + 1))
                act.wait_ge(product, 2 * per * i + (n + 1))
                nc.scalar.activation(wH[c % per][:, :, :], wb[j][:, :, c % per * P:(c % per + 1) * P], ACT.Identity).then_inc(high, 1)

            def step(i, n, c, run, last):
                if not last:
                    move_high(i, n + 2, c + 2)
                _, _, first, then = run
                if isinstance(then, tuple):
                    act.wait_ge(convd, 2 * per * i + (n + 1))
                    nc.scalar.activation(slot(i, first + c)[:, :, 0:T], y[:, c % 2:c % 2 + 1, :], ACT.Silu).then_inc(used, 1)
                elif then is not None:
                    act.wait_ge(product, 2 * per * i + (n + 1 + 2))
                    act.wait_ge(evicted, 2 * per * i + (n + 2))
                    nc.scalar.activation(split(slot(i, first + c)), ps[c % per][:, :, 0:HN], then).then_inc(evicted, 1)

            act.sem_inc(used, 2)
            move_high(0, 0, 0)
            move_high(0, 1, 1)
            over_runs(act, step, peel=True)

        @block.gpsimd
        def _(pool):
            pool.sem_inc(low, 2 * per)

            def move_low(i, n, c, *_):
                pool.wait_ge(high, 2 * per * i + (n + 1))
                nc.gpsimd.tensor_tensor(wL[c % per][:, :, :], wb[c // per][:, :, c % per * P:(c % per + 1) * P], wH[c % per][:, :, :].bitcast(F32),
                                        ALU.subtract).then_inc(low, 1)
            over_runs(pool, move_low)

        @block.tensor
        def _(pe):
            pe.sem_inc(product, 2)

            def multiply(i, n, c, *_):
                pe.wait_ge(low, 2 * per * i + (n + 1 + 2 * per))
                pe.wait_ge(evicted, 2 * per * i + (n + 1))
                for h in range(2):
                    tok = slice(h * HN, (h + 1) * HN)
                    for k in range(KD):
                        for p, (a, b) in enumerate(((wH, XH), (wH, XL), (wL, XH))):
                            mm = nc.tensor.matmul(ps[c % per][:, h, 0:HN], a[c % per][:, k, :], b[:, k, tok],
                                                  start=(k == 0 and p == 0), stop=(k == KD - 1 and p == 2))
                mm.then_inc(product, 1)
            over_runs(pe, multiply)

        @block.vector
        def _(dve):
            V = nc.vector
            dve.sem_inc(evicted, 2)
            LINKS = 6

            def step(i, n, c, run, _):
                _, _, first, then = run
                if then is not None and not isinstance(then, tuple):
                    return
                x = slot(i, first + c)
                dve.wait_ge(product, 2 * per * i + (n + 1 + 2))
                V.tensor_copy(split(x), ps[c % per][:, :, 0:HN]).then_inc(evicted, 1)
                if then is None:
                    return
                raw, taps, stride, bias = then
                own_taps = columns[:, c % 2, :]
                chunk = bass.ds(2 * per * i + c, 1)
                V.tensor_copy(own_taps[:, 0:CONV].rearrange("p (j r) -> p j r", r=1),
                              S.vec[:, taps:taps + CONV * stride].rearrange("p (j r) -> p j r", j=CONV)[:, :, chunk]).then_inc(own, 1)
                V.tensor_copy(own_taps[:, CONV:CONV + 1], S.vec[:, bass.ds(2 * per * i + (bias + c), 1)]).then_inc(own, 1)
                yc = y[:, c % 2:c % 2 + 1, :]
                link = lambda k: dve.wait_ge(own, 2 * per * LINKS * i + (LINKS * n + k))
                link(2)
                dve.wait_ge(evicted, 2 * per * i + (n + 1 + 2))
                dve.wait_ge(used, 2 * per * i + (n + 1))
                V.tensor_scalar(yc, x[:, :, 0:T], own_taps[:, 3:4], own_taps[:, CONV:CONV + 1], ALU.mult, ALU.add).then_inc(own, 1)
                V.tensor_copy(S.raw[:, bass.ds(2 * per * i + (raw + c), 1), :], x[:, :, T - 3:N]).then_inc(own, 1)
                link(4)
                for j in (2, 1, 0):
                    d = 3 - j
                    tap = V.scalar_tensor_tensor(out=yc[:, :, d:T], in0=x[:, :, 0:T - d], scalar=own_taps[:, j:j + 1],
                                                 in1=yc[:, :, d:T], op0=ALU.mult, op1=ALU.add)
                    if j:
                        tap.then_inc(own, 1)
                        link(4 + d)
                    else:
                        tap.then_inc(convd, 1)
            over_runs(dve, step)


def bcast(ap, dim, n):
    return ap.unsqueeze(dim).to_broadcast(ap.shape[:dim] + (n,) + ap.shape[dim:])


class Modulation:

    COLS = 2

    def __init__(self, nc, A, S, name, ctx, first, n):
        self.nc, self.S, self.first, self.n, self.blocks = nc, S, first, n, n // self.COLS
        two = lambda make, n, shape: [ctx.enter_context(make(f"{n}{i}_{name}", shape, F32)) for i in range(2)]
        self.w = two(nc.sbuf_tensor, "w", [P, KD, self.COLS * P])
        self.rows = two(nc.sbuf_tensor, "rows", [9, self.COLS * P])
        self.row_bank = two(nc.psum_tensor, "row_bank", [P, 512])
        self.bank = ctx.enter_context(nc.psum_tensor(f"bank_{name}", [P, 512], F32))
        self.w_in = [ctx.sem(f"w_in{i}_{name}") for i in range(2)]
        self.product, self.moved, self.turned, self.modded = (ctx.sem(f"{n}_{name}") for n in ("product", "moved", "turned", "modded"))
        self.view = A["w_ada"][0].rearrange("(k p) n -> p k n", p=P)

    def load(self, sp):
        cols = self.COLS * P
        with sp.Fori(0, self.blocks // 2) as i:
            for j in range(2):
                sp.wait_ge(self.product, 2 * i + (j + 1))
                sp.dma_start(self.w[j][:, :, :], self.view[:, :, bass.ds(i * (2 * cols) + (self.first * P + j * cols), cols)]).then_inc(self.w_in[j], 16)

    def multiply(self, pe):
        pe.sem_inc(self.product, 2)
        with pe.Fori(0, self.blocks // 2) as i:
            for j in range(2):
                pe.wait_ge(self.w_in[j], 16 * i + 16)
                for k in range(KD):
                    mm = self.nc.tensor.matmul(self.row_bank[j][0:9, 0:self.COLS * P], self.S.silc[:, k, :], self.w[j][:, k, :],
                                               start=(k == 0), stop=(k == KD - 1))
                mm.then_inc(self.product, 1)
            for j in range(2):
                pe.wait_ge(self.moved, 2 * i + (j + 1))
                for m in range(self.COLS):
                    mm = self.nc.tensor.matmul(self.bank[:, bass.ds(i * (2 * self.COLS * 9) + (j * self.COLS + m) * 9, 9)],
                                               self.rows[j][:, m * P:(m + 1) * P], self.S.ident[0:9, 0:9], start=True, stop=True)
                mm.then_inc(self.turned, 1)

    def move(self, act):
        act.sem_inc(self.turned, 2)
        with act.Fori(0, self.blocks // 2) as i:
            for j in range(2):
                act.wait_ge(self.product, 2 * i + (j + 3))
                act.wait_ge(self.turned, 2 * i + (j + 1))
                self.nc.scalar.activation(self.rows[j][:, :], self.row_bank[j][0:9, 0:self.COLS * P], ACT.Copy).then_inc(self.moved, 1)

    def keep(self, dve):
        dve.wait_ge(self.turned, self.blocks + 2)
        at = slice(self.first, self.first + self.n)
        self.nc.vector.tensor_tensor(self.S.mod[:, at, :], self.bank[:, 0:9 * self.n].rearrange("p (c s) -> p c s", s=9),
                                     bcast(self.S.vec[:, V_BADA + self.first:V_BADA + self.first + self.n], 2, 9), ALU.add).then_inc(self.modded, 1)
        dve.wait_ge(self.modded, 1)


def modulation_phase(nc, A, S):
    with Phase(nc) as ctx:
        M = Modulation(nc, A, S, "ada", ctx, 0, 16)
        block = ctx.enter_context(nc.Block())

        @block.sync
        def _(sp):
            M.load(sp)

        @block.scalar
        def _(act):
            M.move(act)

        @block.tensor
        def _(pe):
            M.multiply(pe)

        @block.vector
        def _(dve):
            M.keep(dve)


def norm_phase(nc, name, S, X, n_chunks, finish, residual=None):
    with Phase(nc) as ctx:
        sq = ctx.enter_context(nc.sbuf_tensor(f"sq_{name}", [P, 2, N], F32))
        ps = ctx.enter_context(nc.psum_tensor(f"ps_{name}", [P, 2, 512], F32))
        t = ctx.enter_context(nc.sbuf_tensor(f"t_{name}", [P, KD, B], F32))
        squared, summed, scaled, rooted, fresh = (ctx.sem(f"{n}_{name}") for n in ("squared", "summed", "scaled", "rooted", "fresh"))
        act_own = ctx.sem(f"act_own_{name}")
        dve_own = ctx.sem(f"dve_own_{name}")
        block = ctx.enter_context(nc.Block())

        @block.scalar
        def _(act):
            for k in range(n_chunks):
                if k >= 2:
                    act.wait_ge(summed, k - 1)
                if residual:
                    act.wait_ge(fresh, k + 1)
                nc.scalar.activation(sq[:, k % 2, :], X(k), ACT.Square).then_inc(squared, 1)
            act.wait_ge(scaled, 1)
            own = Chain(act, act_own)
            own(nc.scalar.activation(S.rb[:, :], S.rb[:, :], ACT.Ln))
            nc.scalar.activation(S.rb[:, :], S.rb[:, :], ACT.Exp, scale=-0.5).then_inc(rooted, 1)

        @block.tensor
        def _(pe):
            for k in range(n_chunks):
                pe.wait_ge(squared, k + 1)
                for h in range(2):
                    mm = nc.tensor.matmul(ps[:, h, 0:HN], S.ones[:, :], sq[:, k % 2, h * HN:(h + 1) * HN],
                                          start=(k == 0), stop=(k == n_chunks - 1))
                mm.then_inc(summed, 1)

        @block.vector
        def _(dve):
            own = Chain(dve, dve_own)
            if residual:
                src, gate = residual
                own(nc.vector.tensor_tensor(t[:, :, :], src[:, :, T:N], S.mod[:, gate:gate + KD, 1:9], ALU.mult))
                own(nc.vector.tensor_tensor(S.xT[:, :, T:N], S.xT[:, :, T:N], t[:, :, :], ALU.add))
                for k in range(KD):
                    nc.vector.scalar_tensor_tensor(out=S.xT[:, k, 0:T], in0=src[:, k, 0:T], scalar=S.mod[:, gate + k, 0:1],
                                                   in1=S.xT[:, k, 0:T], op0=ALU.mult, op1=ALU.add).then_inc(fresh, 1)
            dve.wait_ge(summed, n_chunks)
            nc.vector.tensor_scalar(halves(S.rb[:, :]), ps[:, :, 0:HN], 1.0 / (n_chunks * P), EPS, ALU.mult, ALU.add).then_inc(scaled, 1)
            dve.wait_ge(rooted, 1)
            finish(dve, own)


def modulate(nc, S, dst, gain, shift, scale):
    def finish(dve, own):
        own(nc.vector.tensor_scalar(S.gs[:, :, :], S.mod[:, scale:scale + KD, :], 1.0, None, ALU.add))
        own(nc.vector.tensor_tensor(S.gs[:, :, :], S.gs[:, :, :], bcast(S.vec[:, gain:gain + KD], 2, 9), ALU.mult))
        for k in range(KD):
            nc.vector.scalar_tensor_tensor(out=dst[:, k, 0:T], in0=S.xT[:, k, 0:T], scalar=S.gs[:, k, 0:1],
                                           in1=S.rb[:, 0:T], op0=ALU.mult, op1=ALU.mult)
        own(nc.vector.tensor_tensor(dst[:, :, T:N], S.xT[:, :, T:N], bcast(S.rb[:, T:N], 1, KD), ALU.mult))
        for k in range(KD):
            nc.vector.tensor_scalar(dst[:, k, 0:T], dst[:, k, 0:T], S.mod[:, shift + k, 0:1], None, ALU.add)
        own(nc.vector.tensor_tensor(dst[:, :, T:N], dst[:, :, T:N], S.gs[:, :, 1:9], ALU.mult))
        own(nc.vector.tensor_tensor(dst[:, :, T:N], dst[:, :, T:N], S.mod[:, shift:shift + KD, 1:9], ALU.add))
    return finish


def gates_phase(nc, A, S, R, O):
    with Phase(nc) as ctx:
        sem = ctx.sem
        sb = lambda n, s: ctx.enter_context(nc.sbuf_tensor(n, s, F32))
        pt = ctx.enter_context(nc.psum_tensor("pt_gate", [P, 2, 512], F32))
        pb = ctx.enter_context(nc.psum_tensor("pb_gate", [P, 4, 512], F32))
        fg, ef, lf, ig = (sb(f"{n}_gate", [H_A, N]) for n in ("fg", "ef", "lf", "ig"))
        dx, du, de = (sb(f"{n}_gate", [H_B, N]) for n in ("dx", "du", "de"))
        bt = sb("bt_gate", [H_A, N])
        reset = sb("reset_gate", [H_B, T])
        zero = sb("zero_gate", [SPLIT, T])
        mc = sb("mc_gate", [H_A, NC + 1])
        va = sb("va_gate", [H_A, 28])
        vb = sb("vb_gate", [H_B, 21])
        xa = sb("xa_gate", [H_A, H_A, 28])
        xb = sb("xb_gate", [H_B, H_B, 21])
        pick = sb("pick_gate", [SPLIT, H_B, P])
        row = {n: sb(f"row_{n}", [H_A, N]) for n in ("inter", "w", "em")}
        rw = sb("row_ws", [H_B, T])
        re = sb("row_ec", [H_B, T])
        acted, zeroed, dve_own, act_own, pool_own = sem("acted"), sem("zeroed_gate"), sem("dve_own_gate"), sem("act_own_gate"), sem("pool_own_gate")
        rowed, columned, expanded, spread, out_done = sem("rowed"), sem("columned"), sem("expanded"), sem("spread"), sem("gate_out")
        block = ctx.enter_context(nc.Block())

        @block.gpsimd
        def _(pool):
            own = Chain(pool, pool_own)
            own(nc.gpsimd.memset(pick[:, :, :], 0.0))
            for at in (0, 32):
                own(nc.gpsimd.affine_select(out=pick[:, :, :], in_=pick[:, :, :], compare_op=ALU.not_equal, fill=1.0,
                                            base=-at, pattern=[[-1, H_B], [0, P]], channel_multiplier=1))
            own(nc.gpsimd.tensor_copy(S.pick[:, :, :], pick[:, :, :]))

        @block.tensor
        def _(pe):
            pe.wait_ge(acted, 2)
            for q, r in enumerate((R.a, row["inter"], row["w"], row["em"], R.cum, R.dt, rw, re)):
                n = H_A if q < 4 else H_B
                for c in range(NC):
                    at = (c * 8 + q) * 16
                    mm = nc.tensor.transpose(pt[:, 0, at:at + n], r[0:n, c * L:(c + 1) * L], S.ident[0:n, 0:n])
            mm.then_inc(columned, 1)
            pe.wait_ge(expanded, 1)
            nc.tensor.matmul(pb[:, 0, 0:224], S.ones[0:H_A, :], xa[:, :, :].rearrange("p a b -> p (a b)"), start=True, stop=True)
            nc.tensor.matmul(pb[:, 1, 0:336], S.ones[0:H_B, :], xb[:, :, :].rearrange("p a b -> p (a b)"), start=True, stop=True).then_inc(columned, 1)

        @block.scalar
        def _(act):
            own = Chain(act, act_own)
            nc.scalar.activation(ig[:, :], S.gate[0:H_A, :], ACT.Identity, bias=S.col[0:H_A, 0:1])
            nc.scalar.activation(fg[:, :], S.gate[32:32 + H_A, :], ACT.Identity, bias=S.col[0:H_A, 1:2])
            own(nc.scalar.activation(dx[:, :], S.gate[64:64 + H_B, :], ACT.Identity, bias=S.col[0:H_B, 2:3]))
            nc.scalar.activation(ef[:, :], fg[:, :], ACT.Abs)
            own(nc.scalar.activation(de[:, :], dx[:, :], ACT.Abs))
            nc.scalar.activation(ef[:, :], ef[:, :], ACT.Exp, scale=-1.0)
            nc.scalar.activation(S.ea[:, :], S.col[0:H_B, 3:4], ACT.Exp)
            own(nc.scalar.activation(de[:, :], de[:, :], ACT.Exp, scale=-1.0))
            nc.scalar.activation(ef[:, :], ef[:, :], ACT.Ln, bias=1.0)
            nc.scalar.activation(de[:, :], de[:, :], ACT.Ln, bias=1.0).then_inc(acted, 1)
            act.wait_ge(rowed, 2)
            for t in (row["inter"][:, :], row["w"][:, :], row["em"][:, :], rw[:, :], re[:, :], va[:, :], vb[:, 0:12]):
                last = nc.scalar.activation(t, t, ACT.Exp, scale=-1.0)
            last.then_inc(acted, 1)
            act.wait_ge(zeroed, 2)
            nc.scalar.activation(R.split_M[0:H_A, :], R.M[:, 0:T], ACT.Copy)
            nc.scalar.activation(R.split_cum[0:H_B, :], R.cum[:, 0:T], ACT.Copy).then_inc(acted, 1)

        @block.vector
        def _(dve):
            own = Chain(dve, dve_own)
            v = nc.vector
            v.memset(reset[:, :], 1.0)
            v.memset(zero[:, :], 0.0).then_inc(zeroed, 1)
            own(v.memset(mc[:, 0:1], 0.0))
            v.tensor_copy(R.split_M[:, :], zero[:, :])
            v.tensor_copy(R.split_cum[:, :], zero[:, :]).then_inc(zeroed, 1)
            own(v.memset(reset[:, :].rearrange("p (c l) -> p c l", c=NC)[:, :, 0:1], 0.0))
            dve.wait_ge(acted, 1)
            v.scalar_tensor_tensor(out=lf[:, :], in0=fg[:, :], scalar=0.0, in1=ef[:, :], op0=ALU.min, op1=ALU.subtract)
            own(v.scalar_tensor_tensor(out=R.dt[:, :], in0=dx[:, :], scalar=0.0, in1=de[:, :], op0=ALU.max, op1=ALU.add))
            own(v.tensor_scalar(du[:, :], R.dt[:, :], S.ea[:, 0:1], None, ALU.mult))
            v.tensor_tensor_scan(bt[:, 0:T], reset[0:H_A, :], lf[:, 0:T], 0.0, ALU.mult, ALU.add)
            v.tensor_copy(bt[:, T:N], lf[:, T:N])
            v.tensor_tensor_scan(R.cum[:, 0:T], reset[:, :], du[:, 0:T], 0.0, ALU.mult, ALU.add)
            own(v.tensor_copy(R.cum[:, T:N], du[:, T:N]))
            own(v.tensor_tensor(R.a[:, :], ig[:, :], bt[:, :], ALU.subtract))
            for c in range(NC):
                at = slice(c * L, (c + 1) * L)
                own(v.tensor_tensor_scan(R.M[:, at], R.a[:, at], R.a[:, at], mc[:, c:c + 1], ALU.max, ALU.max))
                own(v.tensor_tensor(mc[:, c + 1:c + 2], R.M[:, (c + 1) * L - 1:(c + 1) * L], bt[:, (c + 1) * L - 1:(c + 1) * L], ALU.add))
            own(v.tensor_tensor(R.M[:, T:N], R.a[:, T:N], S.m0T[:, :], ALU.max))
            for c in range(NC):
                at = slice(c * L, (c + 1) * L)
                last = slice((c + 1) * L - 1, (c + 1) * L)
                v.tensor_scalar(row["inter"][:, at], R.M[:, at], mc[:, c:c + 1], None, ALU.subtract)
                v.tensor_scalar(row["w"][:, at], R.a[:, at], R.M[:, last], -1.0, ALU.subtract, ALU.mult)
                v.tensor_tensor(va[:, c:c + 1], R.M[:, last], mc[:, c:c + 1], ALU.subtract)
                v.tensor_scalar(rw[:, at], R.cum[:, at], R.cum[:, last], -1.0, ALU.subtract, ALU.mult)
                v.tensor_copy(vb[:, c:c + 1], R.cum[:, last])
            v.tensor_tensor(row["inter"][:, T:N], R.M[:, T:N], S.m0T[:, :], ALU.subtract)
            v.tensor_tensor(row["w"][:, T:N], R.M[:, T:N], R.a[:, T:N], ALU.subtract)
            v.tensor_copy(re[:, :], R.cum[:, 0:T])
            own(v.tensor_tensor(row["em"][:, :], R.M[:, :], bt[:, :], ALU.add))
            v.tensor_copy(va[:, 4:12], row["inter"][:, T:N])
            v.tensor_copy(va[:, 12:20], row["w"][:, T:N])
            v.tensor_copy(va[:, 20:28], row["em"][:, T:N])
            v.tensor_copy(vb[:, 4:12], R.cum[:, T:N])
            v.tensor_copy(vb[:, 12:20], R.dt[:, T:N])
            v.tensor_copy(S.mS[:, :], row["em"][:, T:N])
            own(v.tensor_copy(vb[:, 20:21], S.col[0:H_B, 4:5]))
            v.tensor_copy(S.mP[:, :], mc[:, NC:NC + 1]).then_inc(rowed, 2)
            dve.wait_ge(acted, 2)
            v.tensor_tensor(xa[:, :, :], bcast(va[:, :], 1, H_A), bcast(S.ident[0:H_A, 0:H_A], 2, 28), ALU.mult)
            v.tensor_tensor(xb[:, :, :], bcast(vb[:, :], 1, H_B), bcast(S.ident[0:H_B, 0:H_B], 2, 21), ALU.mult).then_inc(expanded, 1)
            dve.wait_ge(acted, 3)
            v.tensor_tensor(R.split_M[32:32 + H_A, :], R.M[:, 0:T], R.split_M[0:H_A, :].bitcast(F32), ALU.subtract)
            v.tensor_tensor(R.split_cum[32:32 + H_B, :], R.cum[:, 0:T], R.split_cum[0:H_B, :].bitcast(F32), ALU.subtract)
            dve.wait_ge(columned, 1)
            v.tensor_copy(S.cols[:, :, 0:4, 0:8], pt[:, 0, :].rearrange("p (c q n) -> p c q n", c=NC, q=8)[:, :, 0:4, 0:8])
            v.tensor_copy(S.cols[:, :, 4:8, :], pt[:, 0, :].rearrange("p (c q n) -> p c q n", c=NC, q=8)[:, :, 4:8, :])
            dve.wait_ge(columned, 2)
            v.tensor_copy(S.ba[:, :, :].rearrange("p a b -> p (a b)"), pb[:, 0, 0:224])
            v.tensor_copy(S.bb[:, :, :].rearrange("p a b -> p (a b)"), pb[:, 1, 0:336]).then_inc(spread, 1)

        @block.sync
        def _(sp):
            sp.wait_ge(rowed, 2)
            sp.dma_start(O["p_m"][0, 0].rearrange("(h a) -> h a", a=1), S.mP[:, :]).then_inc(out_done, 16)
            sp.dma_start(O["s_m"][0].rearrange("b h -> h b"), S.mS[:, :], allow_slow_non_contiguous=True).then_inc(out_done, 16)
            sp.wait_ge(out_done, 32)


def conv_phase(nc, A, S, O):
    with Phase(nc) as ctx:
        M = Modulation(nc, A, S, "ada2", ctx, 16, 32)
        sem = ctx.sem
        sb = lambda n, s: ctx.enter_context(nc.sbuf_tensor(n, s, F32))
        ys = sb("ys_conv", [P, 28, B])
        ts = sb("ts_conv", [P, 28, B])
        tail = sb("tail_conv", [32, 28 * P])
        ps = [ctx.enter_context(nc.psum_tensor(f"ps_conv{i}", [P, 512], F32)) for i in range(5)]
        dve_own, tailed, rowed, out_done, samples = (sem(n) for n in ("dve_own_conv", "tail_turned", "tail_moved", "conv_out", "samples_convd"))
        block = ctx.enter_context(nc.Block())

        @block.scalar
        def _(act):
            M.move(act)
            act.wait_ge(samples, 1)
            nc.scalar.activation(S.proj[:, 0:16, T:N], ys[:, 0:16, :], ACT.Silu)
            nc.scalar.activation(S.proj[:, NX:NX + 12, T:N], ys[:, 16:28, :], ACT.Silu).then_inc(samples, 1)

        @block.vector
        def _(dve):
            own = Chain(dve, dve_own)
            v = nc.vector
            for lo, n, w, b, buf in ((0, 16, V_CAW, V_CAB, S.cbufa), (16, 12, V_CBW, V_CBB, S.cbufb)):
                o = ys[:, lo:lo + n, :]
                t = ts[:, lo:lo + n, :]
                bv = buf[:, :].rearrange("p (b j r) -> p j r b", b=B, j=3)
                own(v.tensor_tensor(o, S.raw[:, lo:lo + n, 3:11], bcast(S.vec[:, w + 3 * n:w + 4 * n], 2, B), ALU.mult))
                own(v.tensor_tensor(o, o, bcast(S.vec[:, b:b + n], 2, B), ALU.add))
                for j in range(3):
                    own(v.tensor_tensor(t, bv[:, j], bcast(S.vec[:, w + j * n:w + (j + 1) * n], 2, B), ALU.mult))
                    own(v.tensor_tensor(o, o, t, ALU.add))
            dve.sem_inc(samples, 1)
            for i in range(7):
                dve.wait_ge(tailed, i + 1)
                v.tensor_copy(tail[0:11, i * 512:(i + 1) * 512], ps[i % 5][0:11, :]).then_inc(rowed, 1)
            v.tensor_scalar(S.proj[:, NK:NK + 8, 0:T], S.proj[:, NK:NK + 8, 0:T], KSCALE, None, ALU.mult)
            dve.wait_ge(samples, 2)
            v.tensor_scalar(S.proj[:, NK:NK + 8, T:N], S.proj[:, NK:NK + 8, T:N], KSCALE, None, ALU.mult)
            M.keep(dve)

        @block.tensor
        def _(pe):
            for i in range(28):
                if i in (20, 24):
                    pe.wait_ge(rowed, i // 4 - 4)
                mm = nc.tensor.transpose(ps[i // 4 % 5][0:11, i % 4 * P:i % 4 * P + P], S.raw[:, i, :], S.ident[:, :])
                if i % 4 == 3:
                    mm.then_inc(tailed, 1)
            M.multiply(pe)

        @block.sync
        def _(sp):
            for key, src in (("conva", A["state_mlstm_conv"]), ("convb", A["state_ssm_conv"])):
                sp.dma_start(O["s_" + key][0, :, 0:2, :], src[0, :, 1:3, :]).then_inc(out_done, 16)
            M.load(sp)
            sp.wait_ge(rowed, 7)
            for key, cols, at in (("conva", 2048, 0), ("convb", 1536, 2048)):
                sp.dma_start(O["p_" + key][0, 0], tail[0:3, at:at + cols]).then_inc(out_done, 16)
                sp.dma_start(O["s_" + key][0, :, 2, :], tail[3:11, at:at + cols]).then_inc(out_done, 16)
            sp.wait_ge(out_done, 16 * 6)


def mlstm_phase(nc, S, R, O):
    with Phase(nc) as ctx:
        sem = ctx.sem
        sb = lambda n, s: ctx.enter_context(nc.sbuf_tensor(n, s, F32))
        V1 = P + 1
        num = sb("num_ml", [P, NC, H_A, V1])
        va = [sb(f"vaug{i}", [P, NC, V1]) for i in range(2)]
        kw = [sb(f"kw{i}", [P, NC, P]) for i in range(2)]
        X = [sb(f"x_ml{i}", [P, NC, L]) for i in range(2)]
        E = [sb(f"e_ml{i}", [P, NC, L]) for i in range(2)]
        C = sb("c_ml", [P, H_A, V1])
        ti = [sb(f"ti_ml{i}", [P, V1]) for i in range(2)]
        sq = sb("sq_ml", [P, H_A, P])
        den, r, mean, var = (sb(f"{n}_ml", [P, NC, H_A]) for n in ("den", "r", "mean", "var"))
        bank = lambda n: ctx.enter_context(nc.psum_tensor(n, [P, 512], F32))
        qk, mb, st = ([bank(f"{n}{i}_ml") for i in range(2)] for n in ("qk", "mb", "st"))
        trk, trv = bank("trk_ml"), bank("trv_ml")
        scored, turned, kv_ready, exps, xs, weighed, stepped, scaled_i, c_ready, num_ready = (
            sem(n + "_ml") for n in ("scored", "turned", "kv_ready", "exps", "xs", "weighed", "stepped", "scaled_i", "c_ready", "num_ready"))
        ones_set, squared, centred, var_ready, rooted, normed, hturned, hmoved, dve_own, act_own, n_out, o_done = (
            sem(n + "_ml") for n in ("ones_set", "squared", "centred", "var_ready", "rooted", "normed", "hturned", "hmoved", "dve_own", "act_own", "n_out", "out_done"))
        block = ctx.enter_context(nc.Block())
        q, k, v = (lambda h, c, s=s: S.proj[:, s + h, c * L:(c + 1) * L] for s in (NQ, NK, NV))
        col = lambda c, quantity, h: S.cols[:, c, quantity, h:h + 1]

        @block.tensor
        def _(pe):
            def prepare(h, part):
                if part == 0 and h >= 2:
                    pe.wait_ge(weighed, h - 1)
                if part < 2:
                    for c in (2 * part, 2 * part + 1):
                        nc.tensor.matmul(qk[h % 2][:, c * L:(c + 1) * L], k(h, c), q(h, c), start=True, stop=True)
                    if part == 1:
                        nc.tensor.matmul(mb[h % 2][:, :], S.pick[:, h, :], R.split_M[:, :], start=True, stop=True).then_inc(scored, 1)
                    return
                if part == 2 and h >= 1:
                    pe.wait_ge(kv_ready, h)
                for c in range(NC):
                    src, to = (k, trk) if part == 2 else (v, trv)
                    mm = nc.tensor.transpose(to[:, c * L:(c + 1) * L], src(h, c), S.ident[:, :])
                if part == 3:
                    mm.then_inc(turned, 1)

            def step(h, c):
                n = NC * h + c
                if n >= 2:
                    pe.wait_ge(num_ready, n - 1)
                nc.tensor.matmul(st[n % 2][:, 0:V1], X[h % 2][:, c, :], va[h % 2][:, c, :], start=True, stop=True)
                if c:
                    pe.wait_ge(c_ready, n)
                    nc.tensor.matmul(st[n % 2][:, 130:130 + V1], q(h, c), C[:, h, :], start=True, stop=True)
                nc.tensor.matmul(st[n % 2][:, 260:260 + V1], kw[h % 2][:, c, :], va[h % 2][:, c, :], start=True, stop=True).then_inc(stepped, 1)

            for h in range(2):
                for part in range(4):
                    prepare(h, part)
            for h in range(H_A):
                pe.wait_ge(weighed, h + 1)
                pe.wait_ge(kv_ready, h + 1)
                for c in range(NC):
                    step(h, c)
                    if h + 2 < H_A:
                        prepare(h + 2, c)
            pe.wait_ge(c_ready, NC * H_A)
            nc.tensor.transpose(mb[0][0:H_A, 0:P], C[:, :, P], S.ident[:, :]).then_inc(n_out, 1)
            pe.wait_ge(normed, 1)
            for h in range(H_A):
                if h >= 2:
                    pe.wait_ge(hmoved, h - 1)
                for c in range(NC):
                    mm = nc.tensor.transpose(qk[h % 2][:, c * L:(c + 1) * L], num[:, c, h, 0:P], S.ident[:, :])
                mm.then_inc(hturned, 1)

        @block.scalar
        def _(act):
            def keys_values(h):
                act.wait_ge(turned, h + 1)
                if h >= 2:
                    act.wait_ge(stepped, NC * (h - 1))
                nc.scalar.activation(va[h % 2][:, :, 0:P], trv[:, :].rearrange("p (c l) -> p c l", c=NC), ACT.Copy)
                for c in range(NC):
                    last = nc.scalar.activation(kw[h % 2][:, c, :], trk[:, c * L:(c + 1) * L], ACT.Copy, scale=col(c, 2, h))
                last.then_inc(kv_ready, 1)

            def exponentials(h):
                act.wait_ge(xs, h + 1)
                nc.scalar.activation(E[h % 2][:, :, :], X[h % 2][:, :, :], ACT.Exp, scale=-1.0).then_inc(exps, 1)

            act.wait_ge(ones_set, 1)
            keys_values(0)
            exponentials(0)
            for h in range(H_A):
                if h + 1 < H_A:
                    keys_values(h + 1)
                for c in range(1, NC):
                    n = NC * h + c
                    act.wait_ge(stepped, n + 1)
                    if n >= 2:
                        act.wait_ge(num_ready, n - 1)
                    nc.scalar.activation(ti[n % 2][:, :], st[n % 2][:, 130:130 + V1], ACT.Copy, scale=col(c, 1, h)).then_inc(scaled_i, 1)
                    if c == 1 and h + 1 < H_A:
                        exponentials(h + 1)
            for c in range(NC):
                act.wait_ge(centred, c + 1)
                if c:
                    act.wait_ge(var_ready, c)
                nc.scalar.activation(sq[:, :, :], num[:, c, :, 0:P], ACT.Square).then_inc(squared, 1)
            act.wait_ge(var_ready, NC + 1)
            own = Chain(act, act_own)
            own(nc.scalar.activation(var[:, :, :], var[:, :, :], ACT.Ln))
            nc.scalar.activation(var[:, :, :], var[:, :, :], ACT.Exp, scale=-0.5).then_inc(rooted, 1)

        @block.vector
        def _(dve):
            own = Chain(dve, dve_own)
            V = nc.vector
            for i in range(2):
                last = V.memset(va[i][:, :, P:V1], 1.0)
            last.then_inc(ones_set, 1)

            def exponents(h):
                dve.wait_ge(scored, h + 1)
                if h >= 2:
                    dve.wait_ge(stepped, NC * (h - 1))
                for c in range(NC):
                    last = V.scalar_tensor_tensor(out=X[h % 2][:, c, :], in0=mb[h % 2][:, c * L:(c + 1) * L], scalar=col(c, 0, h),
                                                  in1=S.far[:, :], op0=ALU.subtract, op1=ALU.max)
                last.then_inc(xs, 1)

            def weigh(h):
                dve.wait_ge(exps, h + 1)
                V.tensor_tensor(X[h % 2][:, :, :], E[h % 2][:, :, :], qk[h % 2][:, :].rearrange("p (c l) -> p c l", c=NC), ALU.mult).then_inc(weighed, 1)

            exponents(0)
            weigh(0)
            for h in range(H_A):
                for c in range(NC):
                    n = NC * h + c
                    dve.wait_ge(stepped, n + 1)
                    if c:
                        dve.wait_ge(scaled_i, 3 * h + c)
                        V.scalar_tensor_tensor(out=C[:, h, :], in0=C[:, h, :], scalar=S.ba[:, h, c:c + 1],
                                               in1=st[n % 2][:, 260:260 + V1], op0=ALU.mult, op1=ALU.add).then_inc(c_ready, 1)
                        V.tensor_tensor(num[:, c, h, :], ti[n % 2][:, :], st[n % 2][:, 0:V1], ALU.add).then_inc(num_ready, 1)
                    else:
                        V.tensor_copy(C[:, h, :], st[n % 2][:, 260:260 + V1]).then_inc(c_ready, 1)
                        V.tensor_copy(num[:, c, h, :], st[n % 2][:, 0:V1]).then_inc(num_ready, 1)
                    if h + 1 < H_A and c == 0:
                        exponents(h + 1)
                    if h + 1 < H_A and c == 2:
                        weigh(h + 1)
            dve.wait_ge(n_out, 1)
            V.tensor_copy(S.nrow[:, :], mb[0][0:H_A, 0:P]).then_inc(n_out, 1)
            dve.wait_ge(num_ready, NC * H_A)
            own(V.scalar_tensor_tensor(out=den[:, :, :], in0=num[:, :, :, P], scalar=-1.0, in1=num[:, :, :, P], op0=ALU.mult, op1=ALU.max))
            own(V.tensor_tensor(den[:, :, :], den[:, :, :], S.cols[:, :, 3, 0:H_A], ALU.max))
            own(V.reciprocal(r[:, :, :], den[:, :, :]))
            for c in range(NC):
                h_c = num[:, c, :, 0:P]
                own(V.tensor_tensor(h_c, h_c, bcast(r[:, c, :], 2, P), ALU.mult))
                own(V.reduce_sum(mean[:, c, :], h_c, AX_X))
                own(V.tensor_scalar(mean[:, c, :], mean[:, c, :], 1.0 / P, None, ALU.mult))
                V.tensor_tensor(h_c, h_c, bcast(mean[:, c, :], 2, P), ALU.subtract).then_inc(centred, 1)
                dve.wait_ge(squared, c + 1)
                V.reduce_sum(var[:, c, :], sq[:, :, :], AX_X).then_inc(var_ready, 1)
            dve.wait_ge(var_ready, NC)
            V.tensor_scalar(var[:, :, :], var[:, :, :], 1.0 / P, EPS, ALU.mult, ALU.add).then_inc(var_ready, 1)
            dve.wait_ge(rooted, 1)
            for c in range(NC):
                last = V.tensor_tensor(num[:, c, :, 0:P], num[:, c, :, 0:P], bcast(var[:, c, :], 2, P), ALU.mult)
            last.then_inc(normed, 1)
            for h in range(H_A):
                dve.wait_ge(hturned, h + 1)
                V.scalar_tensor_tensor(out=S.proj[:, NQ + h, 0:T], in0=qk[h % 2][:, :], scalar=S.vec[:, V_GA + h:V_GA + h + 1],
                                       in1=S.proj[:, NO + h, 0:T], op0=ALU.mult, op1=ALU.mult).then_inc(hmoved, 1)

        @block.sync
        def _(sp):
            sp.wait_ge(c_ready, NC * H_A)
            sp.dma_start(O["p_c"][0, 0].rearrange("h d v -> d h v"), C[:, :, 0:P]).then_inc(o_done, 16)
            sp.wait_ge(n_out, 2)
            sp.dma_start(O["p_n"][0, 0], S.nrow[:, :]).then_inc(o_done, 16)
            sp.wait_ge(o_done, 32)


def ssd_phase(nc, S, R, O):
    with Phase(nc) as ctx:
        sem = ctx.sem
        sb = lambda n, s: ctx.enter_context(nc.sbuf_tensor(n, s, F32))
        HG = H_B // G_B
        BC = sb("bc_ssd", [P, NC, L])
        Bt = sb("bt_ssd", [P, NC, P])
        xdt, xw, Y = (sb(f"{n}_ssd", [P, NC, HG, P_B]) for n in ("xdt", "xw", "y"))
        ST = sb("st_ssd", [P, HG, P_B])
        tmp = sb("tmp_ssd", [P, HG, P_B])
        X = [sb(f"x_ssd{i}", [P, NC, L]) for i in range(2)]
        E = [sb(f"e_ssd{i}", [P, NC, L]) for i in range(2)]
        so = sb("so_ssd", [P, 4, P])
        bank = lambda n: ctx.enter_context(nc.psum_tensor(n, [P, 512], F32))
        a, cb, py = ([bank(f"{n}{i}_ssd") for i in range(2)] for n in ("a", "cb", "py"))
        pi, pu = bank("pi_ssd"), bank("pu_ssd")
        names = ("bc_in", "bc_out", "x_in", "x_out", "spread", "xs", "exps", "weighed", "y_in", "y_out", "inter_in", "state", "inter_out",
                 "t_in", "t_out", "so_in", "so_ready", "o_done", "dve_own")
        m = {n: sem(n + "_ssd") for n in names}
        block = ctx.enter_context(nc.Block())
        tok = lambda slot, c: S.proj[:, slot, c * L:(c + 1) * L]
        col = lambda c, quantity, h: S.cols[:, c, quantity, h:h + 1]

        @block.tensor
        def _(pe):
            for g in range(G_B):
                if g:
                    pe.wait_ge(m["t_out"], 4)
                    pe.wait_ge(m["so_ready"], 1)
                for c in range(NC):
                    nc.tensor.matmul(a[0][:, c * L:(c + 1) * L], tok(NX + 8 + g, c), tok(NX + 10 + g, c), start=True, stop=True)
                    mm = nc.tensor.transpose(a[1][:, c * L:(c + 1) * L], tok(NX + 8 + g, c), S.ident[:, :])
                mm.then_inc(m["bc_in"], 1)
                for c in range(NC):
                    if c >= 2:
                        pe.wait_ge(m["x_out"], NC * g + c - 1)
                    for f in range(4):
                        mm = nc.tensor.transpose(py[c % 2][:, f * P:(f + 1) * P], tok(NX + 4 * g + f, c), S.ident[:, :])
                    mm.then_inc(m["x_in"], 1)

                def spread(h):
                    n = HG * g + h
                    if n >= 2:
                        pe.wait_ge(m["xs"], n - 1)
                    nc.tensor.matmul(cb[n % 2][:, :], S.pick[:, n, :], R.split_cum[:, :], start=True, stop=True).then_inc(m["spread"], 1)

                spread(0)
                spread(1)
                for h in range(HG):
                    n = HG * g + h
                    if h + 2 < HG:
                        spread(h + 2)
                    pe.wait_ge(m["weighed"], n + 1)
                    pe.wait_ge(m["x_out"], NC * (g + 1))
                    if h >= 2:
                        pe.wait_ge(m["y_out"], n - 1)
                    for c in range(NC):
                        mm = nc.tensor.matmul(py[n % 2][:, c * P_B:(c + 1) * P_B], E[n % 2][:, c, :], xdt[:, c, h, :], start=True, stop=True)
                    mm.then_inc(m["y_in"], 1)
                for c in range(NC):
                    n = NC * g + c
                    if n:
                        pe.wait_ge(m["state"], n)
                        pe.wait_ge(m["inter_out"], n)
                    if c:
                        nc.tensor.matmul(pi[:, :], tok(NX + 10 + g, c), ST[:, :, :].rearrange("p h d -> p (h d)"), start=True, stop=True)
                    nc.tensor.matmul(pu[:, :], Bt[:, c, :], xw[:, c, :, :].rearrange("p h d -> p (h d)"), start=True, stop=True).then_inc(m["inter_in"], 1)
                pe.wait_ge(m["inter_out"], NC * (g + 1))
                pe.wait_ge(m["state"], NC * (g + 1))
                pe.wait_ge(m["y_out"], HG * (g + 1))
                for f in range(4):
                    if f >= 2:
                        pe.wait_ge(m["t_out"], 4 * g + f - 1)
                    for c in range(NC):
                        mm = nc.tensor.transpose(a[f % 2][:, c * L:(c + 1) * L], Y[:, c, 2 * f:2 * f + 2, :].rearrange("p h d -> p (h d)"), S.ident[:, :])
                    mm.then_inc(m["t_in"], 1)
                for f in range(4):
                    mm = nc.tensor.transpose(pi[:, f * P:(f + 1) * P], ST[:, 2 * f:2 * f + 2, :].rearrange("p h d -> p (h d)"), S.ident[:, :])
                mm.then_inc(m["so_in"], 1)

        @block.scalar
        def _(act):
            for g in range(G_B):
                act.wait_ge(m["bc_in"], g + 1)
                nc.scalar.activation(BC[:, :, :], a[0][:, :].rearrange("p (c l) -> p c l", c=NC), ACT.Copy)
                nc.scalar.activation(Bt[:, :, :], a[1][:, :].rearrange("p (c l) -> p c l", c=NC), ACT.Copy).then_inc(m["bc_out"], 1)
                for h in range(HG):
                    n = HG * g + h
                    act.wait_ge(m["xs"], n + 1)
                    nc.scalar.activation(X[n % 2][:, :, :], X[n % 2][:, :, :], ACT.Exp, scale=-1.0).then_inc(m["exps"], 1)

        @block.vector
        def _(dve):
            own = Chain(dve, m["dve_own"])
            V = nc.vector
            for g in range(G_B):
                hs = slice(HG * g, HG * (g + 1))
                for c in range(NC):
                    dve.wait_ge(m["x_in"], NC * g + c + 1)
                    px = py[c % 2][:, :].rearrange("p (h d) -> p h d", h=HG)
                    own(V.tensor_tensor(xdt[:, c], px, bcast(S.cols[:, c, 5, hs], 2, P_B), ALU.mult))
                    V.tensor_tensor(xw[:, c], xdt[:, c], bcast(S.cols[:, c, 6, hs], 2, P_B), ALU.mult)
                    V.tensor_tensor(Y[:, c], px, bcast(S.bb[:, hs, 20], 2, P_B), ALU.mult).then_inc(m["x_out"], 1)
                dve.wait_ge(m["x_out"], NC * (g + 1))

                def exponents(h):
                    n = HG * g + h
                    dve.wait_ge(m["spread"], n + 1)
                    if n >= 2:
                        dve.wait_ge(m["weighed"], n - 1)
                    for c in range(NC):
                        last = V.scalar_tensor_tensor(out=X[n % 2][:, c, :], in0=cb[n % 2][:, c * L:(c + 1) * L], scalar=col(c, 4, n),
                                                      in1=S.far[:, :], op0=ALU.subtract, op1=ALU.max)
                    last.then_inc(m["xs"], 1)

                def weigh(h):
                    n = HG * g + h
                    dve.wait_ge(m["exps"], n + 1)
                    dve.wait_ge(m["bc_out"], g + 1)
                    if n >= 2:
                        dve.wait_ge(m["y_in"], n - 1)
                    V.tensor_tensor(E[n % 2][:, :, :], X[n % 2][:, :, :], BC[:, :, :], ALU.mult).then_inc(m["weighed"], 1)

                exponents(0)
                exponents(1)
                weigh(0)
                for h in range(HG):
                    n = HG * g + h
                    if h + 2 < HG:
                        exponents(h + 2)
                    if h + 1 < HG:
                        weigh(h + 1)
                    dve.wait_ge(m["y_in"], n + 1)
                    V.tensor_tensor(Y[:, :, h, :], Y[:, :, h, :], py[n % 2][:, 0:NC * P_B].rearrange("p (c d) -> p c d", c=NC), ALU.add).then_inc(m["y_out"], 1)
                for c in range(NC):
                    n = NC * g + c
                    dve.wait_ge(m["inter_in"], n + 1)
                    pu_v = pu[:, :].rearrange("p (h d) -> p h d", h=HG)
                    if c == 0:
                        V.tensor_copy(ST[:, :, :], pu_v).then_inc(m["state"], 1)
                        dve.sem_inc(m["inter_out"], 1)
                        continue
                    own(V.tensor_tensor(ST[:, :, :], ST[:, :, :], bcast(S.bb[:, hs, c], 2, P_B), ALU.mult))
                    V.tensor_tensor(ST[:, :, :], ST[:, :, :], pu_v, ALU.add).then_inc(m["state"], 1)
                    own(V.tensor_tensor(tmp[:, :, :], pi[:, :].rearrange("p (h d) -> p h d", h=HG), bcast(S.cols[:, c, 7, hs], 2, P_B), ALU.mult))
                    V.tensor_tensor(Y[:, c], Y[:, c], tmp[:, :, :], ALU.add).then_inc(m["inter_out"], 1)
                for f in range(4):
                    dve.wait_ge(m["t_in"], 4 * g + f + 1)
                    z = S.proj[:, NZ + 4 * g + f, 0:T]
                    V.tensor_tensor(z, a[f % 2][:, :], z, ALU.mult).then_inc(m["t_out"], 1)
                dve.wait_ge(m["so_in"], g + 1)
                if g:
                    dve.wait_ge(m["o_done"], 16 * g)
                V.tensor_copy(so[:, :, :], pi[:, :].rearrange("p (f n) -> p f n", f=4)).then_inc(m["so_ready"], 1)

        @block.sync
        def _(sp):
            for g in range(G_B):
                sp.wait_ge(m["so_ready"], g + 1)
                sp.dma_start(O["p_ssm"][0, 0, HG * g:HG * (g + 1)].rearrange("(f a) p n -> (a p) f n", a=2), so[:, :, :]).then_inc(m["o_done"], 16)
            sp.wait_ge(m["o_done"], 16 * G_B)


def sample_phase(nc, A, S, O):
    SQ, BUFS = 2, 4
    NU = B // SQ
    with Phase(nc) as ctx:
        sem = ctx.sem
        sb = lambda n, s: ctx.enter_context(nc.sbuf_tensor(n, s, F32))
        st = [sb(f"state{i}", [P, SQ, 8, P]) for i in range(BUFS)]
        vrow = ctx.enter_context(nc.sbuf_tensor("vrow", [SPLIT, D], F32R))
        brow = ctx.enter_context(nc.sbuf_tensor("brow", [SPLIT, 512], F32R))
        wk, qn, nd, hh, t1, t2 = (sb(f"{n}_sm", [P, B, H_A]) for n in ("wk", "qn", "nd", "hh", "t1", "t2"))
        dec, dt, yv, xd = (sb(f"{n}_sm", [P, KD, B]) for n in ("dec", "dt", "yv", "xd"))
        dsk = sb("dsk_sm", [P, KD])
        junk = sb("junk_sm", [P, KD, P])
        zero = junk[0:SPLIT, :, :].rearrange("p a b -> p (a b)")
        nrow = sb("nrow_sm", [64, P])
        pr = ctx.enter_context(nc.psum_tensor("pr_sm", [P, 2, 512], F32))
        pv = [ctx.enter_context(nc.psum_tensor(f"pv{i}_sm", [P, 2, 512], F32)) for i in range(2)]
        ph = ctx.enter_context(nc.psum_tensor("ph_sm", [P, 512], F32))
        pm = ctx.enter_context(nc.psum_tensor("pm_sm", [P, 512], F32))
        m = {n: sem(n + "_sm") for n in ("zeroed", "highs", "gathered", "decayed", "in0", "in1", "in2", "in3", "turned", "rows", "spread", "updated", "read", "unit", "qn_in", "den_in", "num_in",
                                         "mean_in", "meant", "sq_in", "var_in", "var_out", "rooted", "n_in", "n_out", "o_done0", "o_done1", "o_done2", "o_done3", "o_done", "dve_own", "act_own")}
        block = ctx.enter_context(nc.Block())
        cv = A["state_mlstm_c"][0].rearrange("b h d v -> d b h v")
        sv = A["state_ssm"][0].rearrange("b (c a) p n -> (a p) b c n", a=2)
        oc = O["s_c"][0].rearrange("b h d v -> d b h v")
        os_ = O["s_ssm"][0].rearrange("b (c a) p n -> (a p) b c n", a=2)
        units = [(a, b, SQ * u) for a, b in ((cv, oc), (sv, os_)) for u in range(NU)]

        @block.sync
        def _(sp):
            for u, (src, _, b0) in enumerate(units):
                i = u % BUFS
                if u >= BUFS:
                    sp.wait_ge(m[f"o_done{i}"], 16 * SQ)
                for b in range(SQ):
                    sp.dma_start(st[i][:, b], src[:, b0 + b]).then_inc(m[f"in{i}"], 16)
            sp.wait_ge(m["n_out"], 1)
            sp.dma_start(O["s_n"][0].rearrange("b h d -> (b h) d"), nrow[:, :]).then_inc(m["o_done"], 16)
            sp.wait_ge(m["o_done"], 16)
            for i in range(BUFS):
                sp.wait_ge(m[f"o_done{i}"], 2 * 16 * SQ)

        @block.gpsimd
        def _(pool):
            for u in range(2 * NU):
                pool.wait_ge(m[f"in{u % BUFS}"], 16 * SQ * (u // BUFS + 1))
                if u == NU:
                    pool.wait_ge(m["gathered"], 1)
                for b in range(SQ):
                    s = SQ * (u % NU) + b
                    decay = S.ba[:, :, 4 + s] if u < NU else dec[:, :, s]
                    last = nc.gpsimd.tensor_tensor(st[u % BUFS][:, b], st[u % BUFS][:, b], bcast(decay, 2, P), ALU.mult)
                last.then_inc(m["decayed"], 1)

        def store(act, u):
            act.wait_ge(m["unit"], u + 1)
            for b in range(SQ):
                act.dma_start(units[u][1][:, units[u][2] + b], st[u % BUFS][:, b]).then_inc(m[f"o_done{u % BUFS}"], 16)

        @block.tensor
        def _(pe):
            for k in range(KD):
                nc.tensor.transpose(pr[0:B, k // 4, k % 4 * P:k % 4 * P + P], S.proj[:, NV + k, T:N], S.ident[:, :])
            for k in range(4):
                mm = nc.tensor.transpose(ph[0:B, k * P:(k + 1) * P], S.proj[:, NX + 8 + k, T:N], S.ident[:, :])
            mm.then_inc(m["turned"], 1)
            pe.wait_ge(m["rows"], 1)

            def spread(s):
                b = s % B
                if s >= 2:
                    pe.wait_ge(m["read"], s - 1)
                if s < B:
                    for j in range(2):
                        mm = nc.tensor.matmul(pv[s % 2][:, j, :], S.pick[:, b, :], vrow[:, j * 512:(j + 1) * 512], start=True, stop=True)
                else:
                    mm = nc.tensor.matmul(pv[s % 2][:, 0, :], S.pick[:, b, :], brow[:, :], start=True, stop=True)
                mm.then_inc(m["spread"], 1)

            for b in range(SQ):
                spread(b)
            for u in range(NU):
                for b in range(SQ * (u + 1), SQ * (u + 2)):
                    spread(b)
                pe.wait_ge(m["unit"], u + 1)
                for b in range(SQ * u, SQ * (u + 1)):
                    for h in range(H_A):
                        mm = nc.tensor.matmul(pm[:, b * H_A + h:b * H_A + h + 1], st[u][:, b % SQ, h, :], S.proj[:, NQ + h, T + b:T + b + 1],
                                              start=True, stop=True)
                mm.then_inc(m["num_in"], 1)
            pe.wait_ge(m["qn_in"], 1)
            nc.tensor.matmul(pm[:, 64:128], S.ones[:, :], qn[:, :, :].rearrange("p b h -> p (b h)"), start=True, stop=True).then_inc(m["den_in"], 1)
            nc.tensor.transpose(pr[0:64, 0, 0:P], S.n0[:, :], S.ident[:, :]).then_inc(m["n_in"], 1)
            pe.wait_ge(m["mean_in"], 1)
            nc.tensor.matmul(pm[:, 128:192], S.ones[:, :], hh[:, :, :].rearrange("p b h -> p (b h)"), start=True, stop=True).then_inc(m["meant"], 1)
            pe.wait_ge(m["sq_in"], 1)
            nc.tensor.matmul(pm[:, 192:256], S.ones[:, :], t1[:, :, :].rearrange("p b h -> p (b h)"), start=True, stop=True).then_inc(m["var_in"], 1)
            for s in range(B + SQ, 2 * B):
                spread(s)

        @block.scalar
        def _(act):
            own = Chain(act, m["act_own"])
            act.wait_ge(m["zeroed"], 2)
            act.wait_ge(m["turned"], 1)
            nc.scalar.activation(vrow[0:B, :].rearrange("p (a n) -> p a n", a=2), pr[0:B, :, :], ACT.Copy)
            nc.scalar.activation(brow[0:B, :], ph[0:B, :], ACT.Copy).then_inc(m["highs"], 1)
            for u in range(NU):
                if u < BUFS:
                    act.wait_ge(m["num_in"], u + 1)
                store(act, u)
            act.wait_ge(m["var_out"], 1)
            own(nc.scalar.activation(t2[:, :, :], t2[:, :, :], ACT.Ln))
            nc.scalar.activation(t2[:, :, :], t2[:, :, :], ACT.Exp, scale=-0.5).then_inc(m["rooted"], 1)
            for u in range(NU, 2 * NU):
                store(act, u)

        @block.vector
        def _(dve):
            own = Chain(dve, m["dve_own"])
            V = nc.vector
            V.memset(zero[:, :], 0.0).then_inc(m["zeroed"], 1)
            dve.wait_ge(m["zeroed"], 1)
            V.tensor_copy(vrow[:, :], zero[:, :])
            V.tensor_copy(brow[:, :], zero[:, 0:512]).then_inc(m["zeroed"], 1)
            dve.wait_ge(m["highs"], 1)
            V.tensor_tensor(vrow[32:32 + B, :].rearrange("p (a n) -> p a n", a=2), pr[0:B, :, :],
                            vrow[0:B, :].bitcast(F32).rearrange("p (a n) -> p a n", a=2), ALU.subtract)
            V.tensor_tensor(brow[32:32 + B, :], ph[0:B, :], brow[0:B, :].bitcast(F32), ALU.subtract).then_inc(m["rows"], 1)
            perm = lambda t: t.rearrange("p h b -> p b h")
            kT, qT = (perm(S.proj[:, s:s + 8, T:N]) for s in (NK, NQ))
            own(V.tensor_tensor(wk[:, :, :], kT, perm(S.ba[:, :, 12:20]), ALU.mult))
            n0 = S.n0[:, :].rearrange("p (b h) -> p b h", b=B)
            own(V.tensor_tensor(n0, n0, perm(S.ba[:, :, 4:12]), ALU.mult))
            own(V.tensor_tensor(n0, n0, wk[:, :, :], ALU.add))
            V.tensor_tensor(qn[:, :, :], n0, qT, ALU.mult).then_inc(m["qn_in"], 1)
            for a in range(2):
                ps = slice(64 * a, 64 * a + 64)
                V.tensor_copy(dec[ps], S.bb[ps, a::2, 4:12])
                V.tensor_copy(dt[ps], S.bb[ps, a::2, 12:20])
                last = V.tensor_copy(dsk[ps], S.bb[ps, a::2, 20])
            last.then_inc(m["gathered"], 1)
            xs = S.proj[:, NX:NX + KD, T:N]
            dve.wait_ge(m["rows"], 1)
            own(V.memset(yv[:, :, :], 0.0))
            own(V.tensor_tensor(xd[:, :, :], dt[:, :, :], xs, ALU.mult))
            for u in range(NU):
                dve.wait_ge(m["decayed"], u + 1)
                for b in range(SQ):
                    s = SQ * u + b
                    dve.wait_ge(m["spread"], s + 1)
                    for h in range(H_A):
                        last = V.scalar_tensor_tensor(out=st[u][:, b, h, :], in0=pv[s % 2][:, h // 4, h % 4 * P:h % 4 * P + P], scalar=wk[:, s, h:h + 1],
                                                      in1=st[u][:, b, h, :], op0=ALU.mult, op1=ALU.add)
                    last.then_inc(m["read"], 1)
                dve.wait_ge(m["read"], SQ * (u + 1))
                dve.sem_inc(m["unit"], 1)
            def ssd_unit(u):
                dve.wait_ge(m["decayed"], NU + u + 1)
                for b in range(SQ):
                    s = SQ * u + b
                    dve.wait_ge(m["spread"], B + s + 1)
                    for c in range(KD):
                        g = c // 4
                        last = V.scalar_tensor_tensor(out=st[u][:, b, c, :], in0=pv[s % 2][:, 0, g * P:(g + 1) * P], scalar=xd[:, c, s:s + 1],
                                                      in1=st[u][:, b, c, :], op0=ALU.mult, op1=ALU.add)
                    own(last)
                    for c in range(KD):
                        g = c // 4
                        last = V.tensor_tensor_reduce(out=junk[:, c, :], in0=pv[s % 2][:, 0, 256 + g * P:256 + (g + 1) * P], in1=st[u][:, b, c, :],
                                                      scale=1.0, scalar=0.0, op0=ALU.mult, op1=ALU.add, accum_out=yv[:, c, s:s + 1])
                    own(last)
                    dve.sem_inc(m["read"], 1)
                dve.sem_inc(m["unit"], 1)

            ssd_unit(0)
            dve.wait_ge(m["den_in"], 1)
            dve.wait_ge(m["num_in"], NU)
            flat = lambda t: t.rearrange("p b h -> p (b h)")
            own(V.tensor_copy(flat(nd[:, :, :]), pm[:, 64:128]))
            own(V.scalar_tensor_tensor(out=nd[:, :, :], in0=nd[:, :, :], scalar=-1.0, in1=nd[:, :, :], op0=ALU.mult, op1=ALU.max))
            own(V.tensor_tensor(nd[:, :, :], nd[:, :, :], perm(S.ba[:, :, 20:28]), ALU.max))
            own(V.reciprocal(nd[:, :, :], nd[:, :, :]))
            V.tensor_tensor(flat(hh[:, :, :]), pm[:, 0:64], flat(nd[:, :, :]), ALU.mult).then_inc(m["mean_in"], 1)
            dve.wait_ge(m["meant"], 1)
            own(V.scalar_tensor_tensor(out=flat(hh[:, :, :]), in0=pm[:, 128:192], scalar=-1.0 / P, in1=flat(hh[:, :, :]), op0=ALU.mult, op1=ALU.add))
            V.tensor_tensor(t1[:, :, :], hh[:, :, :], hh[:, :, :], ALU.mult).then_inc(m["sq_in"], 1)
            dve.wait_ge(m["var_in"], 1)
            V.tensor_scalar(flat(t2[:, :, :]), pm[:, 192:256], 1.0 / P, EPS, ALU.mult, ALU.add).then_inc(m["var_out"], 1)
            dve.wait_ge(m["rooted"], 1)
            own(V.tensor_tensor(hh[:, :, :], hh[:, :, :], t2[:, :, :], ALU.mult))
            own(V.tensor_tensor(hh[:, :, :], hh[:, :, :], bcast(S.vec[:, V_GA:V_GA + 8], 1, B), ALU.mult))
            V.tensor_tensor(qT, hh[:, :, :], perm(S.proj[:, NO:NO + 8, T:N]), ALU.mult)
            dve.wait_ge(m["n_in"], 1)
            V.tensor_copy(nrow[:, :], pr[0:64, 0, 0:P]).then_inc(m["n_out"], 1)
            for u in range(1, NU):
                ssd_unit(u)
            own(V.tensor_tensor(xd[:, :, :], xs, bcast(dsk[:, :], 2, B), ALU.mult))
            own(V.tensor_tensor(yv[:, :, :], yv[:, :, :], xd[:, :, :], ALU.add))
            own(V.tensor_tensor(S.proj[:, NZ:NZ + KD, T:N], yv[:, :, :], S.proj[:, NZ:NZ + KD, T:N], ALU.mult))


NB = [TOPK // (a + 1) for a in range(TOPK)]
NCAND = sum(NB)
LOW = -3.0e38
TB = 52
NTB = N // TB
JG = 4
NG = NKEY // JG
PAIRS_TK = 6
PAIRS_GM = 4


def residual_phase(nc, name, S, src, gate):
    with Phase(nc) as ctx:
        own_s = ctx.sem(f"own_{name}")
        t = ctx.enter_context(nc.sbuf_tensor(f"t_{name}", [P, KD, B], F32))
        block = ctx.enter_context(nc.Block())

        @block.vector
        def _(dve):
            own = Chain(dve, own_s)
            for k in range(KD):
                nc.vector.scalar_tensor_tensor(out=S.xT[:, k, 0:T], in0=src[:, k, 0:T], scalar=S.mod[:, gate + k, 0:1],
                                               in1=S.xT[:, k, 0:T], op0=ALU.mult, op1=ALU.add)
            own(nc.vector.tensor_tensor(t[:, :, :], src[:, :, T:N], S.mod[:, gate:gate + KD, 1:9], ALU.mult))
            own(nc.vector.tensor_tensor(S.xT[:, :, T:N], S.xT[:, :, T:N], t[:, :, :], ALU.add))


def split_phase(nc, name, src, XH, XL, gates_of=None):
    S = gates_of
    with Phase(nc) as ctx:
        high, low, gated, moved = (ctx.sem(f"{n}_{name}") for n in ("high", "low", "gated", "moved"))
        ps = ctx.enter_context(nc.psum_tensor(f"ps_{name}", [P, 2, 512], F32))
        block = ctx.enter_context(nc.Block())

        @block.scalar
        def _(act):
            for k in range(KD):
                nc.scalar.activation(XH[:, k, :], src[:, k, :], ACT.Copy).then_inc(high, 1)
            if S:
                act.wait_ge(gated, 1)
                nc.scalar.activation(halves(S.gate[:, :]), ps[0:96, :, 0:HN], ACT.Copy).then_inc(moved, 1)

        @block.tensor
        def _(pe):
            if S:
                for h in range(2):
                    for k in range(KD):
                        mm = nc.tensor.matmul(ps[0:96, h, 0:HN], S.wg[:, k, :], src[:, k, h * HN:(h + 1) * HN],
                                              start=(k == 0), stop=(k == KD - 1))
                mm.then_inc(gated, 1)

        @block.vector
        def _(dve):
            for k in range(KD):
                dve.wait_ge(high, k + 1)
                nc.vector.tensor_tensor(XL[:, k, :], src[:, k, :], XH[:, k, :].bitcast(F32), ALU.subtract).then_inc(low, 1)
            dve.wait_ge(low, KD)


def score_phase(nc, A, S, qry):
    with Phase(nc) as ctx:
        keys = ctx.enter_context(nc.sbuf_tensor("keys", [P, 2, P], F32))
        keysT = ctx.enter_context(nc.sbuf_tensor("keysT", [P, 2, P], F32))
        qs = ctx.enter_context(nc.sbuf_tensor("qs", [P, 2, PH, B], F32))
        ps = [ctx.enter_context(nc.psum_tensor(f"ps_sc{i}", [P, 4, P], F32)) for i in range(4)]
        pk = ctx.enter_context(nc.psum_tensor("pk_sc", [P, 4, P], F32))
        keys_in, keys_t, keys_s, gathered, scored, kept = (ctx.sem(n + "_sc") for n in ("keys_in", "keys_t", "keys_s", "gathered", "scored", "kept"))
        block = ctx.enter_context(nc.Block())

        @block.sync
        def _(sp):
            sp.dma_start(keys[:, :, :], A["peer_sub_keys"][0].rearrange("j k d -> k j d")).then_inc(keys_in, 16)
            sp.wait_ge(keys_in, 16)

        @block.vector
        def _(dve):
            nc.vector.tensor_copy(qs[:, :, :, :].rearrange("p j h b -> p h j b"),
                                  qry[:, :, T:N].rearrange("p (h j) b -> p h j b", j=2)).then_inc(gathered, 1)

        @block.tensor
        def _(pe):
            pe.wait_ge(keys_in, 16)
            nc.tensor.transpose(pk[:, 0, :], keys[:, 0, :], S.ident[:, :])
            nc.tensor.transpose(pk[:, 1, :], keys[:, 1, :], S.ident[:, :]).then_inc(keys_t, 1)
            pe.wait_ge(keys_s, 1)
            pe.wait_ge(gathered, 1)
            for j in range(2):
                mm = nc.tensor.matmul(pk[0:PH * B, j, :], qs[:, j, :, :].rearrange("p h b -> p (h b)"), keysT[:, j, :], start=True, stop=True)
            mm.then_inc(scored, 1)
            for t in range(NC):
                for q in range(4):
                    n = 4 * t + q
                    if n >= 4:
                        pe.wait_ge(kept, n - 2)
                    for i in range(4):
                        l = 4 * q + i
                        mm = nc.tensor.matmul(ps[q][:, i, :], qry[:, l, t * L:(t + 1) * L], keysT[:, l % 2, :], start=True, stop=True)
                    mm.then_inc(scored, 1)

        @block.scalar
        def _(act):
            act.wait_ge(keys_t, 1)
            nc.scalar.activation(keysT[:, :, :], pk[:, 0:2, :], ACT.Copy).then_inc(keys_s, 1)
            act.wait_ge(scored, 1)
            nc.scalar.activation(S.scS[:, :, :], pk[0:PH * B, 0:2, :], ACT.Copy).then_inc(kept, 1)
            for n in range(16):
                act.wait_ge(scored, n + 2)
                nc.scalar.activation(S.sc[:, n // 4, 4 * (n % 4):4 * (n % 4) + 4, :], ps[n % 4][:, :, :], ACT.Copy).then_inc(kept, 1)


class TopK:

    LINKS = 24

    def __init__(self, nc, S, name, ctx, rows, H, lists=None):
        sb = lambda n, s, d=F32: ctx.enter_context(nc.sbuf_tensor(f"{n}_{name}", s, d))
        self.nc, self.S, self.H, self.rows = nc, S, H, rows
        self.lists = lists if lists is not None else sb("lists", [rows, 2 * H, NKEY])
        self.top = sb("top", [rows, 2 * H, TOPK])
        self.idx = sb("idx", [rows, 2 * H, TOPK], U32)
        self.idf = sb("idf", [rows, 2 * H, TOPK])
        self.cand, self.cidx, self.cwk = (sb(n, [rows, H, NCAND]) for n in ("cand", "cidx", "cwk"))
        self.best = sb("best", [rows, H, TOPK])
        self.pos = sb("pos", [rows, H, TOPK], U32)
        self.posf = sb("posf", [rows, H, TOPK])
        self.hit = sb("hit", [rows, H * TOPK, NCAND])
        self.wk = self.hit[:, :, :].rearrange("p a b -> p (a b)")[:, 0:2 * H * NKEY].rearrange("p (l k) -> p l k", k=NKEY)
        self.ei = sb("ei", [rows, H * TOPK])
        self.eu = sb("eu", [rows, 2, H * TOPK], U32)
        self.eh = sb("eh", [rows, H * TOPK], U32)
        self.sum = sb("sum", [rows, H])

    def best_of(self, own, half, values, work, top, idx, lists):
        V = self.nc.vector
        at = slice(8 * half, 8 * half + 8)
        src = work if half else values
        own.take(V)
        for l in lists:
            last = V.max(top[:, l, at], src[:, l, :])
        own(last)
        own.take(V)
        for l in lists:
            last = V.max_index(idx[:, l, at], top[:, l, at], src[:, l, :])
            if not half:
                last = V.match_replace(work[:, l, :], top[:, l, at], src[:, l, :], LOW)
        own(last)

    def best_of_lists(self, own, half, part):
        n = max(self.H, 2)
        self.best_of(own, half, self.lists, self.wk, self.top, self.idx, range(part * n, part * n + n))

    def candidates(self, own):
        V, n, H = self.nc.vector, self.rows, self.H
        own(V.tensor_copy(self.idf[:, :, :], self.idx[:, :, :]))
        t4 = self.top[:, :, :].rearrange("p (h j) k -> p h j k", j=2)
        i4 = self.idf[:, :, :].rearrange("p (h j) k -> p h j k", j=2)
        own(V.tensor_scalar(i4[:, :, 0, :], i4[:, :, 0, :], float(NKEY), None, ALU.mult))
        off = 0
        for a in range(8):
            o = slice(off, off + NB[a])
            V.tensor_tensor(self.cand[:, :, o], bcast(t4[:, :, 0, a], 2, NB[a]), t4[:, :, 1, 0:NB[a]], ALU.add)
            V.tensor_tensor(self.cidx[:, :, o], bcast(i4[:, :, 0, a], 2, NB[a]), i4[:, :, 1, 0:NB[a]], ALU.add)
            off += NB[a]
        o = slice(off, off + 8)
        V.tensor_tensor(self.cand[:, :, o], t4[:, :, 0, 8:16], t4[:, :, 1, 0:1].to_broadcast((n, H, 8)), ALU.add)
        own(V.tensor_tensor(self.cidx[:, :, o], i4[:, :, 0, 8:16], i4[:, :, 1, 0:1].to_broadcast((n, H, 8)), ALU.add))

    def best_of_sums(self, own, half):
        self.best_of(own, half, self.cand, self.cwk, self.best, self.pos, range(self.H))
        if half:
            own(self.nc.vector.tensor_copy(self.posf[:, :, :], self.pos[:, :, :]))

    def half_of(self, part):
        n = self.H * TOPK // 2
        return slice(0, 2 * n) if part is None else slice(part * n, (part + 1) * n)

    def find(self, part=None):
        at = self.half_of(part)
        n = at.stop - at.start
        return self.nc.vector.tensor_tensor(self.hit[:, at, :], bcast(self.posf[:, :, :].rearrange("p h k -> p (h k)")[:, at], 2, NCAND),
                                            bcast(self.S.iota[0:self.rows, 0:NCAND], 1, n), ALU.is_equal)

    def shift(self, own):
        V = self.nc.vector
        own(V.tensor_copy(self.sum[:, :], self.best[:, :, 0]))
        return V.tensor_tensor(self.best[:, :, :], self.best[:, :, :], bcast(self.sum[:, :], 2, TOPK), ALU.subtract)

    def gates(self, own, out):
        V = self.nc.vector
        own(V.reduce_sum(self.sum[:, :], self.best[:, :, :], AX_X))
        own(V.reciprocal(self.sum[:, :], self.sum[:, :]))
        own(V.tensor_tensor(out.rearrange("p (h k) -> p h k", h=self.H), self.best[:, :, :], bcast(self.sum[:, :], 2, TOPK), ALU.mult))

    def numbers(self, own, part=None):
        at = self.half_of(part)
        own(self.nc.vector.reduce_sum(self.ei[:, at], self.hit[:, at, :], AX_X))

    def experts(self, own, row, column):
        V = self.nc.vector
        own(V.tensor_copy(self.eu[:, 0, :], self.ei[:, :]))
        V.tensor_scalar(self.eu[:, 1, :], self.eu[:, 0, :], NKEY - 1, None, ALU.bitwise_and)
        own(V.tensor_scalar(self.eh[:, :], self.eu[:, 0, :], 7, None, ALU.logical_shift_right))
        V.tensor_copy(row, self.eh[:, :])
        return V.tensor_copy(column, self.eu[:, 1, :])


class LoopChain:

    def __init__(self, engine, sem, i, links, target, source):
        self.engine, self.sem, self.i, self.links, self.n = engine, sem, i, links, 0
        self.target, self.source = target, source

    def take(self, vector):
        vector.tensor_copy(self.target, self.source)

    def __call__(self, instruction):
        self.n += 1
        assert self.n <= self.links
        instruction.then_inc(self.sem, 1)
        self.engine.wait_ge(self.sem, self.links * self.i + self.n)


class Hidden:

    def __init__(self, nc, A, S, name, ctx, base, pairs, bufs, hidden_dram):
        sb = lambda n, s, d=F32: ctx.enter_context(nc.sbuf_tensor(f"{n}_{name}", s, d))
        self.nc, self.S, self.base, self.pairs, self.bufs, self.dram = nc, S, base, pairs, bufs, hidden_dram
        self.units = 2 * pairs
        self.u = [sb(f"u{i}", [P, 2, D]) for i in range(bufs)]
        self.ge = [sb(f"ge{i}", [P, 2, N]) for i in range(bufs)]
        self.utH = [sb(f"utH{i}", [P, KD, P], F32R) for i in range(2)]
        self.utL = [sb(f"utL{i}", [P, KD, P], F32R) for i in range(2)]
        self.pt = [ctx.enter_context(nc.psum_tensor(f"pt{i}_{name}", [P, 4, P], F32)) for i in range(2)]
        self.pa = [ctx.enter_context(nc.psum_tensor(f"pa{i}_{name}", [P, 512], F32)) for i in range(2)]
        self.uv = A["peer_u"][0].rearrange("(i j) d -> i j d", j=NKEY)
        self.u_in = [ctx.sem(f"u_in{i}_{name}") for i in range(bufs)]
        self.stored = [ctx.sem(f"ge_stored{i}_{name}") for i in range(bufs)]
        self.turned, self.high, self.low, self.hidden, self.gelued = (ctx.sem(f"{n}_{name}") for n in ("turned", "high", "low", "hidden", "gelued"))

    def load(self, sp, i, p):
        b = p % self.bufs
        sp.wait_ge(self.turned, 4 * self.pairs * i + 4 * (p + 1))
        sp.dma_start(self.u[b][:, :, :], self.uv[:, bass.ds(i * (2 * self.pairs) + 2 * (self.base + p), 2), :]).then_inc(self.u_in[b], 16)

    def start(self, pe):
        pe.sem_inc(self.turned, 4 * self.bufs)

    def turn(self, pe, i, u):
        p, b, per = u // 2, u // 2 % self.bufs, self.pairs // self.bufs
        if u % 2 == 0:
            pe.wait_ge(self.u_in[b], 16 * per * i + 16 * (p // self.bufs + 1))
        for x in range(2):
            pe.wait_ge(self.low, 2 * self.units * i + (2 * u + x + 1))
            for k in range(4):
                mm = self.nc.tensor.transpose(self.pt[x][:, k, :], self.u[b][:, u % 2, (4 * x + k) * P:(4 * x + k + 1) * P], self.S.ident[:, :])
            mm.then_inc(self.turned, 1)

    def hide(self, pe, i, u):
        S = self.S
        pe.wait_ge(self.low, 2 * self.units * i + (2 * u + 2 + 2))
        for h in range(2):
            tok = slice(h * HN, (h + 1) * HN)
            pe.wait_ge(self.gelued, 2 * self.units * i + (2 * u + h + 1))
            n = 0
            for k in range(KD):
                for w, x in ((self.utH, S.hH), (self.utH, S.hL), (self.utL, S.hH)):
                    mm = self.nc.tensor.matmul(self.pa[h][:, 0:HN], w[u % 2][:, k, :], x[:, k, tok], start=(n == 0), stop=(n == 3 * KD - 1))
                    n += 1
            mm.then_inc(self.hidden, 1)

    def move_high(self, act, i, u):
        for x in range(2):
            act.wait_ge(self.turned, 2 * self.units * i + (2 * u + x + 1 + 4 * self.bufs))
            if x == 0:
                act.wait_ge(self.hidden, 2 * self.units * i + (2 * u + 2))
            self.nc.scalar.activation(self.utH[u % 2][:, 4 * x:4 * x + 4, :], self.pt[x][:, :, :], ACT.Copy).then_inc(self.high, 1)

    def gelu(self, act, i, u):
        b, per = u // 2 % self.bufs, self.pairs // self.bufs
        if u % 2 == 0:
            act.wait_ge(self.stored[b], 16 * per * i + 16 * (u // 2 // self.bufs + 1))
        for h in range(2):
            act.wait_ge(self.hidden, 2 * self.units * i + (2 * u + h + 1 + 4))
            self.nc.scalar.activation(self.ge[b][:, u % 2, h * HN:(h + 1) * HN], self.pa[h][:, 0:HN], ACT.Gelu).then_inc(self.gelued, 1)
        if u % 2:
            act.wait_ge(self.gelued, 2 * self.units * i + (2 * u + 2 + 2))
            act.dma_start(self.dram[bass.ds(i * self.pairs + (self.base + u // 2), 1)].rearrange("q i e -> (q i) e"),
                          self.ge[b][:, :, :].rearrange("p j n -> p (j n)")).then_inc(self.stored[b], 16)

    def start_act(self, act):
        act.sem_inc(self.gelued, 2)
        for s in self.stored:
            act.sem_inc(s, 16)

    def finish_act(self, act, iterations):
        for s in self.stored:
            act.wait_ge(s, 16 * (self.pairs // self.bufs * iterations + 1))

    def start_dve(self, dve):
        dve.sem_inc(self.low, 2)
        dve.sem_inc(self.hidden, 4)

    def move_low(self, dve, i, u):
        for x in range(2):
            dve.wait_ge(self.high, 2 * self.units * i + (2 * u + x + 1))
            self.nc.vector.tensor_tensor(self.utL[u % 2][:, 4 * x:4 * x + 4, :], self.pt[x][:, :, :],
                                         self.utH[u % 2][:, 4 * x:4 * x + 4, :].bitcast(F32), ALU.subtract).then_inc(self.low, 1)


def topk_phase(nc, A, S, hidden_dram):
    with Phase(nc) as ctx:
        H = Hidden(nc, A, S, "tk", ctx, 0, PAIRS_TK, 3, hidden_dram)
        K = TopK(nc, S, "tk", ctx, P, PH)
        KS = TopK(nc, S, "ts", ctx, PH * B, 1, S.scS)
        res = ctx.enter_context(nc.sbuf_tensor("res_tk", [P, 3, P], F32))
        rs = ctx.enter_context(nc.sbuf_tensor("rs_tk", [PH * B, 3, TOPK], F32))
        rt = ctx.enter_context(nc.sbuf_tensor("rt_tk", [B, 3, P], F32))
        taken = ctx.enter_context(nc.sbuf_tensor("taken_tk", [1, 1], F32))
        pr = ctx.enter_context(nc.psum_tensor("pr_tk", [P, 4, P], F32))
        m = {n: ctx.sem(n + "_tk") for n in ("s_shifted", "s_gates", "s_res", "s_moved", "lists", "hit", "picked", "shifted",
                                             "gates", "res", "res_t", "res_s", "own", "s_own")}
        block = ctx.enter_context(nc.Block())
        U = H.units

        @block.sync
        def _(sp):
            with sp.Fori(0, NC) as i:
                for p in range(PAIRS_TK):
                    H.load(sp, i, p)
            sp.wait_ge(m["s_res"], 1)
            for h in range(PH):
                sp.dma_start(rt[:, :, h * TOPK:(h + 1) * TOPK], rs[h * B:(h + 1) * B, :, :]).then_inc(m["s_moved"], 16)
            sp.wait_ge(m["s_moved"], 16 * PH)

        @block.tensor
        def _(pe):
            H.start(pe)

            def tile(i, last=False):
                for u in range(U):
                    if not (last and u == U - 1):
                        H.turn(pe, i, u + 1)
                    H.hide(pe, i, u)
                    if u == U - 1:
                        pe.wait_ge(m["res"], 1 * i + 1)
                        pe.wait_ge(m["res_s"], 1 * i + 1)
                        for q in range(3):
                            mm = nc.tensor.transpose(pr[:, q, :], res[:, q, :], S.ident[:, :])
                        mm.then_inc(m["res_t"], 1)

            H.turn(pe, 0, 0)
            with pe.Fori(0, NC - 1) as i:
                tile(i)
            tile(NC - 1, last=True)
            pe.wait_ge(m["s_moved"], 16 * PH)
            pe.wait_ge(m["res_s"], NC + 1)
            for q in range(3):
                mm = nc.tensor.transpose(pr[:, q, 0:B], rt[:, q, :], S.ident[0:B, 0:B])
            mm.then_inc(m["res_t"], 1)

        @block.scalar
        def _(act):
            H.start_act(act)
            act.sem_inc(m["res_s"], 1)

            def take_lists(i):
                act.wait_ge(m["shifted"], 1 * i + 1)
                nc.scalar.activation(K.lists[:, :, :], S.sc[:, bass.ds(i, 1), :, :].rearrange("p a l k -> p (a l) k"), ACT.Copy).then_inc(m["lists"], 1)

            def tile(i, last=False):
                for u in range(U):
                    if not (last and u == U - 1):
                        H.move_high(act, i, u + 1)
                    H.gelu(act, i, u)
                    if u == 7:
                        act.wait_ge(m["shifted"], 1 * i + 2)
                        nc.scalar.activation(K.best[:, :, :], K.best[:, :, :], ACT.Exp).then_inc(m["gates"], 1)
                    if u == 8 and not last:
                        take_lists(i + 1)
                    if last and u == 5:
                        act.wait_ge(m["s_shifted"], 1)
                        nc.scalar.activation(KS.best[:, :, :], KS.best[:, :, :], ACT.Exp).then_inc(m["s_gates"], 1)
                    if u == U - 1:
                        act.wait_ge(m["res_t"], 1 * i + 1)
                        nc.scalar.activation(S.sel[:, :, bass.ds(i * L, L)], pr[:, 0:3, :], ACT.Copy).then_inc(m["res_s"], 1)

            take_lists(0)
            H.move_high(act, 0, 0)
            with act.Fori(0, NC - 1) as i:
                tile(i)
            tile(NC - 1, last=True)
            act.wait_ge(m["res_t"], NC + 1)
            nc.scalar.activation(S.sel[:, :, T:N], pr[:, 0:3, 0:B], ACT.Copy).then_inc(m["res_s"], 1)
            H.finish_act(act, NC)

        @block.gpsimd
        def _(pool):
            with pool.Fori(0, NC) as i:
                for h in range(PH):
                    if h % (PH // 2) == 0:
                        pool.wait_ge(m["hit"], 2 * i + (h // (PH // 2) + 1))
                    k = slice(h * TOPK, (h + 1) * TOPK)
                    last = nc.gpsimd.tensor_tensor(K.hit[:, k, :], K.hit[:, k, :], bcast(K.cidx[:, h, :], 1, TOPK), ALU.mult)
                    if h % (PH // 2) == PH // 2 - 1:
                        last.then_inc(m["picked"], 1)

        @block.vector
        def _(dve):
            V = nc.vector
            H.start_dve(dve)
            dve.sem_inc(m["shifted"], 1)

            def tile(i, last=False):
                own = LoopChain(dve, m["own"], i, TopK.LINKS, taken[:, :], S.ones[0:1, 0:1])
                s_own = Chain(dve, m["s_own"])
                for u in range(U):
                    if not (last and u == U - 1):
                        H.move_low(dve, i, u + 1)
                    if u < 4:
                        if u == 0:
                            dve.wait_ge(m["lists"], 1 * i + 1)
                        K.best_of_lists(own, u // 2, u % 2)
                    elif u == 4:
                        K.candidates(own)
                    elif u == 5:
                        K.best_of_sums(own, 0)
                    elif u == 6:
                        K.best_of_sums(own, 1)
                        K.shift(own).then_inc(m["shifted"], 1)
                    elif u < 9:
                        K.find(u - 7).then_inc(m["hit"], 1)
                    elif u < 11:
                        if u == 9:
                            dve.wait_ge(m["gates"], 1 * i + 1)
                            dve.wait_ge(m["res_s"], 1 * i + 1)
                            K.gates(own, res[:, 2, :])
                        dve.wait_ge(m["picked"], 2 * i + (u - 8))
                        K.numbers(own, u - 9)
                    else:
                        K.experts(own, res[:, 0, :], res[:, 1, :]).then_inc(m["res"], 1)
                    if last and u < 2:
                        KS.best_of_lists(s_own, u, 0)
                    elif last and u == 2:
                        KS.candidates(s_own)
                    elif last and u == 3:
                        KS.best_of_sums(s_own, 0)
                        KS.best_of_sums(s_own, 1)
                    elif last and u == 4:
                        s_own(KS.find())
                        KS.shift(s_own).then_inc(m["s_shifted"], 1)
                    elif last and u == 6:
                        s_own(V.tensor_tensor(KS.hit[:, :, :], KS.hit[:, :, :], bcast(KS.cidx[:, 0, :], 1, TOPK), ALU.mult))
                        KS.numbers(s_own)
                        dve.wait_ge(m["s_gates"], 1)
                        KS.gates(s_own, rs[:, 2, :])
                        KS.experts(s_own, rs[:, 0, :], rs[:, 1, :]).then_inc(m["s_res"], 1)
                assert own.n == TopK.LINKS, own.n

            H.move_low(dve, 0, 0)
            with dve.Fori(0, NC - 1) as i:
                tile(i)
            tile(NC - 1, last=True)


def gate_matrix_phase(nc, A, S, gates, hidden_dram):
    QUADS = (0, 1, 2, 2, 2, 2, 2, 2)
    Q = TB // 4
    BANKS = 4
    assert sum(QUADS) == Q and NTB * PAIRS_GM + NC * PAIRS_TK == NKEY // 2
    with Phase(nc) as ctx:
        H = Hidden(nc, A, S, "gm", ctx, NC * PAIRS_TK, PAIRS_GM, 2, hidden_dram)
        sb = lambda n, s: ctx.enter_context(nc.sbuf_tensor(n, s, F32))
        pick = sb("pick_gm", [P, 3, TB])
        oh = sb("oh_gm", [P, 2, 4, 2, P])
        stage = sb("stage_gm", [P, NG, JG, TB])
        ps = [ctx.enter_context(nc.psum_tensor(f"ps_gm{i}", [P, 4, P], F32)) for i in range(BANKS)]
        picks, hot, multiplied, staged, stored = (ctx.sem(n + "_gm") for n in ("picks", "hot", "multiplied", "staged", "stored"))
        block = ctx.enter_context(nc.Block())
        gv = gates.rearrange("g i b e -> i b g e")
        U = H.units
        first = [sum(QUADS[:u]) for u in range(U + 1)]

        @block.sync
        def _(sp):
            with sp.Fori(0, NTB) as i:
                for p in range(PAIRS_GM):
                    H.load(sp, i, p)

        @block.vector
        def _(dve):
            V = nc.vector
            H.start_dve(dve)

            def tokens(i, last=False):
                dve.wait_ge(multiplied, Q * i + 2)
                V.tensor_copy(pick[:, :, :], S.sel[:, :, bass.ds(i * TB, TB)]).then_inc(picks, 1)
                for u in range(U):
                    if not (last and u == U - 1):
                        H.move_low(dve, i, u + 1)
                    if u == 0:
                        dve.wait_ge(picks, 1 * i + 1)
                    for q in range(first[u], first[u + 1]):
                        dve.wait_ge(multiplied, Q * i + (max(q, 1) + 1))
                        for t in range(4):
                            k = 4 * q + t
                            V.tensor_scalar(oh[:, q % 2, t, 0, :], S.iota[:, :], pick[:, 0, k:k + 1], None, ALU.is_equal)
                            hot_t = V.tensor_scalar(oh[:, q % 2, t, 1, :], S.iota[:, :], pick[:, 1, k:k + 1], pick[:, 2, k:k + 1], ALU.is_equal, ALU.mult)
                        hot_t.then_inc(hot, 1)

            H.move_low(dve, 0, 0)
            with dve.Fori(0, NTB - 1) as i:
                tokens(i)
            tokens(NTB - 1, last=True)

        @block.tensor
        def _(pe):
            H.start(pe)
            pe.sem_inc(multiplied, 2)

            def tokens(i, last=False):
                for u in range(U):
                    if not (last and u == U - 1):
                        H.turn(pe, i, u + 1)
                    H.hide(pe, i, u)
                    for q in range(first[u], first[u + 1]):
                        pe.wait_ge(hot, Q * i + (q + 1))
                        pe.wait_ge(staged, Q * i + max(q + 1, BANKS))
                        for t in range(4):
                            mm = nc.tensor.matmul(ps[q % BANKS][:, t, :], oh[:, q % 2, t, 0, :], oh[:, q % 2, t, 1, :], start=True, stop=True)
                        mm.then_inc(multiplied, 1)

            H.turn(pe, 0, 0)
            with pe.Fori(0, NTB - 1) as i:
                tokens(i)
            tokens(NTB - 1, last=True)

        @block.scalar
        def _(act):
            H.start_act(act)
            act.sem_inc(staged, BANKS)
            act.sem_inc(stored, 16)

            def tokens(i, last=False):
                for u in range(U + 1):
                    if u < U:
                        if not (last and u == U - 1):
                            H.move_high(act, i, u + 1)
                        H.gelu(act, i, u)
                    for q in range(first[max(u, 1) - 1], first[u]):
                        if q == 0:
                            act.wait_ge(stored, 16 * i + 16)
                        act.wait_ge(multiplied, Q * i + (q + 3))
                        nc.scalar.activation(stage[:, :, :, 4 * q:4 * q + 4].rearrange("p g j t -> p t (g j)"), ps[q % BANKS][:, :, :], ACT.Copy).then_inc(staged, 1)
                act.wait_ge(staged, Q * i + (Q + BANKS))
                act.dma_start(gv[:, bass.ds(i, 1), :, :].rearrange("i b g e -> i (b g) e"),
                              stage[:, :, :, :].rearrange("p g j t -> p g (j t)")).then_inc(stored, 16)

            H.move_high(act, 0, 0)
            with act.Fori(0, NTB - 1) as i:
                tokens(i)
            tokens(NTB - 1, last=True)
            act.wait_ge(stored, 16 * (NTB + 1))
            H.finish_act(act, NTB)


def value_phase(nc, A, S, gates, hidden_dram):
    with Phase(nc) as ctx:
        sem = ctx.sem
        sb = lambda n, s, d=F32: ctx.enter_context(nc.sbuf_tensor(n, s, d))
        vs = [sb(f"vs{i}", [P, 2, D]) for i in range(2)]
        vH = [sb(f"vH{i}", [P, JG, D], F32R) for i in range(2)]
        vL = [sb(f"vL{i}", [P, JG, D], F32R) for i in range(2)]
        ab = [sb(f"ab{i}", [P, JG, N]) for i in range(2)]
        gb = [sb(f"gb{i}", [P, NTB, JG, TB]) for i in range(2)]
        wH = [sb(f"wH{i}", [P, JG, N], F32R) for i in range(2)]
        wL = [sb(f"wL{i}", [P, JG, N], F32R) for i in range(2)]
        po = [ctx.enter_context(nc.psum_tensor(f"po_v{i}", [P, 2, 512], F32)) for i in range(4)]
        v_in, a_in, g_in = ([sem(f"{n}_in{i}_v") for i in range(2)] for n in "vag")
        high, low, weighted, w_high, w_low, mixed, added, zero = (
            sem(n + "_v") for n in ("high", "low", "weighted", "w_high", "w_low", "mixed", "added", "zero"))
        block = ctx.enter_context(nc.Block())
        vv = A["peer_v"][0].rearrange("(i j) d -> i j d", j=NKEY)
        blocked = lambda t: t.rearrange("p (b t) -> p b t", t=TB)

        @block.sync
        def _(sp):
            with sp.Fori(0, NG // 2) as i:
                for s in range(2):
                    def load_v(q):
                        sp.wait_ge(low, 2 * JG * i + (JG * s + 2 * q + 2))
                        sp.dma_start(vs[q][:, :, :], vv[:, bass.ds(8 * i + (4 * s + 2 * q), 2), :]).then_inc(v_in[q], 16)

                    load_v(0)
                    sp.wait_ge(w_low, 2 * JG * i + JG * (s + 1))
                    sp.dma_start(ab[s][:, :, :].rearrange("p (q j) n -> p q (j n)", q=2),
                                 hidden_dram[bass.ds(4 * i + 2 * s, 2)].rearrange("q i e -> i q e")).then_inc(a_in[s], 16)
                    sp.dma_start(gb[s][:, :, :, :].rearrange("p b j t -> p (b j t)"),
                                 gates[bass.ds(2 * i + s, 1)].rearrange("g i b e -> (g i) (b e)")).then_inc(g_in[s], 16)
                    load_v(1)

        @block.gpsimd
        def _(pool):
            pool.sem_inc(low, 4)
            with pool.Fori(0, NG // 2) as i:
                for s in range(2):
                    for j in range(JG):
                        pool.wait_ge(high, 2 * JG * i + (JG * s + j + 1))
                        nc.gpsimd.tensor_tensor(vL[s][:, j, :], vs[j // 2][:, j % 2, :], vH[s][:, j, :].bitcast(F32), ALU.subtract).then_inc(low, 1)

        @block.scalar
        def _(act):
            with act.Fori(0, NG // 2) as i:
                for s in range(2):
                    act.wait_ge(mixed, 2 * KD * i + KD * (s + 1))
                    for j in range(JG):
                        if j % 2 == 0:
                            act.wait_ge(v_in[j // 2], 32 * i + 16 * (s + 1))
                        nc.scalar.activation(vH[s][:, j, :], vs[j // 2][:, j % 2, :], ACT.Copy).then_inc(high, 1)
                        act.wait_ge(weighted, 2 * JG * i + (JG * s + j + 1))
                        nc.scalar.activation(wH[s][:, j, :], ab[s][:, j, :], ACT.Copy).then_inc(w_high, 1)

        @block.vector
        def _(dve):
            V = nc.vector
            V.memset(S.acc[:, :, :], 0.0).then_inc(zero, 1)
            dve.wait_ge(zero, 1)
            dve.sem_inc(w_low, 2 * JG)
            dve.sem_inc(added, 4 + KD)

            def weigh(i, s, j):
                if j == 0:
                    dve.wait_ge(a_in[s], 16 * i + 16)
                    dve.wait_ge(g_in[s], 16 * i + 16)
                V.tensor_tensor(blocked(ab[s][:, j, :]), blocked(ab[s][:, j, :]), gb[s][:, :, j, :], ALU.mult).then_inc(weighted, 1)
                dve.wait_ge(w_high, 2 * JG * i + (JG * s + j + 1))
                V.tensor_tensor(wL[s][:, j, :], ab[s][:, j, :], wH[s][:, j, :].bitcast(F32), ALU.subtract).then_inc(w_low, 1)

            def add(i, s, k):
                dve.wait_ge(mixed, 2 * KD * i + (KD * s + k + 1 + 2 * KD))
                V.tensor_tensor(halves(S.acc[:, k, :]), halves(S.acc[:, k, :]), po[k % 4][:, :, 0:HN], ALU.add).then_inc(added, 1)

            def two_groups(i, last=False):
                for s in range(2):
                    for j in range(JG):
                        if not (last and s == 1):
                            weigh(i if s == 0 else i + 1, 1 - s, j)
                        add(i, s, 2 * j)
                        add(i, s, 2 * j + 1)

            for j in range(JG):
                weigh(0, 0, j)
            with dve.Fori(0, NG // 2 - 1) as i:
                two_groups(i)
            two_groups(NG // 2 - 1, last=True)

        @block.tensor
        def _(pe):
            pe.sem_inc(mixed, 2 * KD)
            with pe.Fori(0, NG // 2) as i:
                for s in range(2):
                    for kp in range(KD // 2):
                        pe.wait_ge(added, 2 * KD * i + (KD * s + 2 * kp + 2 + KD))
                        for j in range(JG):
                            if kp == 0:
                                pe.wait_ge(low, 2 * JG * i + (JG * s + j + 1 + 4))
                                pe.wait_ge(w_low, 2 * JG * i + (JG * s + j + 1 + 2 * JG))
                            for x in range(2):
                                k = 2 * kp + x
                                cols = slice(k * P, (k + 1) * P)
                                for h in range(2):
                                    tok = slice(h * HN, (h + 1) * HN)
                                    for n, (v, w) in enumerate(((vH, wH), (vH, wL), (vL, wH))):
                                        mm = nc.tensor.matmul(po[k % 4][:, h, 0:HN], v[s][:, j, cols], w[s][:, j, tok],
                                                              start=(j == 0 and n == 0), stop=(j == JG - 1 and n == 2))
                                if j == JG - 1:
                                    mm.then_inc(mixed, 1)


def output_phase(nc, S, O, y):
    with Phase(nc) as ctx:
        st = [ctx.enter_context(nc.sbuf_tensor(f"st_out{i}", [P, 2, 512], F32)) for i in range(2)]
        ps = [ctx.enter_context(nc.psum_tensor(f"ps_out{i}", [P, 2, 512], F32)) for i in range(2)]
        turned, moved = (ctx.sem(n + "_out") for n in ("turned", "moved"))
        done = [ctx.sem(f"done{i}_out") for i in range(2)]
        block = ctx.enter_context(nc.Block())
        tiles = [(t * L, L, O["y_p"][0, t * L:(t + 1) * L, :]) for t in range(NC)] + [(T, B, O["y_s"].rearrange("b t d -> (b t) d"))]

        @block.tensor
        def _(pe):
            for t, (at, n, _) in enumerate(tiles):
                if t >= 2:
                    pe.wait_ge(moved, t - 1)
                for k in range(KD):
                    mm = nc.tensor.transpose(ps[t % 2][0:n, k // 4, k % 4 * P:k % 4 * P + P], y[:, k, at:at + n], S.ident[:, :])
                mm.then_inc(turned, 1)

        @block.scalar
        def _(act):
            for t, (_, n, _) in enumerate(tiles):
                act.wait_ge(turned, t + 1)
                if t >= 2:
                    act.wait_ge(done[t % 2], 16 * (t // 2))
                nc.scalar.activation(st[t % 2][0:n], ps[t % 2][0:n], ACT.Copy).then_inc(moved, 1)

        @block.sync
        def _(sp):
            for t, (_, n, dst) in enumerate(tiles):
                sp.wait_ge(moved, t + 1)
                sp.dma_start(dst, st[t % 2][0:n].rearrange("p a b -> p (a b)")).then_inc(done[t % 2], 16)
            for i in range(2):
                sp.wait_ge(done[i], 16 * ((len(tiles) + 1 - i) // 2))


class Buffers:
    pass


def program(nc, A, O, gates, hidden_dram):
    S, R = Buffers(), Buffers()
    with ExitStack() as whole:
        def sb(ctx, name, shape, dt=F32):
            t = ctx.enter_context(nc.sbuf_tensor(name, shape, dt))
            return t

        S.ident = sb(whole, "ident", [P, P])
        S.ones = sb(whole, "ones", [P, P])
        S.iota = sb(whole, "iota", [P, P])
        S.vec = sb(whole, "vec", [P, NVEC])
        S.mod = sb(whole, "mod", [P, 48, 9])
        S.rb = sb(whole, "rb", [P, N])
        S.gs = sb(whole, "gs", [P, KD, 9])
        S.xT = sb(whole, "xT", [P, KD, N])
        with ExitStack() as mixers:
            S.far = sb(mixers, "far", [P, P])
            S.wg = sb(mixers, "wg", [P, KD, 96])
            S.col = sb(mixers, "col", [H_B, 5])
            S.gate = sb(mixers, "gate", [96, N])
            S.m0T = sb(mixers, "m0T", [H_A, B])
            S.silc = sb(mixers, "silc", [P, KD, 9])
            S.raw = sb(mixers, "raw", [P, 28, 3 + B])
            S.n0 = sb(mixers, "n0", [P, 64])
            S.cbufa = sb(mixers, "cbufa", [P, 384])
            S.cbufb = sb(mixers, "cbufb", [P, 288])
            S.ea = sb(mixers, "ea", [H_B, 1])
            S.mS = sb(mixers, "mS", [H_A, B])
            S.mP = sb(mixers, "mP", [H_A, 1])
            setup_phase(nc, A, S)
            modulation_phase(nc, A, S)
            S.proj = sb(mixers, "proj", [P, SLOTS, N])
            with ExitStack() as ctx:
                hT = S.proj[:, SLOTS - KD:SLOTS, :]
                hH = sb(ctx, "hH_in", [P, KD, N], F32R)
                hL = sb(ctx, "hL_in", [P, KD, N], F32R)
                norm_phase(nc, "n1", S, lambda k: S.xT[:, k, :], KD, modulate(nc, S, hT, V_N1, 0, 8))
                split_phase(nc, "split1", hT, hH, hL, gates_of=S)
                input_phase(nc, A, S, hH, hL)
            S.cols = sb(mixers, "cols", [P, NC, 8, H_B])
            S.ba = sb(mixers, "ba", [P, H_A, 28])
            S.bb = sb(mixers, "bb", [P, H_B, 21])
            S.nrow = sb(mixers, "nrow", [H_A, P])
            R.split_M = sb(mixers, "split_M", [SPLIT, T], F32R)
            R.split_cum = sb(mixers, "split_cum", [SPLIT, T], F32R)
            S.pick = sb(mixers, "pick", [SPLIT, H_B, P], F32R)
            with ExitStack() as rows:
                R.a = sb(rows, "row_a", [H_A, N])
                R.M = sb(rows, "row_M", [H_A, N])
                R.cum = sb(rows, "row_cum", [H_B, N])
                R.dt = sb(rows, "row_dt", [H_B, N])
                gates_phase(nc, A, S, R, O)
            conv_phase(nc, A, S, O)
            mlstm_phase(nc, S, R, O)
            ssd_phase(nc, S, R, O)
            sample_phase(nc, A, S, O)

            def gain(dve, own):
                for k in range(KD):
                    last = nc.vector.scalar_tensor_tensor(out=S.proj[:, NZ + k, :], in0=S.proj[:, NZ + k, :], scalar=S.vec[:, V_GB + k:V_GB + k + 1],
                                                          in1=S.rb[:, :], op0=ALU.mult, op1=ALU.mult)
                own(last)
            norm_phase(nc, "ssm", S, lambda k: S.proj[:, NZ + k, :], KD, gain)
            mixed = lambda c, bank: nc.scalar.activation(S.proj[:, bass.ds(c + NK, 1), :].rearrange("p c (a n) -> p (c a) n", a=2), bank[:, :, 0:HN], ACT.Copy)
            project(nc, "out", [(0, 2, 0)], A["w_out"][0], 2 * KD, lambda k: S.proj[:, (NQ + k if k < KD else NZ + k - KD), :], mixed)
            residual_phase(nc, "r1", S, S.proj[:, NK:NK + KD, :], 16)
        with ExitStack() as experts:
            S.sel = sb(experts, "sel", [P, 3, N])
            S.hH = sb(experts, "hH", [P, KD, N], F32R)
            S.hL = sb(experts, "hL", [P, KD, N], F32R)
            with ExitStack() as scores:
                S.sc = sb(scores, "sc", [P, NC, 16, NKEY])
                S.scS = sb(scores, "scS", [PH * B, 2, NKEY])
                with ExitStack() as ctx:
                    h2T = sb(ctx, "h2T", [P, KD, N])
                    qry = sb(ctx, "qry", [P, 16, N])
                    norm_phase(nc, "n2", S, lambda k: S.xT[:, k, :], KD, modulate(nc, S, h2T, V_N2, 24, 32))
                    split_phase(nc, "split2", h2T, S.hH, S.hL)
                    project_split(nc, "query", [(0, 4, 0)], A["peer_w_query"][0], S.hH, S.hL, qry)
                    score_phase(nc, A, S, qry)
                topk_phase(nc, A, S, hidden_dram)
            gate_matrix_phase(nc, A, S, gates, hidden_dram)
        S.acc = sb(whole, "acc", [P, KD, N])
        value_phase(nc, A, S, gates, hidden_dram)
        def final(dve, own):
            for k in range(KD):
                last = nc.vector.scalar_tensor_tensor(out=S.acc[:, k, :], in0=S.xT[:, k, :], scalar=S.vec[:, V_GF + k:V_GF + k + 1],
                                                      in1=S.rb[:, :], op0=ALU.mult, op1=ALU.mult)
            own(last)
        norm_phase(nc, "nf", S, lambda k: S.xT[:, k, :], KD, final, residual=(S.acc, 40))
        output_phase(nc, S, O, S.acc)


_INS = ["x_prompt", "x_sample", "c_prompt", "c_sample", "state_mlstm_c", "state_mlstm_n", "state_mlstm_m", "state_mlstm_conv",
        "state_ssm", "state_ssm_conv", "w_ada", "b_ada", "norm1_g", "norm2_g", "w_in", "mlstm_gate_b", "conv_a_w", "conv_a_b",
        "mlstm_norm_g", "conv_b_w", "conv_b_b", "dt_bias", "a_log", "d_skip", "ssm_norm_g", "w_out", "peer_w_query",
        "peer_sub_keys", "peer_u", "peer_v", "final_norm_g"]
_OUTS = [("y_p", (1, T, D)), ("y_s", (B, 1, D)),
         ("p_c", (1, 1, H_A, P, P)), ("p_n", (1, 1, H_A, P)), ("p_m", (1, 1, H_A)), ("p_conva", (1, 1, 3, 2 * D)),
         ("p_ssm", (1, 1, H_B, P_B, P)), ("p_convb", (1, 1, 3, 1536)),
         ("s_c", (1, B, H_A, P, P)), ("s_n", (1, B, H_A, P)), ("s_m", (1, B, H_A)), ("s_conva", (1, B, 3, 2 * D)),
         ("s_ssm", (1, B, H_B, P_B, P)), ("s_convb", (1, B, 3, 1536))]


def kernel(**inputs):
    import numpy as _np
    import concourse.bacc as _bacc
    from concourse import mybir as _mybir
    from concourse.bass_utils import run_bass_kernel_spmd as _run

    nc = _bacc.Bacc("TRN2", target_bir_lowering=False, num_devices=1)
    arrays, ins, outs = {}, {}, {}
    for name in _INS:
        a = _np.ascontiguousarray(inputs[name])
        arrays[f"in_{name}_dram"] = a
        ins[name] = nc.dram_tensor(f"in_{name}_dram", a.shape, _mybir.dt.from_np(a.dtype), kind="ExternalInput").ap()
    for i, (name, shape) in enumerate(_OUTS):
        outs[name] = nc.dram_tensor(f"out_{i}_dram", shape, F32, kind="ExternalOutput").ap()
    gates = nc.dram_tensor("gates_dram", (NG, P, NTB, JG * TB), F32, kind="Internal").ap()
    hidden = nc.dram_tensor("hidden_dram", (NKEY // 2, P, 2 * N), F32, kind="Internal").ap()
    program(nc, ins, outs, gates, hidden)
    r = _run(nc, [arrays], core_ids=[0])
    return tuple(r.results[0][f"out_{i}_dram"] for i in range(len(_OUTS)))
```
